# Optimizing a Trainium2 kernel written in Bass

```python
import jax, jax.numpy as jnp
from jax import lax
import numpy as np

D_MODEL = 1024
BATCH = 1
SEQ = 1024
DEPTH = 1
DEC_BATCH = 1
DEC_SEQ = 64
PAST_LEN = 512

CHUNK = 64
D_MIX = D_MODEL
POOL_WINDOWS = (2, 4, 8, 16)
POOL_GROUPS = len(POOL_WINDOWS)
POOL_WIDTH = D_MIX // 2
POOL_GROUP_DIM = POOL_WIDTH // POOL_GROUPS
POOL_HIST = max(POOL_WINDOWS) - 1
SB_WIDTH = D_MIX - POOL_WIDTH
SB_HEAD_DIM = 64
SB_HEADS = SB_WIDTH // SB_HEAD_DIM
QBLOCK = 128
N_GROUPS = 4
EXPERTS_PER_GROUP = 4
N_EXPERTS = N_GROUPS * EXPERTS_PER_GROUP
TOP_K = 2
D_EXPERT = D_MODEL // 4
ALPHA = (2 * DEPTH) ** 0.25
BETA = (8 * DEPTH) ** -0.25
LN_EPS = 1e-5

kernel_name = "hybrid_pool_stickbreak_hmoe_stream_step"

def _norm(x):
    xf = x.astype(jnp.float32)
    mu = jnp.mean(xf, axis=-1, keepdims=True)
    var = jnp.mean(jnp.square(xf - mu), axis=-1, keepdims=True)
    return (xf - mu) * lax.rsqrt(var + LN_EPS)

def _layer_norm(x, g, b):
    return (_norm(x) * g + b).astype(x.dtype)

def _pool_mixer(u, hist, pos0, w_pool, pool_scale):
    b, n, _ = u.shape
    ue = jnp.concatenate([hist, u], axis=1)
    cs = jnp.cumsum(ue.astype(jnp.float32), axis=1)
    cs = jnp.pad(cs, ((0, 0), (1, 0), (0, 0)))
    pos = pos0 + jnp.arange(n)
    end = cs[:, POOL_HIST + 1:POOL_HIST + 1 + n]
    means = []
    for gi, w in enumerate(POOL_WINDOWS):
        sl = slice(gi * POOL_GROUP_DIM, (gi + 1) * POOL_GROUP_DIM)
        start = cs[:, POOL_HIST + 1 - w:POOL_HIST + 1 - w + n, sl]
        cnt = jnp.minimum(w, pos + 1).astype(jnp.float32)
        means.append((end[..., sl] - start) / cnt[None, :, None])
    pooled = jnp.concatenate(means, axis=-1) - u.astype(jnp.float32)
    pooled = pooled.reshape(b, n, POOL_GROUPS, POOL_GROUP_DIM).astype(u.dtype)
    mixed = jnp.einsum('bngc,gcd->bngd', pooled, w_pool).reshape(b, n, POOL_WIDTH)
    return mixed * pool_scale, ue[:, -POOL_HIST:]

def _stick_breaking(q, k, v, q_pos, k_pos):
    b, nq, h, dh = q.shape
    qb = min(QBLOCK, nq)
    nblk = -(-nq // qb)
    pad = nblk * qb - nq
    qp = jnp.pad(q, ((0, 0), (0, pad), (0, 0), (0, 0)))
    pp = jnp.pad(q_pos, (0, pad))
    qblocks = qp.reshape(b, nblk, qb, h, dh).transpose(1, 0, 2, 3, 4)
    pblocks = pp.reshape(nblk, qb)
    scale = 1.0 / np.sqrt(dh)

    def one_block(args):
        qi, pi = args
        z = jnp.einsum('bqhd,bkhd->bhqk', qi, k).astype(jnp.float32) * scale
        valid = (k_pos[None, :] < pi[:, None])[None, None]
        log_beta = jax.nn.log_sigmoid(z)
        log_1m = jnp.where(valid, jax.nn.log_sigmoid(-z), 0.0)
        suffix = lax.cumsum(log_1m, axis=3, reverse=True) - log_1m
        a = jnp.where(valid, jnp.exp(log_beta + suffix), 0.0)
        return jnp.einsum('bhqk,bkhd->bqhd', a.astype(v.dtype), v)

    out = lax.map(one_block, (qblocks, pblocks))
    out = out.transpose(1, 0, 2, 3, 4).reshape(b, nblk * qb, h, dh)
    return out[:, :nq]

def _moe(hn, w_group, b_group, w_router, b_router, w_up, w_down):
    b, n, d = hn.shape
    t = hn.reshape(b * n, d)
    pg_all = jax.nn.softmax((t @ w_group + b_group).astype(jnp.float32), axis=-1)
    g = jnp.argmax(pg_all, axis=-1)
    pg = jnp.max(pg_all, axis=-1)
    el = (t @ w_router + b_router).astype(jnp.float32).reshape(-1, N_GROUPS, EXPERTS_PER_GROUP)
    el = jnp.take_along_axis(el, g[:, None, None], axis=1)[:, 0]
    pe = jax.nn.softmax(el, axis=-1)
    wv, idx = lax.top_k(pe, TOP_K)
    wv = wv / jnp.sum(wv, axis=-1, keepdims=True) * pg[:, None]
    ids = g[:, None] * EXPERTS_PER_GROUP + idx
    gate = jnp.sum(jax.nn.one_hot(ids, N_EXPERTS, dtype=jnp.float32) * wv[..., None], axis=1)
    hid = jnp.einsum('td,edf->tef', t, w_up)
    a, u = jnp.split(hid, 2, axis=-1)
    act = jax.nn.silu(a) * u * gate.astype(hn.dtype)[..., None]
    y = jnp.einsum('tef,efd->td', act, w_down)
    return y.reshape(b, n, d)

def _layer(x, c, hist_pool, hist_k, hist_v, w_mod, b_mod, w_in, w_pool, pool_scale, w_out,
           ln1_g, ln1_b, ln2_g, ln2_b, w_group, b_group, w_router, b_router, w_up, w_down):
    b, n, _ = x.shape
    past = hist_k.shape[1]
    mod = (c @ w_mod + b_mod)[:, None, :]
    sh1, sc1, g1, sh2, sc2, g2 = jnp.split(mod, 6, axis=-1)
    hn = (_norm(x) * (1 + sc1) + sh1).astype(x.dtype)
    proj = hn @ w_in
    u, q, k, v = jnp.split(proj, [POOL_WIDTH, POOL_WIDTH + SB_WIDTH, POOL_WIDTH + 2 * SB_WIDTH], axis=-1)
    q = q.reshape(b, n, SB_HEADS, SB_HEAD_DIM)
    k = k.reshape(b, n, SB_HEADS, SB_HEAD_DIM)
    v = v.reshape(b, n, SB_HEADS, SB_HEAD_DIM)
    pool_out, new_pool = _pool_mixer(u, hist_pool, past, w_pool, pool_scale)
    k_all = jnp.concatenate([hist_k, k], axis=1)
    v_all = jnp.concatenate([hist_v, v], axis=1)
    q_pos = past + jnp.arange(n)
    k_pos = jnp.arange(past + n)
    attn = _stick_breaking(q, k_all, v_all, q_pos, k_pos).reshape(b, n, SB_WIDTH)
    mix = jnp.concatenate([pool_out, attn], axis=-1) @ w_out
    x = _layer_norm(ALPHA * x + (1 + g1) * mix, ln1_g, ln1_b)
    hn2 = (_norm(x) * (1 + sc2) + sh2).astype(x.dtype)
    ff = _moe(hn2, w_group, b_group, w_router, b_router, w_up, w_down)
    x = _layer_norm(ALPHA * x + (1 + g2) * ff, ln2_g, ln2_b)
    return x, k, v, new_pool

def setup_inputs(seed: int = 0) -> dict:
    key = jax.random.key(seed)
    ks = jax.random.split(key, 24)

    def nrm(k, shape, scale=1.0):
        return jax.random.normal(k, shape, jnp.float32) * scale

    d = D_MODEL
    col_scale = jnp.concatenate([
        jnp.full((POOL_WIDTH,), BETA, jnp.float32),
        jnp.ones((2 * SB_WIDTH,), jnp.float32),
        jnp.full((SB_WIDTH,), BETA, jnp.float32)])
    return {
        'x_prompt': nrm(ks[0], (BATCH, SEQ, d)),
        'x_sample': nrm(ks[1], (DEC_BATCH, DEC_SEQ, d)),
        'c_prompt': nrm(ks[2], (BATCH, d)),
        'c_sample': nrm(ks[3], (DEC_BATCH, d)),
        'cache_k': nrm(ks[4], (DEPTH, DEC_BATCH, PAST_LEN, SB_HEADS, SB_HEAD_DIM)),
        'cache_v': nrm(ks[5], (DEPTH, DEC_BATCH, PAST_LEN, SB_HEADS, SB_HEAD_DIM), BETA),
        'state_pool': nrm(ks[6], (DEPTH, DEC_BATCH, POOL_HIST, POOL_WIDTH), BETA),
        'w_mod': nrm(ks[7], (DEPTH, d, 6 * d), 0.1 * d ** -0.5),
        'b_mod': nrm(ks[8], (DEPTH, 6 * d), 0.02),
        'w_in': nrm(ks[9], (DEPTH, d, POOL_WIDTH + 3 * SB_WIDTH), d ** -0.5) * col_scale,
        'w_pool': nrm(ks[10], (DEPTH, POOL_GROUPS, POOL_GROUP_DIM, POOL_GROUP_DIM), POOL_GROUP_DIM ** -0.5),
        'pool_scale': 1.0 + nrm(ks[11], (DEPTH, POOL_WIDTH), 0.1),
        'w_out': nrm(ks[12], (DEPTH, D_MIX, d), BETA * D_MIX ** -0.5),
        'ln1_g': 1.0 + nrm(ks[13], (DEPTH, d), 0.05),
        'ln1_b': nrm(ks[14], (DEPTH, d), 0.02),
        'ln2_g': 1.0 + nrm(ks[15], (DEPTH, d), 0.05),
        'ln2_b': nrm(ks[16], (DEPTH, d), 0.02),
        'w_group': nrm(ks[17], (DEPTH, d, N_GROUPS), d ** -0.5),
        'b_group': nrm(ks[18], (DEPTH, N_GROUPS), 0.01),
        'w_router': nrm(ks[19], (DEPTH, d, N_EXPERTS), d ** -0.5),
        'b_router': nrm(ks[20], (DEPTH, N_EXPERTS), 0.01),
        'w_up': nrm(ks[21], (DEPTH, N_EXPERTS, d, 2 * D_EXPERT), d ** -0.5),
        'w_down': nrm(ks[22], (DEPTH, N_EXPERTS, D_EXPERT, d), BETA * D_EXPERT ** -0.5),
    }

def reference(x_prompt, x_sample, c_prompt, c_sample, cache_k, cache_v, state_pool,
              w_mod, b_mod, w_in, w_pool, pool_scale, w_out, ln1_g, ln1_b, ln2_g, ln2_b,
              w_group, b_group, w_router, b_router, w_up, w_down):
    params = (w_mod, b_mod, w_in, w_pool, pool_scale, w_out, ln1_g, ln1_b, ln2_g, ln2_b,
              w_group, b_group, w_router, b_router, w_up, w_down)

    bp = x_prompt.shape[0]
    zero_pool = jnp.zeros((bp, POOL_HIST, POOL_WIDTH), x_prompt.dtype)
    empty_kv = jnp.zeros((bp, 0, SB_HEADS, SB_HEAD_DIM), x_prompt.dtype)
    y = x_prompt
    kp, vp, pp = [], [], []
    for l in range(DEPTH):
        y, k_new, v_new, p_new = _layer(y, c_prompt, zero_pool, empty_kv, empty_kv,
                                        *[w[l] for w in params])
        kp.append(k_new); vp.append(v_new); pp.append(p_new)
    y_prompt = y

    y = x_sample
    kd, vd, pd = [], [], []
    for l in range(DEPTH):
        y, k_new, v_new, p_new = _layer(y, c_sample, state_pool[l], cache_k[l], cache_v[l],
                                        *[w[l] for w in params])
        kd.append(k_new); vd.append(v_new); pd.append(p_new)
    y_sample = y

    k_prompt = jnp.stack(kp); v_prompt = jnp.stack(vp); pool_prompt = jnp.stack(pp)
    k_sample = jnp.stack(kd); v_sample = jnp.stack(vd); pool_sample = jnp.stack(pd)
    return (y_prompt, y_sample, k_prompt, v_prompt, pool_prompt, k_sample, v_sample, pool_sample)


_drawn_inputs = setup_inputs


def setup_inputs(seed=0):
    import zlib

    import numpy as np

    out = dict(_drawn_inputs(seed))
    spreads = {}
    factors = {'cache_k': 5.884,
     'cache_v': 2.904,
     'state_pool': 3.453,
     'ln2_b': 2.859,
     'b_group': 6.268,
     'b_router': 26.479}
    for name, (base, spread) in spreads.items():
        noise = np.random.default_rng([zlib.crc32(name.encode()), seed]).standard_normal(out[name].shape)
        drawn = base * np.exp(spread * noise) if base else spread * noise
        out[name] = __import__('jax').numpy.asarray(drawn.astype(out[name].dtype))
    for name, factor in factors.items():
        out[name] = (out[name] * factor).astype(out[name].dtype)
    return out
```

```python
from contextlib import ExitStack, contextmanager

import concourse.bass as bass
from concourse import mybir

ALU = mybir.AluOpType
ACT = mybir.ActivationFunctionType
AX_X = mybir.AxisListType.X
F32 = mybir.dt.float32
F32R = mybir.dt.float32r
BF16 = mybir.dt.bfloat16
I32 = mybir.dt.int32

P = 128
D = 1024
KC = D // P
SEQ, DEC = 1024, 64
NT = SEQ + DEC
PT = SEQ // P
TILES = PT + 1
PAST = 512
HEADS, DH = 8, 64
PAIRS = HEADS // 2
NMOD = 6 * D
SECS = 3
WIN = (2, 4, 8, 16)
HIST = 15
EPS = 1e-5
ALPHA = 2.0 ** 0.25
FC = 16
CH = [(0, 364), (364, 364), (728, 360)]
NG, EPG, NE = 4, 4, 16
DE = 256
SLOT_TILES = (2 * NT - NE) // P + NE
SLOT_TILES_MIN = -(-2 * NT // P)
NSLOT = SLOT_TILES * P
NLOG = NG + NE
MASKED = -1.0e30


def rows(i):
    return P if i < PT else DEC


class Tally:

    def __init__(self, sem):
        self.sem, self.n, self.turns = sem, 0, 0

    def inc(self, ins, by=1):
        ins.then_inc(self.sem, by)
        self.n += by
        return ins

    @property
    def now(self):
        return self.turns + self.n if not isinstance(self.turns, int) or self.turns else self.n


@contextmanager
def turns(eng, count, per):
    before = {t: t.n for t in per}
    with eng.Fori(0, count) as i:
        for t, by in per.items():
            t.turns = i * by
        yield i
    for t, by in per.items():
        assert t.n - before[t] == by, (t.sem, t.n - before[t], by)
        t.turns = 0
        t.n = before[t] + by * count


def build(nc, x_prompt, x_sample, c_prompt, c_sample, cache_k, cache_v, state_pool,
          w_mod, b_mod, w_in, w_pool, pool_scale, w_out, ln1_g, ln1_b, ln2_g, ln2_b,
          w_group, b_group, w_router, b_router, w_up, w_down,
          y_prompt, y_sample, k_prompt, v_prompt, pool_prompt, k_sample, v_sample, pool_sample):
    def dram(name, shape, dt=F32):
        return nc.dram_tensor(name, shape, dt, kind="Internal").ap()

    mod_d = dram("mod_d", [2, NMOD])
    x1_d = dram("x1_d", [NT, D])
    hn2_d = dram("hn2_d", [NT, D])
    y_d = dram("y_d", [NSLOT, D])

    with ExitStack() as outer:
        def osb(name, shape, dt=F32):
            return outer.enter_context(nc.sbuf_tensor(name, shape, dt))

        ident = osb("ident", [P, P])
        psum = outer.enter_context(nc.psum_tensor("psum", [P, 8, 512], F32))
        logits = osb("logits", [P, TILES, NLOG])
        mhalf = osb("mhalf", [P, 16])
        slots = osb("slots", [P, TILES, 2], I32)
        gates = osb("gates", [P, TILES, 2])
        with ExitStack() as mid:
            proj = mid.enter_context(nc.sbuf_tensor("proj", [P, FC, NT], F32))
            utail = mid.enter_context(nc.sbuf_tensor("utail", [P, 4, 2, HIST], F32))
            block_a(nc, ident, mhalf, psum, proj, utail, mod_d, x_prompt, x_sample, c_prompt,
                    c_sample, w_mod, b_mod, w_in, state_pool)
            block_b(nc, ident, mhalf, psum, proj, utail, logits, mod_d, x1_d, hn2_d, x_prompt,
                    x_sample, y_d, cache_k, cache_v, w_pool, pool_scale, w_out, ln1_g, ln1_b,
                    w_group, b_group, w_router, b_router, k_prompt, v_prompt, pool_prompt,
                    k_sample, v_sample, pool_sample)
        block_c(nc, ident, psum, logits, hn2_d, y_d, slots, gates, w_up, w_down)
        block_d(nc, mhalf, mod_d, x1_d, y_d, slots, gates, ln2_g, ln2_b, y_prompt, y_sample)


def block_a(nc, ident, mhalf, psum, proj, utail, mod_d, x_prompt, x_sample, c_prompt, c_sample,
            w_mod, b_mod, w_in, state_pool):
    with ExitStack() as ctx:
        def sb(name, shape, dt=F32):
            return ctx.enter_context(nc.sbuf_tensor(name, shape, dt))

        def sem(name):
            return ctx.enter_context(nc.semaphore(name))

        hn_hi = sb("hn_hi", [P, KC, NT], F32R)
        hn_lo = sb("hn_lo", [P, KC, NT], F32R)
        wm = sb("wm", [P, 2, 2048])
        w_raw = sb("w_raw", [P, 2, KC, P])
        w_hi = sb("w_hi", [P, 2, KC, P], F32R)
        w_lo = sb("w_lo", [P, 2, KC, P], F32R)
        stage = sb("stage", [P, 2, D])
        crow = sb("crow", [16, P])
        cT = sb("cT", [P, KC, 32])
        modb = sb("modb", [P, SECS, 512])
        modrow = sb("modrow", [P, SECS, 512])
        hist = sb("hist", [HIST, 512])
        ext = sb("ext", [P, 4, HIST + DEC])
        exs = sb("exs", [P, 2, HIST + DEC])
        rcnt = sb("rcnt", [P, HIST])
        stats = sb("stats", [P, TILES, 2, 6])
        mv = sb("mv", [P, TILES, 2])
        vpe = sb("vpe", [P, TILES])
        rstd = sb("rstd", [P, TILES])
        arena = proj[:, :, :].rearrange("p a b -> p (a b)")
        xin = arena[:, 0:TILES * D].rearrange("p (t d) -> p t d", d=D)
        mrow = arena[:, TILES * D:(TILES + 4) * D].rearrange("p (r d) -> p r d", d=D)

        c_loaded, hist_loaded, modb_loaded, moments_ready = map(sem, ("c_loaded", "hist_loaded", "modb_loaded", "moments_ready"))
        x_loaded = [sem("x_loaded_prompt"), sem("x_loaded_sample")]
        wm_loaded = [sem("wm_loaded0"), sem("wm_loaded1")]
        w_loaded = [sem("w_loaded0"), sem("w_loaded1")]
        ident0, ident_ready, const_ready = map(sem, ("ident0", "ident_ready", "const_ready"))
        cT_done, cT_ready, hist_ready = map(sem, ("cT_done", "cT_ready", "hist_ready"))
        modb_ready, modb_one = map(sem, ("modb_ready", "modb_one"))
        wm_used, mod_copied, mod_ready, mod_stored = map(sem, ("wm_used", "mod_copied", "mod_ready", "mod_stored"))
        mod_sum0 = sem("mod_sum0")
        rows_loaded = sem("rows_loaded")
        vpe_ready, rstd_ready, a_dve = map(sem, ("vpe_ready", "rstd_ready", "a_dve"))
        stage_ready, xT_done, hi_ready, lo_ready = map(sem, ("stage_ready", "xT_done", "hi_ready", "lo_ready"))
        w_split, w_hi_ready, proj_done, proj_copied = map(sem, ("w_split", "w_hi_ready", "proj_done", "proj_copied"))
        pool_step = sem("pool_step")

        block = ctx.enter_context(nc.Block())

        @block.sync
        def _(sp):
            sp.dma_start(crow[0:KC, :], c_prompt.rearrange("o (k p) -> (o k) p", p=P)).then_inc(c_loaded, 16)
            sp.dma_start(crow[KC:2 * KC, :], c_sample.rearrange("o (k p) -> (o k) p", p=P)).then_inc(c_loaded, 16)
            sp.dma_start(hist[:, :], state_pool[0, 0]).then_inc(hist_loaded, 16)
            def load_wm(sec, k, used):
                if used is not None:
                    sp.wait_ge(wm_used, used)
                src = w_mod[0, k * P:(k + 1) * P, bass.ds(sec * 2048, 2048)]
                sp.dma_start(wm[:, k % 2, :], src).then_inc(wm_loaded[k % 2], 16)

            load_wm(0, 0, None)
            load_wm(0, 1, None)
            sp.wait_ge(modb_ready, 1)
            for b in range(2):
                sp.dma_start(modb[b:P:32, :, :], b_mod[0].rearrange("(s j n) -> j s n", j=4, n=512)).then_inc(modb_loaded, 16)
            for t in range(PT):
                sp.dma_start(xin[:, t, :], x_prompt[0, t * P:(t + 1) * P, :]).then_inc(x_loaded[0], 16)
            sp.dma_start(xin[0:DEC, PT, :], x_sample[0]).then_inc(x_loaded[1], 16)
            for k in range(2, KC):
                load_wm(0, k, k - 1)
            def load_w(m, slot):
                src = w_in[0, :, bass.ds(m * P, P)].rearrange("(k p) c -> p k c", p=P)
                sp.dma_start(w_raw[:, slot, :, :], src).then_inc(w_loaded[slot], 16)

            sp.wait_ge(mod_stored, 32)
            for b in range(2):
                for r in range(2):
                    sp.dma_start(mrow[:, 2 * b + r, :], mod_d[b, r * D:(r + 1) * D].partition_broadcast(P)).then_inc(rows_loaded, 16)
            with sp.Fori(0, 2) as h:
                for mm in range(8):
                    load_wm(h + 1, mm, h * 8 + KC + mm - 1)
                    sp.wait_ge(w_split, h * 8 + mm + 1)
                    load_w(h * 8 + mm, mm % 2)
            sp.wait_ge(mod_stored, 32 * SECS)

        @block.gpsimd
        def _(pool):
            step = Tally(pool_step)

            def then(ins):
                step.inc(ins)
                pool.wait_ge(pool_step, step.n)

            pool.memset(modb[:, :, :], 0.0).then_inc(modb_ready, 1)
            pool.memset(ident[:, :], 0.0).then_inc(ident0, 1)
            pool.wait_ge(ident0, 1)
            pool.affine_select(out=ident[:, :], in_=ident[:, :], compare_op=ALU.not_equal, fill=1.0, base=0,
                               pattern=[[-1, P]], channel_multiplier=1).then_inc(ident_ready, 1)
            pool.memset(cT[:, :, :], 0.0).then_inc(const_ready, 1)
            pool.memset(mv[:, :, :], 0.0).then_inc(const_ready, 1)
            pool.memset(mhalf[:, :], -0.5).then_inc(const_ready, 1)
            for n in range(HIST):
                pool.memset(rcnt[:, n:n + 1], 1.0 / (n + 1)).then_inc(const_ready, 1)
            pool.wait_ge(const_ready, 3)
            pool.wait_ge(vpe_ready, 1)
            pool.tensor_tensor(rstd[:, :], vpe[:, :], mhalf[:, 0:TILES], ALU.pow).then_inc(rstd_ready, 1)
            def store_mod(sec):
                for b in range(2):
                    pool.dma_start(mod_d[b, sec * 2048:(sec + 1) * 2048].rearrange("(j n) -> j n", j=4),
                                   modrow[b:P:32, sec, :]).then_inc(mod_stored, 16)

            pool.wait_ge(mod_sum0, 1)
            store_mod(0)
            pool.wait_ge(proj_copied, 2 + 4)
            pool.wait_ge(hist_ready, 1)
            for g in range(4):
                u = proj[:, g, :]
                pool.tensor_copy(utail[:, g, 0, :], u[:, SEQ - HIST:SEQ])
                then(pool.tensor_copy(utail[:, g, 1, :], u[:, NT - HIST:NT]))
                src = u[:, 0:SEQ]
                for level in range(g + 1):
                    w = 1 << level
                    dst = stage[:, level % 2, :]
                    pool.tensor_copy(dst[:, 0:w], src[:, 0:w])
                    then(pool.tensor_tensor(dst[:, w:SEQ], src[:, w:SEQ], src[:, 0:SEQ - w], ALU.add))
                    src = dst
                w = WIN[g]
                if w > 2:
                    pool.tensor_tensor(src[:, 0:w - 1], src[:, 0:w - 1], rcnt[:, 0:w - 1], ALU.mult)
                    then(pool.tensor_scalar(src[:, w - 1:SEQ], src[:, w - 1:SEQ], 1.0 / w, None, ALU.mult))
                else:
                    then(pool.tensor_scalar(src[:, 1:SEQ], src[:, 1:SEQ], 0.5, None, ALU.mult))
                then(pool.tensor_tensor(u[:, 0:SEQ], src[:, :], u[:, 0:SEQ], ALU.subtract))
                then(pool.tensor_copy(ext[:, g, HIST:HIST + DEC], u[:, SEQ:NT]))
                src, n = ext[:, g, :], HIST + DEC
                for level in range(g + 1):
                    w = 1 << level
                    n -= w
                    dst = exs[:, level % 2, 0:n]
                    then(pool.tensor_tensor(dst, src[:, w:w + n], src[:, 0:n], ALU.add))
                    src = dst
                then(pool.tensor_scalar(src[:, n - DEC:n], src[:, n - DEC:n], 1.0 / WIN[g], None, ALU.mult))
                then(pool.tensor_tensor(u[:, SEQ:NT], src[:, n - DEC:n], u[:, SEQ:NT], ALU.subtract))
            pool.wait_ge(modb_one, 3)
            for sec in range(1, SECS):
                pool.wait_ge(mod_copied, sec + 1)
                pool.tensor_tensor(modrow[:, sec, :], modrow[:, sec, :], modb[:, sec, :], ALU.add).then_inc(mod_ready, 1)
                pool.wait_ge(mod_ready, sec)
                store_mod(sec)

        @block.tensor
        def _(pe):
            psM = psum[:, 7, :]
            pe.wait_ge(ident_ready, 1)
            pe.wait_ge(c_loaded, 32)
            pe.transpose(psum[:, 6, 0:16], crow[:, :], ident[0:16, 0:16])
            pe.wait_ge(hist_loaded, 16)
            for g in range(4):
                last = pe.transpose(psum[:, 6, 16 + 16 * g:16 + 16 * g + HIST], hist[:, g * P:(g + 1) * P], ident[0:HIST, 0:HIST])
            last.then_inc(cT_done, 1)
            pe.wait_ge(cT_ready, 1)

            def mod_chunk(k, loaded):
                pe.wait_ge(wm_loaded[k % 2], loaded)
                for j in range(4):
                    mm = pe.matmul(psM[32 * j:32 * j + 32, :], cT[:, k, :], wm[:, k % 2, 512 * j:512 * j + 512],
                                   start=(k == 0), stop=(k == KC - 1), tile_position=(0, 32 * j))
                mm.then_inc(wm_used, 1)

            for k in range(KC):
                mod_chunk(k, 16 * (k // 2 + 1))
            def turn(t, slot, r, ready, free):
                pe.wait_ge(stage_ready, ready)
                if free is not None:
                    pe.wait_ge(lo_ready, free)
                for k in range(KC):
                    mm = pe.transpose(psum[:, 2 * slot + k // 4, (k % 4) * P:(k % 4) * P + r],
                                      stage[0:r, slot, k * P:(k + 1) * P], ident[0:r, 0:r])
                mm.then_inc(xT_done, 1)

            turn(0, 0, P, 1, None)
            turn(1, 1, P, 2, None)
            with pe.Fori(0, 3) as i:
                for s in range(2):
                    turn(i * 2 + 2 + s, s, P, i * 2 + 3 + s, i * 2 + 1 + s)
            turn(PT, 0, DEC, TILES, TILES - 2)
            pe.wait_ge(lo_ready, TILES)
            with pe.Fori(0, 2) as h:
                for mm_ in range(8):
                    slot = mm_ % 2
                    pe.wait_ge(w_split, h * 8 + mm_ + 3)
                    pe.wait_ge(proj_copied, h * 8 + mm_ + 1)
                    for k in range(KC):
                        for w, parts in ((w_hi, (hn_hi, hn_lo)), (w_lo, (hn_hi,))):
                            for hn in parts:
                                for c, (t0, n) in enumerate(CH):
                                    mm = pe.matmul(psum[:, 3 * slot + c, 0:n], w[:, slot, k, :], hn[:, k, t0:t0 + n],
                                                   start=(k == 0 and w is w_hi and hn is hn_hi),
                                                   stop=(k == KC - 1 and w is w_lo))
                    mm.then_inc(proj_done, 1)
                    if mm_ == 0:
                        pe.wait_ge(mod_sum0, 1)
                        pe.wait_ge(mod_copied, h + 1)
                    mod_chunk(mm_, h * 64 + 16 * (4 + mm_ // 2 + 1))

        @block.scalar
        def _(act):
            act.sem_inc(proj_copied, 2)
            act.sem_inc(mod_copied, 1)

            def high(t, slot, r, done):
                act.wait_ge(xT_done, done)
                src = psum[:, 2 * slot:2 * slot + 2, :].rearrange("p b (k c) -> p (b k) c", c=P)[:, :, 0:r]
                act.activation(hn_hi[:, :, bass.ds(t * P, r)], src, ACT.Copy).then_inc(hi_ready, 1)

            with act.Fori(0, PT // 2) as i:
                for s in range(2):
                    high(i * 2 + s, s, P, i * 2 + s + 1)
            high(PT, 0, DEC, TILES)
            with act.Fori(0, 2) as h:
                for mm in range(8):
                    slot = mm % 2
                    act.wait_ge(proj_done, h * 8 + mm + 1)
                    for c, (t0, n) in enumerate(CH):
                        cp = act.activation(proj[:, bass.ds(h * 8 + mm, 1), t0:t0 + n].rearrange("p a n -> p (a n)"),
                                            psum[:, 3 * slot + c, 0:n], ACT.Copy)
                    cp.then_inc(proj_copied, 1)
                act.wait_ge(wm_used, h * 8 + 2 * KC)
                act.activation(modrow[:, bass.ds(h + 1, 1), :].rearrange("p a n -> p (a n)"), psum[:, 7, :], ACT.Copy).then_inc(mod_copied, 1)

        @block.vector
        def _(dve):
            step = Tally(a_dve)

            def then(ins):
                step.inc(ins)
                dve.wait_ge(a_dve, step.now)

            dve.wait_ge(cT_done, 1)
            dve.wait_ge(const_ready, 3)
            for b in range(2):
                cp = dve.tensor_copy(cT[:, :, b], psum[:, 6, b * KC:(b + 1) * KC])
            cp.then_inc(cT_ready, 1)
            dve.tensor_copy(ext[:, :, 0:HIST], psum[:, 6, 16:80].rearrange("p (g c) -> p g c", c=16)[:, :, 0:HIST]).then_inc(hist_ready, 1)
            dve.wait_ge(modb_loaded, 32)
            for lo, hi, sec in ((64, P, 0), (0, 64, 1), (0, P, 2)):
                dve.tensor_scalar(modb[lo:hi, sec, :], modb[lo:hi, sec, :], 1.0, None, ALU.add).then_inc(modb_one, 1)
            def moments(t, r):
                for half in range(2):
                    dve.bn_stats(stats[0:r, bass.ds(t, 1), half, :].rearrange("p a n -> p (a n)"),
                                 xin[0:r, bass.ds(t, 1), half * 512:(half + 1) * 512].rearrange("p a n -> p (a n)")).then_inc(moments_ready, 1)

            dve.wait_ge(x_loaded[0], 16 * PT)
            with dve.Fori(0, PT) as t:
                moments(t, P)
            dve.wait_ge(x_loaded[1], 16)
            moments(PT, DEC)
            dve.wait_ge(moments_ready, 2 * TILES)
            for t in range(TILES):
                ag = dve.bn_aggr(mv[0:rows(t), t, :], stats[0:rows(t), t, :, :].rearrange("p b n -> p (b n)"))
            then(ag)
            dve.tensor_scalar(vpe[:, :], mv[:, :, 1], EPS, None, ALU.add).then_inc(vpe_ready, 1)
            dve.wait_ge(modb_one, 3)
            dve.wait_ge(wm_used, KC)
            dve.tensor_tensor(modrow[:, 0, :], psum[:, 7, :], modb[:, 0, :], ALU.add).then_inc(mod_sum0, 1)
            dve.wait_ge(rstd_ready, 1)
            dve.wait_ge(rows_loaded, 64)

            def modulate(t, slot, r, b, free):
                if free is not None:
                    dve.wait_ge(xT_done, free)
                x = xin[0:r, bass.ds(t, 1), :].rearrange("p a n -> p (a n)")
                st = stage[0:r, slot, :]
                then(dve.tensor_scalar(st, x, mv[0:r, bass.ds(t, 1), 0:1].rearrange("p a n -> p (a n)"),
                                       rstd[0:r, bass.ds(t, 1)], ALU.subtract, ALU.mult))
                then(dve.tensor_tensor(st, st, mrow[0:r, 2 * b + 1, :], ALU.mult))
                dve.tensor_tensor(st, st, mrow[0:r, 2 * b, :], ALU.add).then_inc(stage_ready, 1)

            def low(t, slot, r, high_done):
                dve.wait_ge(hi_ready, high_done)
                src = psum[:, 2 * slot:2 * slot + 2, :].rearrange("p b (k c) -> p (b k) c", c=P)[:, :, 0:r]
                dve.tensor_tensor(hn_lo[:, :, bass.ds(t * P, r)], src, hn_hi[:, :, bass.ds(t * P, r)].bitcast(F32),
                                  ALU.subtract).then_inc(lo_ready, 1)

            modulate(0, 0, P, 0, None)
            modulate(1, 1, P, 0, None)
            with turns(dve, 3, {step: 4}) as i:
                for s in range(2):
                    low(i * 2 + s, s, P, i * 2 + s + 1)
                    modulate(i * 2 + 2 + s, s, P, 0, i * 2 + s + 1)
            low(PT - 2, 0, P, PT - 1)
            modulate(PT, 0, DEC, 1, PT - 1)
            low(PT - 1, 1, P, PT)
            low(PT, 0, DEC, TILES)
            def split(m, slot, loaded, free):
                dve.wait_ge(w_loaded[slot], loaded)
                if free is not None:
                    dve.wait_ge(proj_done, free)
                dve.tensor_copy(w_hi[:, slot, :, :], w_raw[:, slot, :, :]).then_inc(w_hi_ready, 1)
                dve.wait_ge(w_hi_ready, m + 1)
                dve.tensor_tensor(w_lo[:, slot, :, :], w_raw[:, slot, :, :], w_hi[:, slot, :, :].bitcast(F32),
                                  ALU.subtract).then_inc(w_split, 1)

            dve.sem_inc(w_split, 2)
            split(0, 0, 16, None)
            split(1, 1, 16, None)
            with dve.Fori(0, 7) as i:
                for s in range(2):
                    split(i * 2 + 2 + s, s, i * 16 + 32, i * 2 + 1 + s)


def attention_units():
    units = []
    for i in range(TILES):
        for p in range(PAIRS):
            if i < PT:
                n_all = (i + 1) * P
                starts = list(range(0, n_all, 512))[::-1]
                for s0 in starts:
                    n = min(512, n_all - s0)
                    units.append((i, p, 1024 - n_all + s0, n, False, s0, s0 == starts[0], s0 == 0))
            else:
                units.append((i, p, 1024 - DEC, DEC, False, SEQ, True, False))
                units.append((i, p, 1024 - DEC - PAST, PAST, True, 0, False, True))
    return units


def block_b(nc, ident, mhalf, psum, proj, utail, logits, mod_d, x1_d, hn2_d, x_prompt, x_sample,
            y_d, cache_k, cache_v, w_pool, pool_scale, w_out, ln1_g, ln1_b, w_group, b_group,
            w_router, b_router, k_prompt, v_prompt, pool_prompt, k_sample, v_sample, pool_sample):
    units = attention_units()
    nu = len(units)
    with ExitStack() as ctx:
        def sb(name, shape, dt=F32):
            return ctx.enter_context(nc.sbuf_tensor(name, shape, dt))

        def sem(name):
            return ctx.enter_context(nc.semaphore(name))

        v_nat = sb("v_nat", [P, TILES, 512])
        v_old = sb("v_old", [P, PAST // P, 512])
        wo = sb("wo", [P, KC, D])
        g1 = sb("g1", [P, D])
        l1g, l1b = sb("l1g", [P, D]), sb("l1b", [P, D])
        sc2, sh2 = sb("sc2", [P, D]), sb("sh2", [P, D])
        res = sb("res", [P, 2, D])
        hn2 = sb("hn2", [P, 2, D])
        attT = sb("attT", [P, 2, PAIRS, P])
        stay = sb("stay", [P, 2, 2, 512])
        take = sb("take", [P, 2, 2, 512])
        left = sb("left", [P, 2, 1025])
        aT = sb("aT", [P, 2, 2, 4, P])
        wgr = sb("wgr", [P, KC, NLOG])
        blog = sb("blog", [P, NLOG])
        wp = sb("wp", [P, 4, P])
        psc = sb("psc", [P, 4])
        identb = sb("identb", [P, P], BF16)
        mask = sb("mask", [P, P], BF16)
        zeros = sb("zeros", [P, 256])
        st1 = sb("st1", [P, 2, 6])
        mv1 = sb("mv1", [P, 2])
        ve = sb("ve", [P, 2])
        rs = sb("rs", [P, 2])
        vroom = proj[:, 12:16, :].rearrange("p a b -> p (a b)")
        k_old = vroom[:, 0:4 * PAST].rearrange("p (a b) -> p a b", b=PAST)
        hn2T = vroom[:, 2048:3072].rearrange("p (k c) -> p k c", c=P)
        xb = vroom[:, 3072:4096]
        k_st = stay[:, :, 0, :]
        tail_st = stay[0:HIST, :, 1, :]
        kc = take[:, :, :, :].rearrange("p a b c -> p (a b) c")

        w_loaded, wo_loaded, rows_in, kc_loaded = map(sem, ("bw_loaded", "wo_loaded", "rows_in", "kc_loaded"))
        b_const0, b_const = map(sem, ("b_const0", "b_const"))
        kv_turned, k_copied, v_copied = map(sem, ("kv_turned", "k_copied", "v_copied"))
        k_stored = [sem("k_stored0"), sem("k_stored1")]
        out_stored = sem("out_stored")
        tail_turned, tail_copied = map(sem, ("tail_turned", "tail_copied"))
        old_turned, old_copied = map(sem, ("old_turned", "old_copied"))
        pool_mixed, pool_copied = map(sem, ("pool_mixed", "pool_copied"))
        z_done, stay_ready, take_ready, left_ready, a_ready = map(sem, ("z_done", "stay_ready", "take_ready", "left_ready", "a_ready"))
        a_turned, aT_copied, pv_done, att_copied = map(sem, ("a_turned", "aT_copied", "pv_done", "att_copied"))
        mix_done, mix_copied = map(sem, ("mix_done", "mix_copied"))
        xb_loaded, res_ready, b_dve = map(sem, ("xb_loaded", "res_ready", "b_dve"))
        var_ready, rstd_ready = map(sem, ("var_ready", "b_rstd_ready"))
        n1_ready, x1_mid, x1_ready, n2_ready, hn2_mid, hn2_ready = map(sem, ("n1_ready", "x1_mid", "x1_ready", "n2_ready", "hn2_mid", "hn2_ready"))
        x1_stored = [sem("x1_stored0"), sem("x1_stored1")]
        hn2_stored = [sem("hn2_stored0"), sem("hn2_stored1")]
        h_turned, h_copied, logits_done, logits_copied = map(sem, ("h_turned", "h_copied", "logits_done", "logits_copied"))
        g1_sample, sc2_sample = map(sem, ("g1_sample", "sc2_sample"))
        zeros_ready, spare_zeroed = map(sem, ("zeros_ready", "spare_zeroed"))

        block = ctx.enter_context(nc.Block())

        def mod_row(dst, b, part):
            return dst, mod_d[b, part * D:(part + 1) * D].partition_broadcast(P)

        @block.sync
        def _(sp):
            sp.dma_start(kc, cache_k[0, 0].rearrange("(s p) h d -> p s (h d)", p=P)).then_inc(kc_loaded, 16)
            sp.dma_start(wp[:, :, :], w_pool[0].rearrange("g c d -> c g d")).then_inc(w_loaded, 16)
            sp.dma_start(psc[:, :], pool_scale[0].rearrange("(g p) -> p g", p=P), allow_slow_non_contiguous=True).then_inc(w_loaded, 16)
            sp.dma_start(v_old[:, :, :], cache_v[0, 0].rearrange("(s p) h d -> p s (h d)", p=P)).then_inc(w_loaded, 16)
            sp.dma_start(wgr[:, :, 0:NG], w_group[0].rearrange("(k p) n -> p k n", p=P)).then_inc(w_loaded, 16)
            sp.dma_start(wgr[:, :, NG:NLOG], w_router[0].rearrange("(k p) n -> p k n", p=P)).then_inc(w_loaded, 16)
            sp.dma_start(blog[:, 0:NG], b_group[0].partition_broadcast(P)).then_inc(w_loaded, 16)
            sp.dma_start(blog[:, NG:NLOG], b_router[0].partition_broadcast(P)).then_inc(w_loaded, 16)
            sp.dma_start(wo[:, :, :], w_out[0].rearrange("(k p) n -> p k n", p=P)).then_inc(wo_loaded, 16)
            for dst, src in (mod_row(g1[:, :], 0, 2), mod_row(sh2[:, :], 0, 3), mod_row(sc2[:, :], 0, 4),
                             (l1g[:, :], ln1_g[0].partition_broadcast(P)), (l1b[:, :], ln1_b[0].partition_broadcast(P))):
                sp.dma_start(dst, src).then_inc(rows_in, 16)
            for t in range(TILES):
                r = rows(t)
                ko, vo = (k_prompt[0, 0, t * P:t * P + r], v_prompt[0, 0, t * P:t * P + r]) if t < PT else (k_sample[0, 0], v_sample[0, 0])
                sp.wait_ge(k_copied, t + 1)
                sp.dma_start(ko.rearrange("t h d -> t (h d)"), k_st[0:r, t % 2, :]).then_inc(k_stored[t % 2], 16)
                sp.wait_ge(v_copied, t + 1)
                sp.dma_start(vo.rearrange("t h d -> t (h d)"), v_nat[0:r, t, :]).then_inc(out_stored, 16)
            sp.wait_ge(tail_copied, 2)
            sp.dma_start(pool_prompt[0, 0], tail_st[:, 0, :]).then_inc(out_stored, 16)
            sp.dma_start(pool_sample[0, 0], tail_st[:, 1, :]).then_inc(out_stored, 16)

            def load_x(j):
                src = x_prompt[0, j * P:(j + 1) * P, :] if j < PT else x_sample[0]
                sp.dma_start(xb[0:rows(j), :], src).then_inc(xb_loaded, 16)

            def store_hn2(j):
                sp.wait_ge(hn2_ready, j + 1)
                sp.dma_start(hn2_d[j * P:j * P + rows(j), :], hn2[0:rows(j), j % 2, :]).then_inc(hn2_stored[j % 2], 16)

            load_x(0)
            for j in range(TILES):
                if j + 1 < TILES:
                    sp.wait_ge(res_ready, j + 1)
                    load_x(j + 1)
                sp.wait_ge(x1_ready, j + 1)
                sp.dma_start(x1_d[j * P:j * P + rows(j), :], res[0:rows(j), j % 2, :]).then_inc(x1_stored[j % 2], 16)
                if j == PT - 1:
                    sp.wait_ge(mix_copied, 2 * PT)
                    sp.dma_start(*mod_row(g1[:, :], 1, 2)).then_inc(g1_sample, 16)
                if j >= 1:
                    store_hn2(j - 1)
                if j == PT:
                    sp.dma_start(*mod_row(sh2[:, :], 1, 3)).then_inc(sc2_sample, 16)
                    sp.dma_start(*mod_row(sc2[:, :], 1, 4)).then_inc(sc2_sample, 16)
            store_hn2(PT)
            sp.wait_ge(k_stored[0], 16 * 5)
            sp.wait_ge(k_stored[1], 16 * 4)
            sp.wait_ge(out_stored, 16 * (TILES + 2))
            for q in (x1_stored, hn2_stored):
                sp.wait_ge(q[0], 16 * 5)
                sp.wait_ge(q[1], 16 * 4)

        @block.gpsimd
        def _(pool):
            pool.memset(zeros[:, :], 0.0).then_inc(zeros_ready, 1)
            pool.memset(mask[:, :], MASKED).then_inc(b_const0, 1)
            pool.tensor_copy(identb[:, :], ident[:, :]).then_inc(b_const, 1)
            pool.memset(left[:, :, 1024:1025], 1.0).then_inc(b_const, 1)
            pool.memset(logits[:, PT, :], 0.0).then_inc(b_const, 1)
            pool.wait_ge(b_const0, 1)
            pool.affine_select(out=mask[:, :], in_=mask[:, :], compare_op=ALU.is_ge, fill=0.0, base=0,
                               pattern=[[1, P]], channel_multiplier=-1).then_inc(b_const, 1)
            pool.wait_ge(zeros_ready, 1)
            spare = y_d[SLOT_TILES_MIN * P:NSLOT, :].rearrange("(p a) (b n) -> p (a b) n", p=P, n=256)
            pool.dma_start(spare, zeros[:, None, :].broadcast_to(list(spare.shape))).then_inc(spare_zeroed, 16)
            pool.wait_ge(rows_in, 16 * 5)
            for j in range(TILES):
                r, s = rows(j), j % 2
                pool.wait_ge(var_ready, 2 * j + 1)
                pool.tensor_tensor(rs[:, 0:1], ve[:, 0:1], mhalf[:, 0:1], ALU.pow).then_inc(rstd_ready, 1)
                pool.wait_ge(n1_ready, j + 1)
                pool.tensor_tensor(res[0:r, s, :], res[0:r, s, :], l1g[0:r, :], ALU.mult).then_inc(x1_mid, 1)
                pool.wait_ge(x1_mid, j + 1)
                pool.tensor_tensor(res[0:r, s, :], res[0:r, s, :], l1b[0:r, :], ALU.add).then_inc(x1_ready, 1)
                pool.wait_ge(var_ready, 2 * j + 2)
                pool.tensor_tensor(rs[:, 1:2], ve[:, 1:2], mhalf[:, 0:1], ALU.pow).then_inc(rstd_ready, 1)
                pool.wait_ge(n2_ready, j + 1)
                if j == PT:
                    pool.wait_ge(sc2_sample, 32)
                pool.tensor_tensor(hn2[0:r, s, :], hn2[0:r, s, :], sc2[0:r, :], ALU.mult).then_inc(hn2_mid, 1)
                pool.wait_ge(hn2_mid, j + 1)
                pool.tensor_tensor(hn2[0:r, s, :], hn2[0:r, s, :], sh2[0:r, :], ALU.add).then_inc(hn2_ready, 1)
            pool.wait_ge(spare_zeroed, 16)

        @block.tensor
        def _(pe):
            for t in range(TILES):
                r, s = rows(t), t % 2
                if t >= 2:
                    pe.wait_ge(k_copied, t - 1)
                    pe.wait_ge(v_copied, t - 1)
                for f in range(4):
                    pe.transpose(psum[0:r, 2 * s, f * P:(f + 1) * P], proj[:, 8 + f, t * P:t * P + r], ident[:, :])
                for f in range(4):
                    mm = pe.transpose(psum[0:r, 2 * s + 1, f * P:(f + 1) * P], proj[:, 12 + f, t * P:t * P + r], ident[:, :])
                mm.then_inc(kv_turned, 1)
            for b in range(2):
                for g in range(4):
                    mm = pe.transpose(psum[0:HIST, 4 + b, g * P:(g + 1) * P], utail[:, g, b, :], ident[:, :])
            mm.then_inc(tail_turned, 1)
            pe.wait_ge(kc_loaded, 16)
            pe.wait_ge(k_copied, TILES)
            pe.wait_ge(v_copied, TILES)
            for p in range(PAIRS):
                for s in range(4):
                    mm = pe.transpose(psum[:, p, s * P:(s + 1) * P], kc[:, s, p * P:(p + 1) * P], ident[:, :])
            mm.then_inc(old_turned, 1)
            pe.wait_ge(w_loaded, 16 * 7)
            pe.wait_ge(tail_copied, 2)
            for g in range(4):
                if g:
                    pe.wait_ge(pool_copied, g)
                for c, (t0, n) in enumerate(((0, 512), (512, 512), (SEQ, DEC))):
                    mm = pe.matmul(psum[:, 4 + c, 0:n], wp[:, g, :], proj[:, g, t0:t0 + n], start=True, stop=True)
                mm.then_inc(pool_mixed, 1)
            pe.wait_ge(old_copied, 1)
            pe.wait_ge(pool_copied, 4)
            pe.wait_ge(b_const, 4)

            def scores(u):
                i, p, at, n, old, s0, top, _ = units[u]
                r, s = rows(i), u % 2
                if u >= 2:
                    pe.wait_ge(take_ready, u - 1)
                for h in range(2):
                    q = proj[64 * h:64 * h + 64, 4 + p, i * P:i * P + r]
                    k = k_old[64 * h:64 * h + 64, p, :] if old else proj[64 * h:64 * h + 64, 8 + p, s0:s0 + n]
                    mm = pe.matmul(psum[0:r, 2 * s + h, 0:n], q, k, start=True, stop=not top)
                if top:
                    for h in range(2):
                        lo = 64 * h if r == DEC else 0
                        mm = pe.matmul(psum[0:r, 2 * s + h, n - r:n], identb[lo:lo + r, lo:lo + r], mask[lo:lo + r, lo:lo + r],
                                       start=False, stop=True)
                mm.then_inc(z_done, 1)

            def turn(u):
                i, p, at, n, *_ = units[u]
                r, s = rows(i), u % 2
                pe.wait_ge(a_ready, u + 1)
                for h in range(2):
                    if u >= 1:
                        pe.wait_ge(aT_copied, 2 * u - 1 + h)
                    for b in range(0, n, P):
                        m = min(P, n - b)
                        mm = pe.transpose(psum[0:m, 4 + h, b:b + r], take[0:r, s, h, b:b + m], ident[0:r, 0:r])
                    mm.then_inc(a_turned, 1)

            def values(u):
                i, p, at, n, old, s0, top, bottom = units[u]
                r, s = rows(i), u % 2
                pe.wait_ge(aT_copied, 2 * u + 2)
                if top and (i or p):
                    pe.wait_ge(att_copied, i * PAIRS + p)
                nb = -(-n // P)
                for b in range(nb):
                    m = min(P, n - b * P)
                    v = v_old[0:m, b, :] if old else v_nat[0:m, s0 // P + b, :]
                    for h in range(2):
                        c = p * P + 64 * h
                        mm = pe.matmul(psum[64 * h:64 * h + 64, 6, 0:r], v[:, c:c + 64], aT[0:m, s, h, b, 0:r],
                                       start=(top and b == 0), stop=(bottom and b == nb - 1))
                mm.then_inc(pv_done, 1)

            def mix(j, half):
                r = rows(j)
                if half == 0:
                    pe.wait_ge(att_copied, PAIRS * (j + 1))
                    if j >= 2:
                        pe.wait_ge(logits_copied, j - 1)
                    if j == 1:
                        pe.wait_ge(mix_copied, 2)
                else:
                    pe.wait_ge(mix_copied, 2 * j + 1)
                for k in range(KC):
                    lhs = proj[:, k, j * P:j * P + r] if k < 4 else attT[:, j % 2, k - 4, 0:r]
                    mm = pe.matmul(psum[0:r, 7, :], lhs, wo[:, k, 512 * half:512 * half + 512], start=(k == 0), stop=(k == KC - 1))
                mm.then_inc(mix_done, 1)

            def turn_h(j, half):
                r = rows(j)
                if half == 0:
                    pe.wait_ge(hn2_ready, j + 1)
                    pe.wait_ge(mix_copied, 2 * min(j + 2, TILES))
                else:
                    pe.wait_ge(h_copied, 2 * j + 1)
                for k in range(4 * half, 4 * half + 4):
                    mm = pe.transpose(psum[:, 7, (k % 4) * P:(k % 4) * P + r], hn2[0:r, j % 2, k * P:(k + 1) * P], ident[0:r, 0:r])
                mm.then_inc(h_turned, 1)

            def router(j):
                r = rows(j)
                pe.wait_ge(h_copied, 2 * j + 2)
                for k in range(KC):
                    mm = pe.matmul(psum[0:r, 7, 0:NLOG], hn2T[:, k, 0:r], wgr[:, k, :], start=(k == 0), stop=(k == KC - 1))
                mm.then_inc(logits_done, 1)

            def beside(i, p):
                j1, j2 = i - 1, i - 2
                if p < 2 and 0 <= j1 < TILES:
                    mix(j1, p)
                if p >= 2 and 0 <= j2 < TILES:
                    turn_h(j2, p - 2)
                    if p == 3:
                        router(j2)

            pe.wait_ge(wo_loaded, 16)
            for u in range(nu + 2):
                if u < nu:
                    scores(u)
                if 1 <= u <= nu:
                    turn(u - 1)
                if u >= 2:
                    values(u - 2)
                    if units[u - 2][7]:
                        beside(*units[u - 2][0:2])
            for i in (TILES, TILES + 1):
                for p in range(PAIRS):
                    beside(i, p)

        @block.scalar
        def _(act):
            for t in range(TILES):
                r, s = rows(t), t % 2
                act.wait_ge(kv_turned, t + 1)
                if t >= 2:
                    act.wait_ge(k_stored[s], 16 * (t // 2))
                act.activation(k_st[0:r, s, :], psum[0:r, 2 * s, :], ACT.Copy).then_inc(k_copied, 1)
            act.wait_ge(tail_turned, 1)
            for b in range(2):
                act.activation(tail_st[:, b, :], psum[0:HIST, 4 + b, :], ACT.Copy).then_inc(tail_copied, 1)
            act.wait_ge(old_turned, 1)
            act.activation(k_old, psum[:, 0:4, :], ACT.Copy).then_inc(old_copied, 1)
            for g in range(4):
                act.wait_ge(pool_mixed, g + 1)
                for c, (t0, n) in enumerate(((0, 512), (512, 512), (SEQ, DEC))):
                    cp = act.activation(proj[:, g, t0:t0 + n], psum[:, 4 + c, 0:n], ACT.Copy, scale=psc[:, g:g + 1])
                cp.then_inc(pool_copied, 1)
            act.wait_ge(k_stored[0], 16 * 5)
            act.wait_ge(k_stored[1], 16 * 4)
            act.wait_ge(out_stored, 16 * (TILES + 2))

            def sticks(u):
                i, p, at, n, *_ = units[u]
                r, s = rows(i), u % 2
                act.wait_ge(z_done, u + 1)
                if u >= 2:
                    act.wait_ge(a_ready, u - 1)
                act.activation(stay[0:r, s, :, 0:n], psum[0:r, 2 * s:2 * s + 2, 0:n], ACT.Sigmoid, scale=-0.125).then_inc(stay_ready, 1)
                if u >= 2:
                    act.wait_ge(a_turned, 2 * (u - 1))
                act.activation(take[0:r, s, :, 0:n], psum[0:r, 2 * s:2 * s + 2, 0:n], ACT.Sigmoid, scale=0.125).then_inc(take_ready, 1)

            def copy_aT(u):
                i, p, at, n, *_ = units[u]
                r, s, nb = rows(i), u % 2, -(-n // P)
                m = min(P, n)
                for h in range(2):
                    act.wait_ge(a_turned, 2 * u + h + 1)
                    if u >= 2 and h == 0:
                        act.wait_ge(pv_done, u - 1)
                    src = psum[0:m, 4 + h, :].rearrange("p (b c) -> p b c", c=P)[:, 0:nb, 0:r]
                    act.activation(aT[0:m, s, h, 0:nb, 0:r], src, ACT.Copy).then_inc(aT_copied, 1)

            def copy_h(j, half):
                r = rows(j)
                act.wait_ge(h_turned, 2 * j + half + 1)
                if half == 0 and j:
                    act.wait_ge(logits_done, j)
                src = psum[:, 7, :].rearrange("p (k c) -> p k c", c=P)[:, :, 0:r]
                act.activation(hn2T[:, 4 * half:4 * half + 4, 0:r], src, ACT.Copy).then_inc(h_copied, 1)

            def beside(i, p):
                if p >= 2 and 0 <= i - 2 < TILES:
                    copy_h(i - 2, p - 2)

            for u in range(nu + 2):
                if u < nu:
                    sticks(u)
                if 1 <= u <= nu:
                    copy_aT(u - 1)
                if u >= 2 and units[u - 2][7]:
                    beside(*units[u - 2][0:2])
            for i in (TILES, TILES + 1):
                for p in range(PAIRS):
                    beside(i, p)

        @block.vector
        def _(dve):
            step = Tally(b_dve)

            def then(ins):
                step.inc(ins)
                dve.wait_ge(b_dve, step.n)

            for t in range(TILES):
                r, s = rows(t), t % 2
                dve.wait_ge(kv_turned, t + 1)
                dve.tensor_copy(v_nat[0:r, t, :], psum[0:r, 2 * s + 1, :]).then_inc(v_copied, 1)
            dve.wait_ge(b_const, 4)

            def weights(u):
                i, p, at, n, old, s0, top, _ = units[u]
                r, s = rows(i), u % 2
                dve.wait_ge(stay_ready, u + 1)
                if u:
                    dve.wait_ge(a_ready, u)
                for h in range(2):
                    first = 1.0 if top else left[0:r, h, at + n:at + n + 1]
                    w = stay[0:r, s, h, 0:n][:, ::-1]
                    ins = dve.tensor_tensor_scan(left[0:r, h, at:at + n][:, ::-1], w, w, first, ALU.mult, ALU.bypass)
                ins.then_inc(left_ready, 1)
                dve.wait_ge(take_ready, u + 1)
                dve.wait_ge(left_ready, u + 1)
                dve.tensor_tensor(take[0:r, s, :, 0:n], take[0:r, s, :, 0:n], left[0:r, :, at + 1:at + 1 + n], ALU.mult).then_inc(a_ready, 1)

            def copy_att(u):
                i, p = units[u][0:2]
                r = rows(i)
                dve.wait_ge(pv_done, u + 1)
                if i >= 2 and p == 0:
                    dve.wait_ge(mix_done, 2 * (i - 1))
                dve.tensor_copy(attT[:, i % 2, p, 0:r], psum[:, 6, 0:r]).then_inc(att_copied, 1)

            def copy_mix(j, half):
                r, s = rows(j), j % 2
                dve.wait_ge(mix_done, 2 * j + half + 1)
                if half == 0 and j >= 2:
                    dve.wait_ge(x1_stored[s], 16 * (j // 2))
                if j == PT and half == 0:
                    dve.wait_ge(g1_sample, 16)
                cols = slice(512 * half, 512 * half + 512)
                dve.tensor_tensor(res[0:r, s, cols], psum[0:r, 7, :], g1[0:r, cols], ALU.mult).then_inc(mix_copied, 1)

            def moments(src, r, j, which):
                for half in range(2):
                    st = dve.bn_stats(st1[0:r, half, :], src[:, half * 512:(half + 1) * 512])
                then(st)
                then(dve.bn_aggr(mv1[0:r, :], st1[0:r, :, :].rearrange("p b n -> p (b n)")))
                dve.tensor_scalar(ve[0:r, which:which + 1], mv1[0:r, 1:2], EPS, None, ALU.add).then_inc(var_ready, 1)

            def residual(j):
                r, s = rows(j), j % 2
                dve.wait_ge(xb_loaded, 16 * (j + 1))
                dve.wait_ge(mix_copied, 2 * j + 2)
                dve.scalar_tensor_tensor(out=res[0:r, s, :], in0=xb[0:r, :], scalar=ALPHA, in1=res[0:r, s, :],
                                         op0=ALU.mult, op1=ALU.add).then_inc(res_ready, 1)
                dve.wait_ge(res_ready, j + 1)
                moments(res[0:r, s, :], r, j, 0)

            def norm1(j):
                r, s = rows(j), j % 2
                dve.wait_ge(rstd_ready, 2 * j + 1)
                dve.tensor_scalar(res[0:r, s, :], res[0:r, s, :], mv1[0:r, 0:1], rs[0:r, 0:1], ALU.subtract, ALU.mult).then_inc(n1_ready, 1)

            def norm2(j):
                r, s = rows(j), j % 2
                dve.wait_ge(rstd_ready, 2 * j + 2)
                if j >= 2:
                    dve.wait_ge(hn2_stored[s], 16 * (j // 2))
                    dve.wait_ge(h_turned, 2 * (j - 1))
                dve.tensor_scalar(hn2[0:r, s, :], res[0:r, s, :], mv1[0:r, 0:1], rs[0:r, 1:2], ALU.subtract, ALU.mult).then_inc(n2_ready, 1)

            def copy_logits(j):
                r = rows(j)
                dve.wait_ge(logits_done, j + 1)
                dve.tensor_tensor(logits[0:r, j, :], psum[0:r, 7, 0:NLOG], blog[0:r, :], ALU.add).then_inc(logits_copied, 1)

            def beside(i, p):
                j1, j2 = i - 1, i - 2
                if p == 0 and 0 <= j2 < TILES:
                    norm2(j2)
                if 0 <= j1 < TILES:
                    if p < 2:
                        copy_mix(j1, p)
                    if p == 1:
                        residual(j1)
                    if p == 2:
                        norm1(j1)
                    if p == 3:
                        dve.wait_ge(x1_ready, j1 + 1)
                        moments(res[0:rows(j1), j1 % 2, :], rows(j1), j1, 1)
                if p == 3 and 0 <= j2 < TILES:
                    copy_logits(j2)

            dve.wait_ge(rows_in, 16 * 5)
            dve.wait_ge(w_loaded, 16 * 7)
            for u in range(nu + 2):
                if u < nu:
                    weights(u)
                if u >= 2 and units[u - 2][7]:
                    copy_att(u - 2)
                    beside(*units[u - 2][0:2])
            for i in (TILES, TILES + 1):
                for p in range(PAIRS):
                    beside(i, p)


def block_c(nc, ident, psum, logits, hn2_d, y_d, slots, gates, w_up, w_down):
    with ExitStack() as ctx:
        def sb(name, shape, dt=F32):
            return ctx.enter_context(nc.sbuf_tensor(name, shape, dt))

        def sem(name):
            return ctx.enter_context(nc.semaphore(name))

        TC = SLOT_TILES + 2
        UP, DN = KC * 2 * DE, 2 * D
        raw = sb("raw", [P, 2, UP + DN])
        we_hi = sb("we_hi", [P, 2 * (UP + DN)], F32R)
        we_lo = sb("we_lo", [P, 2 * (UP + DN)], F32R)
        xg = sb("xg", [P, 2, D])
        xf = sb("xf", [P, KC, P])
        x_hi = sb("x_hi", [P, 2, KC, P], F32R)
        x_lo = sb("x_lo", [P, 2, KC, P], F32R)
        au = sb("au", [P, 2 * DE])
        sg = sb("sg", [P, DE])
        actv = sb("actv", [P, DE])
        atf = sb("atf", [P, 2, P])
        at_hi = sb("at_hi", [P, 2, P], F32R)
        at_lo = sb("at_lo", [P, 2, P], F32R)
        yst = sb("yst", [P, 2, D])
        prio = sb("prio", [P, 4])
        gmax = sb("gmax", [P, TILES, 1])
        gsh = sb("gsh", [P, TILES, NG])
        goh = sb("goh", [P, TILES, NG])
        gex = sb("gex", [P, TILES, NG])
        pg = sb("pg", [P, TILES, 1])
        sel = sb("sel", [P, TILES, NE])
        el = sb("el", [P, TILES, EPG])
        tmp4 = sb("tmp4", [P, TILES, EPG])
        l1, l2 = sb("l1", [P, TILES, 1]), sb("l2", [P, TILES, 1])
        best = sb("best", [P, TILES, 1])
        oh = [sb("oh1", [P, TILES, EPG]), sb("oh2", [P, TILES, EPG])]
        e12 = [sb("e1", [P, TILES, NE]), sb("e2", [P, TILES, NE])]
        both = sb("both", [P, TILES, NE])
        rank = sb("rank", [P, TILES, NE])
        before = sb("before", [P, TILES + 1, NE])
        cnt = sb("cnt", [P, TILES, NE])
        tri = sb("tri", [P, P])
        ones = sb("ones", [P, P])
        needf = sb("needf", [P, NE])
        needi = sb("needi", [P, NE], I32)
        cum = sb("cum", [P, NE])
        base = sb("base", [P, NE])
        sv = sb("sv", [P, TILES, NE])
        slotf = sb("slotf", [P, TILES, 2])
        posi = sb("posi", [P, TILES, 2], I32)
        posf = sb("posf", [P, TILES, 2])
        stf = sb("stf", [P, TILES, 2])
        tiota = sb("tiota", [P, TC])
        ciota = sb("ciota", [P, P])
        tokid = sb("tokid", [P, TILES])
        onp = sb("onp", [P, 2, 2, P])
        ont = sb("ont", [P, 2, 2, TC])
        cmp = sb("cmp", [P, TC, NE])
        texpf = sb("texpf", [P, TC])
        texp = sb("texp", [P, TC], I32)
        cumi = sb("cumi", [P, NE], I32)
        ntile = sb("ntile", [P, 1], I32)
        ntf = sb("ntf", [P, 1])
        ids = sb("ids", [P, TC], I32)
        idst = sb("idst", [P, 2], I32)

        r_const, r_dve, r_exp, r_shift, r_both, r_counts = map(sem, ("r_const", "r_dve", "r_exp", "r_shift", "r_both", "r_counts"))
        oneh_ready, tables_ready, ids_ready = map(sem, ("oneh_ready", "tables_ready", "ids_ready"))
        oneh_used = sem("oneh_used")
        raw_loaded = [sem("raw_loaded0"), sem("raw_loaded1")]
        raw_used, wh_ready, up_ready, down_ready = map(sem, ("raw_used", "wh_ready", "up_ready", "down_ready"))
        gathered = [sem("gathered0"), sem("gathered1")]
        idst_ready = sem("idst_ready")
        x_turned, x_copied, x_ready = map(sem, ("x_turned", "x_copied", "x_ready"))
        up_done, au_copied, act_mid, act_ready = map(sem, ("up_done", "au_copied", "act_mid", "act_ready"))
        act_turned, at_copied, at_ready = map(sem, ("act_turned", "at_copied", "at_ready"))
        down_done, y_copied = map(sem, ("down_done", "y_copied"))
        y_stored = [sem("y_stored0"), sem("y_stored1")]
        y_complete = sem("y_complete")

        def wide(ap, n):
            return ap.broadcast_to(list(ap.shape[:-1]) + [n])

        block = ctx.enter_context(nc.Block())

        @block.sync
        def _(sp):
            with sp.Fori(0, NE // 2) as i:
                for s in range(2):
                    sp.wait_ge(raw_used, i * 2 + s + 1)
                    up = w_up[0, bass.ds(i * 2 + s, 1)].rearrange("a (k p) n -> p (a k) n", p=P)
                    dn = w_down[0, bass.ds(i * 2 + s, 1)].rearrange("a (k p) n -> p (a k) n", p=P)
                    sp.dma_start(raw[:, s, 0:UP].rearrange("p (k n) -> p k n", k=KC), up).then_inc(raw_loaded[s], 16)
                    sp.dma_start(raw[:, s, UP:UP + DN].rearrange("p (k n) -> p k n", k=2), dn).then_inc(raw_loaded[s], 16)
            sp.wait_ge(y_complete, 1)

        @block.vector
        def _(dve):
            step = Tally(r_dve)
            dve.sem_inc(raw_used, 2)

            def then(ins):
                step.inc(ins)
                dve.wait_ge(r_dve, step.n)

            G = logits[:, :, 0:NG]
            dve.wait_ge(r_const, 5)

            def pick(dst, v, top):
                then(dve.tensor_reduce(top[:, :, :].rearrange("p t a -> p (t a)"), v, AX_X, ALU.max))
                then(dve.tensor_tensor(tmp4[:, :, :], v, wide(top[:, :, :], 4), ALU.is_equal))
                then(dve.tensor_tensor(tmp4[:, :, :], tmp4[:, :, :], prio[:, None, :].broadcast_to([P, TILES, 4]), ALU.mult))
                then(dve.tensor_reduce(best[:, :, :].rearrange("p t a -> p (t a)"), tmp4[:, :, :], AX_X, ALU.max))
                then(dve.tensor_tensor(dst, tmp4[:, :, :], wide(best[:, :, :], 4), ALU.is_equal))

            pick(goh[:, :, :], G, gmax)
            dve.tensor_tensor(gsh[:, :, :], G, wide(gmax[:, :, :], NG), ALU.subtract).then_inc(r_shift, 1)
            sel4 = sel[:, :, :].rearrange("p t (g e) -> p t g e", g=NG)
            then(dve.tensor_tensor(sel4, logits[:, :, NG:NLOG].rearrange("p t (g e) -> p t g e", g=NG),
                                   goh[:, :, :, None].broadcast_to([P, TILES, NG, EPG]), ALU.mult))
            then(dve.tensor_reduce(el[:, :, :], sel[:, :, :].rearrange("p t (g e) -> p t e g", g=NG), AX_X, ALU.add))
            pick(oh[0][:, :, :], el[:, :, :], l1)
            then(dve.scalar_tensor_tensor(out=el[:, :, :], in0=oh[0][:, :, :], scalar=-3.0e38, in1=el[:, :, :],
                                          op0=ALU.mult, op1=ALU.add))
            pick(oh[1][:, :, :], el[:, :, :], l2)
            then(dve.tensor_tensor(l1[:, :, :], l2[:, :, :], l1[:, :, :], ALU.subtract))
            dve.tensor_copy(l2[:, :, :], l1[:, :, :]).then_inc(r_shift, 1)
            for c in range(2):
                dve.tensor_tensor(e12[c][:, :, :].rearrange("p t (g e) -> p t g e", g=NG),
                                  goh[:, :, :, None].broadcast_to([P, TILES, NG, EPG]),
                                  oh[c][:, :, None, :].broadcast_to([P, TILES, NG, EPG]), ALU.mult).then_inc(r_dve, 1)
                step.n += 1
            dve.wait_ge(r_dve, step.n)
            for c in range(2):
                ms = dve.memset(e12[c][DEC:P, PT, :], 0.0)
            then(ms)
            dve.tensor_tensor(both[:, :, :], e12[0][:, :, :], e12[1][:, :, :], ALU.add).then_inc(r_both, 1)
            dve.wait_ge(r_exp, 2)
            then(dve.tensor_reduce(pg[:, :, :].rearrange("p t a -> p (t a)"), gex[:, :, :], AX_X, ALU.add))
            then(dve.tensor_scalar(l1[:, :, :], l2[:, :, :], 1.0, None, ALU.add))
            then(dve.tensor_tensor(l1[:, :, :], l1[:, :, :], pg[:, :, :], ALU.mult))
            then(dve.reciprocal(gates[:, :, 0:1], l1[:, :, :]))
            then(dve.tensor_tensor(gates[:, :, 1:2], gates[:, :, 0:1], l2[:, :, :], ALU.mult))
            dve.wait_ge(r_counts, 1)
            dve.tensor_copy(rank[:, :, :], psum[:, 6, 0:TILES * NE].rearrange("p (t e) -> p t e", e=NE))
            then(dve.tensor_copy(cnt[:, :, :], psum[:, 7, 0:TILES * NE].rearrange("p (t e) -> p t e", e=NE)))
            for t in range(TILES):
                then(dve.tensor_tensor(before[:, t + 1, :], before[:, t, :], cnt[:, t, :], ALU.add))
            then(dve.tensor_scalar(needi[:, :], before[:, TILES, :], float(P - 1), None, ALU.add))
            then(dve.tensor_scalar(needi[:, :], needi[:, :], 7, None, ALU.logical_shift_right))
            then(dve.tensor_copy(needf[:, :], needi[:, :]))
            then(dve.tensor_tensor_scan(cum[:, :], needf[:, :], needf[:, :], 0.0, ALU.add, ALU.bypass))
            then(dve.tensor_tensor(base[:, :], cum[:, :], needf[:, :], ALU.subtract))
            then(dve.tensor_scalar(base[:, :], base[:, :], float(P), None, ALU.mult))
            then(dve.tensor_tensor(sv[:, :, :], rank[:, :, :], before[:, 0:TILES, :], ALU.add))
            then(dve.tensor_tensor(sv[:, :, :], sv[:, :, :], base[:, None, :].broadcast_to([P, TILES, NE]), ALU.add))
            for c in range(2):
                then(dve.tensor_tensor(sel[:, :, :], sv[:, :, :], e12[c][:, :, :], ALU.mult))
                then(dve.tensor_reduce(slotf[:, :, c], sel[:, :, :], AX_X, ALU.add))
            then(dve.tensor_copy(slots[:, :, :], slotf[:, :, :]))
            then(dve.tensor_scalar(posi[:, :, :], slots[:, :, :], P - 1, None, ALU.bitwise_and))
            then(dve.tensor_copy(posf[:, :, :], posi[:, :, :]))
            then(dve.tensor_scalar(posi[:, :, :], slots[:, :, :], 7, None, ALU.logical_shift_right))
            then(dve.tensor_copy(stf[:, :, :], posi[:, :, :]))
            for t in range(TILES):
                r, s = rows(t), t % 2
                if t >= 2:
                    dve.wait_ge(oneh_used, t - 1)
                for c in range(2):
                    dve.tensor_scalar(onp[0:r, s, c, :], ciota[0:r, :], posf[0:r, t, c:c + 1], None, ALU.is_equal)
                    lt = dve.tensor_scalar(ont[0:r, s, c, :], tiota[0:r, :], stf[0:r, t, c:c + 1], tokid[0:r, t:t + 1],
                                           ALU.is_equal, ALU.mult)
                lt.then_inc(oneh_ready, 1)
            then(dve.tensor_tensor(cmp[:, :, :], cum[:, None, :].broadcast_to([P, TC, NE]),
                                   tiota[:, :, None].broadcast_to([P, TC, NE]), ALU.is_le))
            then(dve.tensor_reduce(texpf[:, :], cmp[:, :, :], AX_X, ALU.add))
            then(dve.tensor_scalar(texp[:, :], texpf[:, :], float(NE - 1), None, ALU.min))
            then(dve.tensor_copy(cumi[:, :], cum[:, :]))
            then(dve.tensor_scalar(ntile[:, :], cum[:, NE - 1:NE], 1.0, None, ALU.add))
            then(dve.tensor_scalar(ntile[:, :], ntile[:, :], 1, None, ALU.logical_shift_right))
            dve.tensor_scalar(ntile[:, :], ntile[:, :], 1, None, ALU.subtract).then_inc(tables_ready, 1)
            dve.wait_ge(oneh_used, TILES)
            dve.tensor_copy(ids[:, :], psum[:, 6, 0:TC]).then_inc(ids_ready, 1)
            dve.wait_ge(tables_ready, 1)

            def split(e, s, loaded, last):
                dve.wait_ge(raw_loaded[s], loaded)
                if last is not None:
                    dve.wait_ge(down_done, last + 1)
                for n, (lo, hi, ready) in enumerate(((0, UP, up_ready), (UP, UP + DN, down_ready))):
                    a, b = s * (UP + DN) + lo, s * (UP + DN) + hi
                    dve.tensor_copy(we_hi[:, a:b], raw[:, s, lo:hi]).then_inc(wh_ready, 1)
                    dve.wait_ge(wh_ready, e * 2 + (n + 1))
                    ins = dve.tensor_tensor(we_lo[:, a:b], raw[:, s, lo:hi], we_hi[:, a:b].bitcast(F32), ALU.subtract)
                    ins.then_inc(ready, 1)
                dve.wait_ge(down_ready, e + 1)
                dve.sem_inc(raw_used, 1)

            split(0, 0, 32, None)
            split(1, 1, 32, None)
            with dve.Fori(1, NE // 2) as i:
                for s in range(2):
                    last = dve.value_load(cumi[0:1, bass.ds(i * 2 + (s - 2), 1)], min_val=0, max_val=SLOT_TILES)
                    split(i * 2 + s, s, i * 32 + 32, last)

        @block.gpsimd
        def _(pool):
            pool.iota(tiota[:, :], [[1, TC]], base=0, channel_multiplier=0, allow_small_or_imprecise_dtypes=True).then_inc(r_const, 1)
            pool.iota(ciota[:, :], [[1, P]], base=0, channel_multiplier=0, allow_small_or_imprecise_dtypes=True).then_inc(r_const, 1)
            pool.iota(tokid[:, :], [[P, TILES]], base=0, channel_multiplier=1, allow_small_or_imprecise_dtypes=True).then_inc(r_const, 1)
            pool.iota(prio[:, :], [[-1, 4]], base=4, channel_multiplier=0, allow_small_or_imprecise_dtypes=True).then_inc(r_const, 1)
            pool.memset(before[:, 0, :], 0.0).then_inc(r_const, 1)
            pool.memset(ones[:, :], 1.0).then_inc(r_const, 1)
            pool.wait_ge(r_const, 6)
            pool.affine_select(out=tri[:, :], in_=ones[:, :], compare_op=ALU.is_gt, fill=0.0, base=0,
                               pattern=[[1, P]], channel_multiplier=-1).then_inc(r_const, 1)
            pool.wait_ge(ids_ready, 1)

            def name_tokens(t, s, turned):
                if turned is not None:
                    pool.wait_ge(x_turned, turned)
                pool.tensor_copy(idst[:, s:s + 1], ids[:, bass.ds(t, 1)]).then_inc(idst_ready, 1)

            def gather(s):
                pool.indirect_dma_start(xg[:, s, :], None, hn2_d, bass.IndirectOffsetOnAxis(idst[:, s:s + 1], 0)).then_inc(gathered[s], 16)

            def low_x(t, s, up):
                pool.wait_ge(x_copied, t + 1)
                if up is not None:
                    pool.wait_ge(up_done, up)
                pool.tensor_tensor(x_lo[:, s, :, :], xf[:, :, :], x_hi[:, s, :, :].bitcast(F32), ALU.subtract).then_inc(x_ready, 1)

            def low_act(t, used, gathers=True):
                if gathers:
                    pool.wait_ge(idst_ready, t + 4)
                pool.wait_ge(at_copied, t + 1)
                if used is not None:
                    pool.wait_ge(down_done, used)
                pool.tensor_tensor(at_lo[:, :, :], atf[:, :, :], at_hi[:, :, :].bitcast(F32), ALU.subtract).then_inc(at_ready, 1)

            def gate_act(t, turned):
                pool.wait_ge(au_copied, t + 1)
                pool.tensor_tensor(sg[:, :], au[:, 0:DE], sg[:, :], ALU.mult).then_inc(act_mid, 1)
                if turned is not None:
                    pool.wait_ge(act_turned, turned)
                pool.wait_ge(act_mid, t + 1)
                pool.tensor_tensor(actv[:, :], sg[:, :], au[:, DE:2 * DE], ALU.mult).then_inc(act_ready, 1)

            for t in range(2):
                name_tokens(t, t, None)
            pool.wait_ge(idst_ready, 2)
            gather(0)
            gather(1)
            low_x(0, 0, None)
            low_x(1, 1, None)
            name_tokens(2, 0, 1)
            pool.wait_ge(idst_ready, 3)
            gather(0)
            gate_act(0, None)
            low_x(2, 0, 1)
            name_tokens(3, 1, 2)
            low_act(0, None)
            gather(1)
            gate_act(1, 1)
            more = pool.value_load(ntile[0:1, 0:1], min_val=SLOT_TILES_MIN // 2, max_val=SLOT_TILES // 2 - 1)
            with pool.Fori(1, more + 1) as i:
                for s in range(2):
                    t = i * 2 + s
                    low_x(t + 1, 1 - s, t)
                    name_tokens(t + 2, s, t + 1)
                    low_act(t - 1, t)
                    gather(s)
                    gate_act(t, t)
            low_act(more * 2 + 1, more * 2 + 2, False)
            pool.wait_ge(gathered[1], more * 16 + 32)

        @block.scalar
        def _(act):
            act.sem_inc(y_stored[1], 16)
            act.wait_ge(r_shift, 1)
            act.activation(gex[:, :, :], gsh[:, :, :], ACT.Exp).then_inc(r_exp, 1)
            act.wait_ge(r_shift, 2)
            act.activation(l2[:, :, :], l2[:, :, :], ACT.Exp).then_inc(r_exp, 1)

            def copy_x(t, s, up, low):
                act.wait_ge(x_turned, t + 1)
                if up is not None:
                    act.wait_ge(up_done, up)
                src = psum[:, 0:2, :].rearrange("p b (k c) -> p (b k) c", c=P)
                act.activation(x_hi[:, s, :, :], src, ACT.Copy)
                if low is not None:
                    act.wait_ge(x_ready, low)
                act.activation(xf[:, :, :], src, ACT.Copy).then_inc(x_copied, 1)

            def copy_act(t, used, low):
                act.wait_ge(act_turned, t + 1)
                if used is not None:
                    act.wait_ge(down_done, used)
                    act.wait_ge(at_ready, low)
                src = psum[:, 3, 0:2 * P].rearrange("p (k c) -> p k c", c=P)
                act.activation(at_hi[:, :, :], src, ACT.Copy)
                act.activation(atf[:, :, :], src, ACT.Copy).then_inc(at_copied, 1)

            def swish(t, free):
                act.wait_ge(up_done, t + 1)
                if free is not None:
                    act.wait_ge(act_ready, free)
                act.activation(sg[:, :], psum[:, 2, 0:DE], ACT.Sigmoid)
                act.activation(au[:, :], psum[:, 2, :], ACT.Copy).then_inc(au_copied, 1)

            def copy_y(t, s, stored):
                act.wait_ge(down_done, t + 2)
                if stored is not None:
                    act.wait_ge(y_stored[s], stored)
                act.activation(yst[:, s, :], psum[:, 4:6, :].rearrange("p b n -> p (b n)"), ACT.Copy).then_inc(y_copied, 1)

            def store_y(t, s):
                act.wait_ge(y_copied, t + 1)
                act.dma_start(y_d[bass.ds(t * P, P), :], yst[:, s, :]).then_inc(y_stored[s], 16)

            act.wait_ge(ids_ready, 1)
            copy_x(0, 0, None, None)
            copy_x(1, 1, None, 1)
            swish(0, None)
            copy_x(2, 0, 1, 2)
            copy_act(0, None, None)
            swish(1, 1)
            copy_y(0, 0, None)
            more = act.value_load(ntile[0:1, 0:1], min_val=SLOT_TILES_MIN // 2, max_val=SLOT_TILES // 2 - 1)
            with act.Fori(1, more + 1) as i:
                for s in range(2):
                    t = i * 2 + s
                    copy_x(t + 1, 1 - s, t, t + 1)
                    store_y(t - 2, s)
                    copy_act(t - 1, t, t - 1)
                    swish(t, t)
                    copy_y(t - 1, 1 - s, i * 16)
            store_y(more * 2, 0)
            copy_act(more * 2 + 1, more * 2 + 2, more * 2 + 1)
            copy_y(more * 2 + 1, 1, more * 16 + 16)
            store_y(more * 2 + 1, 1)
            act.wait_ge(y_stored[0], more * 16 + 16)
            act.wait_ge(y_stored[1], more * 16 + 32)
            act.sem_inc(y_complete, 1)

        @block.tensor
        def _(pe):
            pe.sem_inc(down_done, 1)
            pe.wait_ge(r_both, 1)
            pe.wait_ge(r_const, 7)
            pe.matmul(psum[:, 6, 0:TILES * NE], tri[:, :], both[:, :, :].rearrange("p t e -> p (t e)"), start=True, stop=True)
            pe.matmul(psum[:, 7, 0:TILES * NE], ones[:, :], both[:, :, :].rearrange("p t e -> p (t e)"), start=True, stop=True).then_inc(r_counts, 1)
            for t in range(TILES):
                r, s = rows(t), t % 2
                pe.wait_ge(oneh_ready, t + 1)
                for c in range(2):
                    mm = pe.matmul(psum[:, 6, 0:TC], onp[0:r, s, c, :], ont[0:r, s, c, :], start=(t == 0 and c == 0),
                                   stop=(t == PT and c == 1))
                mm.then_inc(oneh_used, 1)
            pe.wait_ge(tables_ready, 1)

            def turn_x(t, s, count, copied):
                pe.wait_ge(gathered[s], count)
                if copied is not None:
                    pe.wait_ge(x_copied, copied)
                for k in range(KC):
                    mm = pe.transpose(psum[:, k // 4, (k % 4) * P:(k % 4 + 1) * P], xg[:, s, k * P:(k + 1) * P], ident[:, :])
                mm.then_inc(x_turned, 1)

            def turn_act(t, copied):
                pe.wait_ge(act_ready, t + 1)
                if copied is not None:
                    pe.wait_ge(at_copied, copied)
                for k in range(2):
                    mm = pe.transpose(psum[:, 3, k * P:(k + 1) * P], actv[:, k * P:(k + 1) * P], ident[:, :])
                mm.then_inc(act_turned, 1)

            def expert(t):
                return pe.value_load(texp[0:1, bass.ds(t, 1)], min_val=0, max_val=NE - 1)

            def weights_at(e):
                return (e % 2) * (UP + DN)

            def up(t, s, copied):
                e = expert(t)
                at = pe.snap(weights_at(e))
                pe.wait_ge(x_ready, t + 1)
                pe.wait_ge(up_ready, e + 1)
                if copied is not None:
                    pe.wait_ge(au_copied, copied)
                for k in range(KC):
                    for x, w in ((x_hi, we_hi), (x_hi, we_lo), (x_lo, we_hi)):
                        mm = pe.matmul(psum[:, 2, :], x[:, s, k, :], w[:, bass.ds(at + k * 2 * DE, 2 * DE)],
                                       start=(k == 0 and x is x_hi and w is we_hi), stop=(k == KC - 1 and x is x_lo))
                mm.then_inc(up_done, 1)

            def down(t, copied):
                e = expert(t)
                at = pe.snap(weights_at(e))
                pe.wait_ge(at_ready, t + 1)
                pe.wait_ge(down_ready, e + 1)
                if copied is not None:
                    pe.wait_ge(y_copied, copied)
                for k in range(2):
                    for x, w in ((at_hi, we_hi), (at_hi, we_lo), (at_lo, we_hi)):
                        for half in range(2):
                            mm = pe.matmul(psum[:, 4 + half, :], x[:, k, :], w[:, bass.ds(at + (UP + k * D + half * 512), 512)],
                                           start=(k == 0 and x is at_hi and w is we_hi), stop=(k == 1 and x is at_lo))
                mm.then_inc(down_done, 1)

            turn_x(0, 0, 16, None)
            turn_x(1, 1, 16, 1)
            up(0, 0, None)
            turn_x(2, 0, 32, 2)
            turn_act(0, None)
            up(1, 1, 1)
            down(0, None)
            more = pe.value_load(ntile[0:1, 0:1], min_val=SLOT_TILES_MIN // 2, max_val=SLOT_TILES // 2 - 1)
            with pe.Fori(1, more + 1) as i:
                for s in range(2):
                    t = i * 2 + s
                    turn_x(t + 1, 1 - s, i * 16 + 16 * (s + 1), t + 1)
                    turn_act(t - 1, t - 1)
                    up(t, s, t)
                    down(t - 1, t - 1)
            turn_act(more * 2 + 1, more * 2 + 1)
            down(more * 2 + 1, more * 2 + 1)


def block_d(nc, mhalf, mod_d, x1_d, y_d, slots, gates, ln2_g, ln2_b, y_prompt, y_sample):
    with ExitStack() as ctx:
        def sb(name, shape, dt=F32):
            return ctx.enter_context(nc.sbuf_tensor(name, shape, dt))

        def sem(name):
            return ctx.enter_context(nc.semaphore(name))

        NB = 3
        ya = sb("ya", [P, NB, D])
        yb = sb("yb", [P, NB, D])
        x1 = sb("x1", [P, NB, D])
        g2 = sb("g2", [P, 2, D])
        l2g, l2b = sb("l2g", [P, D]), sb("l2b", [P, D])
        st = sb("st2", [P, 2, 6])
        mv = sb("mv2", [P, TILES, 2])
        ve = sb("ve2", [P, TILES])
        rs = sb("rs2", [P, TILES])
        d_rows = sem("d_rows")
        y_in = [sem(f"y_in{n}") for n in range(NB)]
        x1_in = [sem(f"x1_in{n}") for n in range(NB)]
        out_stored = [sem(f"d_out{n}") for n in range(NB)]
        first_gated, summed, scaled, d_sum, d_var, d_rstd, finished, d_dve = map(
            sem, ("first_gated", "summed", "scaled", "d_sum", "d_var", "d_rstd", "finished", "d_dve"))
        block = ctx.enter_context(nc.Block())

        @block.sync
        def _(sp):
            for b in range(2):
                sp.dma_start(g2[:, b, :], mod_d[b, 5 * D:6 * D].partition_broadcast(P)).then_inc(d_rows, 16)
            sp.dma_start(l2g[:, :], ln2_g[0].partition_broadcast(P)).then_inc(d_rows, 16)
            sp.dma_start(l2b[:, :], ln2_b[0].partition_broadcast(P)).then_inc(d_rows, 16)

            def load(j):
                s = j % NB
                if j >= NB:
                    sp.wait_ge(out_stored[s], 16 * (j // NB))
                sp.dma_start(x1[0:rows(j), s, :], x1_d[j * P:j * P + rows(j), :]).then_inc(x1_in[s], 16)

            for j in range(NB):
                load(j)
            for j in range(TILES):
                s = j % NB
                dst = y_prompt[0, j * P:(j + 1) * P, :] if j < PT else y_sample[0]
                sp.wait_ge(finished, j + 1)
                sp.dma_start(dst, x1[0:rows(j), s, :]).then_inc(out_stored[s], 16)
                if j >= 1 and j - 1 + NB < TILES:
                    load(j - 1 + NB)
            for s in range(NB):
                sp.wait_ge(out_stored[s], 16 * (TILES // NB))

        @block.gpsimd
        def _(pool):
            def gather(j):
                r, s = rows(j), j % NB
                if j >= NB:
                    pool.wait_ge(d_sum, j - NB + 1)
                for c, y in enumerate((ya, yb)):
                    pool.indirect_dma_start(y[0:r, s, :], None, y_d,
                                            bass.IndirectOffsetOnAxis(slots[0:r, j, c:c + 1], 0)).then_inc(y_in[s], 16)

            for j in range(NB):
                gather(j)
            pool.wait_ge(d_rows, 64)
            for j in range(TILES + 1):
                if j < TILES:
                    r, s = rows(j), j % NB
                    pool.wait_ge(summed, j + 1)
                    pool.tensor_tensor(ya[0:r, s, :], ya[0:r, s, :], g2[0:r, j // PT, :], ALU.mult).then_inc(scaled, 1)
                if j >= 1:
                    r = rows(j - 1)
                    pool.wait_ge(d_var, j)
                    pool.tensor_tensor(rs[0:r, j - 1:j], ve[0:r, j - 1:j], mhalf[0:r, 0:1], ALU.pow).then_inc(d_rstd, 1)
                    if j - 1 + NB < TILES:
                        gather(j - 1 + NB)

        @block.scalar
        def _(act):
            for j in range(TILES):
                r, s = rows(j), j % NB
                act.wait_ge(y_in[s], 32 * (j // NB + 1))
                act.activation(ya[0:r, s, :], ya[0:r, s, :], ACT.Copy, scale=gates[0:r, j, 0:1]).then_inc(first_gated, 1)

        @block.vector
        def _(dve):
            step = Tally(d_dve)

            def then(ins):
                step.inc(ins)
                dve.wait_ge(d_dve, step.n)

            def combine(j):
                r, s = rows(j), j % NB
                dve.wait_ge(first_gated, j + 1)
                dve.scalar_tensor_tensor(out=ya[0:r, s, :], in0=yb[0:r, s, :], scalar=gates[0:r, j, 1:2], in1=ya[0:r, s, :],
                                         op0=ALU.mult, op1=ALU.add).then_inc(summed, 1)

            def residual(j):
                r, s = rows(j), j % NB
                dve.wait_ge(scaled, j + 1)
                dve.wait_ge(x1_in[s], 16 * (j // NB + 1))
                dve.scalar_tensor_tensor(out=x1[0:r, s, :], in0=x1[0:r, s, :], scalar=ALPHA, in1=ya[0:r, s, :],
                                         op0=ALU.mult, op1=ALU.add).then_inc(d_sum, 1)
                dve.wait_ge(d_sum, j + 1)
                for half in range(2):
                    b = dve.bn_stats(st[0:r, half, :], x1[0:r, s, half * 512:(half + 1) * 512])
                then(b)
                then(dve.bn_aggr(mv[0:r, j, :], st[0:r, :, :].rearrange("p b n -> p (b n)")))
                dve.tensor_scalar(ve[0:r, j:j + 1], mv[0:r, j, 1:2], EPS, None, ALU.add).then_inc(d_var, 1)

            def finish(j):
                r, s = rows(j), j % NB
                dve.wait_ge(d_rstd, j + 1)
                x = x1[0:r, s, :]
                then(dve.tensor_scalar(x, x, mv[0:r, j, 0:1], rs[0:r, j:j + 1], ALU.subtract, ALU.mult))
                then(dve.tensor_tensor(x, x, l2g[0:r, :], ALU.mult))
                dve.tensor_tensor(x, x, l2b[0:r, :], ALU.add).then_inc(finished, 1)

            dve.wait_ge(d_rows, 64)
            for j in range(TILES + 2):
                if j < TILES:
                    combine(j)
                if 1 <= j <= TILES:
                    residual(j - 1)
                if j >= 2:
                    finish(j - 2)


_INS = ["x_prompt", "x_sample", "c_prompt", "c_sample", "cache_k", "cache_v", "state_pool",
        "w_mod", "b_mod", "w_in", "w_pool", "pool_scale", "w_out", "ln1_g", "ln1_b", "ln2_g", "ln2_b",
        "w_group", "b_group", "w_router", "b_router", "w_up", "w_down"]
_OUTS = [(1, SEQ, D), (1, DEC, D), (1, 1, SEQ, HEADS, DH), (1, 1, SEQ, HEADS, DH), (1, 1, HIST, 512),
         (1, 1, DEC, HEADS, DH), (1, 1, DEC, HEADS, DH), (1, 1, HIST, 512)]


def kernel(**inputs):
    import numpy as _np
    import concourse.bacc as _bacc
    from concourse.bass_utils import run_bass_kernel_spmd as _run

    nc = _bacc.Bacc("TRN2", target_bir_lowering=False, num_devices=1)
    arrays, args = {}, []
    for name in _INS:
        a = _np.ascontiguousarray(inputs[name])
        arrays[f"in_{name}_dram"] = a
        args.append(nc.dram_tensor(f"in_{name}_dram", a.shape, mybir.dt.from_np(a.dtype), kind="ExternalInput").ap())
    for i, shape in enumerate(_OUTS):
        args.append(nc.dram_tensor(f"out_{i}_dram", shape, F32, kind="ExternalOutput").ap())
    build(nc, *args)
    r = _run(nc, [arrays], core_ids=[0])
    return tuple(r.results[0][f"out_{i}_dram"] for i in range(len(_OUTS)))
```

```python
from contextlib import ExitStack, contextmanager

import concourse.bass as bass
from concourse import mybir

ALU = mybir.AluOpType
ACT = mybir.ActivationFunctionType
AX_X = mybir.AxisListType.X
F32 = mybir.dt.float32
F32R = mybir.dt.float32r
BF16 = mybir.dt.bfloat16
I32 = mybir.dt.int32

P = 128
D = 1024
KC = D // P
SEQ, DEC = 1024, 64
NT = SEQ + DEC
PT = SEQ // P
TILES = PT + 1
PAST = 512
HEADS, DH = 8, 64
PAIRS = HEADS // 2
NMOD = 6 * D
SECS = 3
WIN = (2, 4, 8, 16)
HIST = 15
EPS = 1e-5
ALPHA = 2.0 ** 0.25
FC = 16
CH = [(0, 364), (364, 364), (728, 360)]
GROUPS = [(0, 4), (4, 8), (8, 9)]
NG, EPG, NE = 4, 4, 16
DE = 256
SLOT_TILES = (2 * NT - NE) // P + NE
SLOT_TILES_MIN = -(-2 * NT // P)
NSLOT = SLOT_TILES * P
NLOG = NG + NE
MASKED = -1.0e30


def rows(i):
    return P if i < PT else DEC


def one_room(nc, ctx, shape, *tensors):
    out = []
    for n, (name, dt) in enumerate(tensors):
        guard = nc.sbuf_tensor(name, shape, dt)
        if n < len(tensors) - 1:
            out.append(guard.__enter__())
            guard.__exit__(None, None, None)
        else:
            out.append(ctx.enter_context(guard))
    return out


class Tally:

    def __init__(self, sem):
        self.sem, self.n, self.turns = sem, 0, 0

    def inc(self, ins, by=1):
        ins.then_inc(self.sem, by)
        self.n += by
        return ins

    @property
    def now(self):
        return self.turns + self.n if not isinstance(self.turns, int) or self.turns else self.n


@contextmanager
def turns(eng, count, per):
    before = {t: t.n for t in per}
    with eng.Fori(0, count) as i:
        for t, by in per.items():
            t.turns = i * by
        yield i
    for t, by in per.items():
        assert t.n - before[t] == by, (t.sem, t.n - before[t], by)
        t.turns = 0
        t.n = before[t] + by * count


def build(nc, x_prompt, x_sample, c_prompt, c_sample, cache_k, cache_v, state_pool,
          w_mod, b_mod, w_in, w_pool, pool_scale, w_out, ln1_g, ln1_b, ln2_g, ln2_b,
          w_group, b_group, w_router, b_router, w_up, w_down,
          y_prompt, y_sample, k_prompt, v_prompt, pool_prompt, k_sample, v_sample, pool_sample):
    def dram(name, shape, dt=F32):
        return nc.dram_tensor(name, shape, dt, kind="Internal").ap()

    mod_d = dram("mod_d", [2, NMOD])
    x1_d = dram("x1_d", [NT, D])
    hn2_d = dram("hn2_d", [NT, D])
    y_d = dram("y_d", [NSLOT, D])

    with ExitStack() as outer:
        def osb(name, shape, dt=F32):
            return outer.enter_context(nc.sbuf_tensor(name, shape, dt))

        ident = osb("ident", [P, P])
        psum = outer.enter_context(nc.psum_tensor("psum", [P, 8, 512], F32))
        logits = osb("logits", [P, TILES, NLOG])
        mhalf = osb("mhalf", [P, 16])
        slots = osb("slots", [P, TILES, 2], I32)
        gates = osb("gates", [P, TILES, 2])
        with ExitStack() as mid:
            proj = mid.enter_context(nc.sbuf_tensor("proj", [P, FC, NT], F32))
            utail = mid.enter_context(nc.sbuf_tensor("utail", [P, 4, 2, HIST], F32))
            block_a(nc, ident, mhalf, psum, proj, utail, mod_d, x_prompt, x_sample, c_prompt,
                    c_sample, w_mod, b_mod, w_in, state_pool)
            block_b(nc, ident, mhalf, psum, proj, utail, logits, mod_d, x1_d, hn2_d, x_prompt,
                    x_sample, y_d, cache_k, cache_v, w_pool, pool_scale, w_out, ln1_g, ln1_b,
                    w_group, b_group, w_router, b_router, k_prompt, v_prompt, pool_prompt,
                    k_sample, v_sample, pool_sample)
        block_c(nc, ident, psum, logits, hn2_d, y_d, slots, gates, w_up, w_down)
        block_d(nc, mhalf, mod_d, x1_d, y_d, slots, gates, ln2_g, ln2_b, y_prompt, y_sample)


def block_a(nc, ident, mhalf, psum, proj, utail, mod_d, x_prompt, x_sample, c_prompt, c_sample,
            w_mod, b_mod, w_in, state_pool):
    with ExitStack() as ctx:
        def sb(name, shape, dt=F32):
            return ctx.enter_context(nc.sbuf_tensor(name, shape, dt))

        def sem(name):
            return ctx.enter_context(nc.semaphore(name))

        wm0a, hn_hi = one_room(nc, ctx, [P, KC, NT], ("wm0a", F32), ("hn_hi", F32R))
        wm0b, hn_lo = one_room(nc, ctx, [P, KC, NT], ("wm0b", F32), ("hn_lo", F32R))
        wm = sb("wm", [P, 2, 2048])
        w_raw = sb("w_raw", [P, 2, KC, P])
        w_hi = sb("w_hi", [P, 2, KC, P], F32R)
        w_lo = sb("w_lo", [P, 2, KC, P], F32R)
        stage = sb("stage", [P, 2, D])
        modf = sb("modf", [P, 4, 4, 2])
        crow = sb("crow", [16, P])
        cT = sb("cT", [P, KC, 32])
        modb = sb("modb", [P, SECS, 512])
        modrow = sb("modrow", [P, SECS, 512])
        hist = sb("hist", [HIST, 512])
        ext = sb("ext", [P, 4, HIST + DEC])
        exs = sb("exs", [P, 2, HIST + DEC])
        rcnt = sb("rcnt", [P, HIST])
        stats = sb("stats", [P, TILES, 2, 6])
        mv = sb("mv", [P, TILES, 2])
        vpe = sb("vpe", [P, TILES])
        rstd = sb("rstd", [P, TILES])
        arena = proj[:, :, :].rearrange("p a b -> p (a b)")
        xp = arena[:, 0:PT * D].rearrange("p (t d) -> p t d", d=D)
        xT = arena[:, PT * D:PT * D + KC * NT].rearrange("p (k c) -> p k c", c=NT)
        wm0 = [r[:, :, :].rearrange("p k c -> p (k c)")[:, 0:KC // 2 * 2048].rearrange("p (k n) -> p k n", n=2048)
               for r in (wm0a, wm0b)]

        c_loaded, hist_loaded, modb_loaded = map(sem, ("c_loaded", "hist_loaded", "modb_loaded"))
        x_loaded = [sem("x_loaded_prompt0"), sem("x_loaded_prompt1"), sem("x_loaded_sample")]
        wm0_loaded = [sem(f"wm0_loaded{n}") for n in range(KC // 2)]
        wm_loaded = [sem("wm_loaded0"), sem("wm_loaded1")]
        w_loaded = [sem("w_loaded0"), sem("w_loaded1")]
        ident0, ident_ready, const_ready = map(sem, ("ident0", "ident_ready", "const_ready"))
        cT_done, cT_ready, hist_ready = map(sem, ("cT_done", "cT_ready", "hist_ready"))
        modb_ready, modb_one = map(sem, ("modb_ready", "modb_one"))
        wm_used, mod_copied, mod_ready, mod_stored = map(sem, ("wm_used", "mod_copied", "mod_ready", "mod_stored"))
        mod_sum0 = sem("mod_sum0")
        modf_done, modf_ready, hn_ready = map(sem, ("modf_done", "modf_ready", "hn_ready"))
        vpe_ready, rstd_ready, a_dve = map(sem, ("vpe_ready", "rstd_ready", "a_dve"))
        xn_ready, xT_done, xT_copied, hi_ready, lo_ready = map(sem, ("xn_ready", "xT_done", "xT_copied", "hi_ready", "lo_ready"))
        w_split, w_hi_ready, proj_done, proj_copied = map(sem, ("w_split", "w_hi_ready", "proj_done", "proj_copied"))
        pool_step = sem("pool_step")

        block = ctx.enter_context(nc.Block())

        @block.sync
        def _(sp):
            sp.dma_start(crow[0:KC, :], c_prompt.rearrange("o (k p) -> (o k) p", p=P)).then_inc(c_loaded, 16)
            sp.dma_start(crow[KC:2 * KC, :], c_sample.rearrange("o (k p) -> (o k) p", p=P)).then_inc(c_loaded, 16)
            sp.dma_start(hist[:, :], state_pool[0, 0]).then_inc(hist_loaded, 16)
            for g in range(2):
                src = x_prompt[0, g * 4 * P:(g + 1) * 4 * P, :].rearrange("(t p) d -> p t d", p=P)
                sp.dma_start(xp[:, 4 * g:4 * g + 4, :], src).then_inc(x_loaded[g], 16)
            sp.dma_start(stage[0:DEC, 0, :], x_sample[0]).then_inc(x_loaded[2], 16)

            def load_w(m, slot):
                src = w_in[0, :, bass.ds(m * P, P)].rearrange("(k p) c -> p k c", p=P)
                sp.dma_start(w_raw[:, slot, :, :], src).then_inc(w_loaded[slot], 16)

            for n in range(KC // 2):
                src = w_mod[0, n * 2 * P:(n + 1) * 2 * P, 0:2048].rearrange("(k p) n -> p k n", p=P)
                sp.dma_start(wm0[n // 2][:, n % 2 * 2:n % 2 * 2 + 2, :], src).then_inc(wm0_loaded[n], 16)
                if n == 0:
                    sp.wait_ge(modb_ready, 1)
                    for b in range(2):
                        sp.dma_start(modb[b:P:32, :, :], b_mod[0].rearrange("(s j n) -> j s n", j=4, n=512)).then_inc(modb_loaded, 16)
            load_w(0, 0)
            load_w(1, 1)
            for m in range(FC):
                if m >= 2:
                    sp.wait_ge(w_split, m - 1)
                    load_w(m, m % 2)
                    sp.wait_ge(wm_used, KC + m - 1)
                sec, k = 1 + m // KC, m % KC
                sp.dma_start(wm[:, m % 2, :], w_mod[0, k * P:(k + 1) * P, sec * 2048:(sec + 1) * 2048]).then_inc(wm_loaded[m % 2], 16)
            sp.wait_ge(mod_stored, 32 * (SECS - 1))

        @block.gpsimd
        def _(pool):
            step = Tally(pool_step)

            def then(ins):
                step.inc(ins)
                pool.wait_ge(pool_step, step.n)

            pool.memset(ident[:, :], 0.0).then_inc(ident0, 1)
            pool.wait_ge(ident0, 1)
            pool.affine_select(out=ident[:, :], in_=ident[:, :], compare_op=ALU.not_equal, fill=1.0, base=0,
                               pattern=[[-1, P]], channel_multiplier=1).then_inc(ident_ready, 1)
            pool.memset(modb[:, :, :], 0.0).then_inc(modb_ready, 1)
            pool.memset(cT[:, :, :], 0.0).then_inc(const_ready, 1)
            pool.memset(mv[:, :, :], 0.0).then_inc(const_ready, 1)
            pool.memset(mhalf[:, :], -0.5).then_inc(const_ready, 1)
            for n in range(HIST):
                pool.memset(rcnt[:, n:n + 1], 1.0 / (n + 1)).then_inc(const_ready, 1)
            pool.wait_ge(const_ready, 3)
            for g, (lo, hi) in enumerate(GROUPS):
                pool.wait_ge(vpe_ready, g + 1)
                pool.tensor_tensor(rstd[:, lo:hi], vpe[:, lo:hi], mhalf[:, lo:hi], ALU.pow).then_inc(rstd_ready, 1)

            def store_mod(sec):
                for b in range(2):
                    pool.dma_start(mod_d[b, sec * 2048:(sec + 1) * 2048].rearrange("(j n) -> j n", j=4),
                                   modrow[b:P:32, sec, :]).then_inc(mod_stored, 16)

            pool.wait_ge(proj_copied, 2 + 4)
            pool.wait_ge(hist_ready, 1)
            for g in range(4):
                u = proj[:, g, :]
                pool.tensor_copy(utail[:, g, 0, :], u[:, SEQ - HIST:SEQ])
                then(pool.tensor_copy(utail[:, g, 1, :], u[:, NT - HIST:NT]))
                src = u[:, 0:SEQ]
                for level in range(g + 1):
                    w = 1 << level
                    dst = stage[:, level % 2, :]
                    pool.tensor_copy(dst[:, 0:w], src[:, 0:w])
                    then(pool.tensor_tensor(dst[:, w:SEQ], src[:, w:SEQ], src[:, 0:SEQ - w], ALU.add))
                    src = dst
                w = WIN[g]
                if w > 2:
                    pool.tensor_tensor(src[:, 0:w - 1], src[:, 0:w - 1], rcnt[:, 0:w - 1], ALU.mult)
                    then(pool.tensor_scalar(src[:, w - 1:SEQ], src[:, w - 1:SEQ], 1.0 / w, None, ALU.mult))
                else:
                    then(pool.tensor_scalar(src[:, 1:SEQ], src[:, 1:SEQ], 0.5, None, ALU.mult))
                then(pool.tensor_tensor(u[:, 0:SEQ], src[:, :], u[:, 0:SEQ], ALU.subtract))
                then(pool.tensor_copy(ext[:, g, HIST:HIST + DEC], u[:, SEQ:NT]))
                src, n = ext[:, g, :], HIST + DEC
                for level in range(g + 1):
                    w = 1 << level
                    n -= w
                    dst = exs[:, level % 2, 0:n]
                    then(pool.tensor_tensor(dst, src[:, w:w + n], src[:, 0:n], ALU.add))
                    src = dst
                then(pool.tensor_scalar(src[:, n - DEC:n], src[:, n - DEC:n], 1.0 / WIN[g], None, ALU.mult))
                then(pool.tensor_tensor(u[:, SEQ:NT], src[:, n - DEC:n], u[:, SEQ:NT], ALU.subtract))
            pool.wait_ge(modb_one, 3)
            for sec in range(1, SECS):
                pool.wait_ge(mod_copied, sec + 1)
                pool.tensor_tensor(modrow[:, sec, :], modrow[:, sec, :], modb[:, sec, :], ALU.add).then_inc(mod_ready, 1)
                pool.wait_ge(mod_ready, sec)
                store_mod(sec)

        @block.tensor
        def _(pe):
            psM = psum[:, 7, :]
            pe.wait_ge(ident_ready, 1)
            pe.wait_ge(c_loaded, 32)
            pe.transpose(psum[:, 6, 0:16], crow[:, :], ident[0:16, 0:16])
            pe.wait_ge(hist_loaded, 16)
            for g in range(4):
                last = pe.transpose(psum[:, 6, 16 + 16 * g:16 + 16 * g + HIST], hist[:, g * P:(g + 1) * P], ident[0:HIST, 0:HIST])
            last.then_inc(cT_done, 1)
            pe.wait_ge(cT_ready, 1)

            def mod_chunk(k, w):
                for j in range(4):
                    mm = pe.matmul(psM[32 * j:32 * j + 32, :], cT[:, k, :], w[:, 512 * j:512 * j + 512],
                                   start=(k == 0), stop=(k == KC - 1), tile_position=(0, 32 * j))
                mm.then_inc(wm_used, 1)

            def turn(t):
                r, slot = rows(t), t % 2
                pe.wait_ge(xn_ready, t + 1)
                if t >= 2:
                    pe.wait_ge(xT_copied, t - 1)
                src = xp[:, t, :] if t < PT else stage[:, 0, :]
                for k in range(KC):
                    mm = pe.transpose(psum[:, 2 * slot + k // 4, (k % 4) * P:(k % 4) * P + r],
                                      src[0:r, k * P:(k + 1) * P], ident[0:r, 0:r])
                mm.then_inc(xT_done, 1)

            for n, tiles in enumerate(((0, 1, 2, 3), (4, 5), (6, 7), (8,))):
                for t in tiles:
                    turn(t)
                pe.wait_ge(wm0_loaded[n], 16)
                for k in (2 * n, 2 * n + 1):
                    mod_chunk(k, wm0[n // 2][:, k % 4, :])
            pe.wait_ge(mod_sum0, 1)
            pe.wait_ge(hist_ready, 1)
            for c in range(4):
                mm = pe.transpose(psum[:, 6, c * P:(c + 1) * P], modrow[:, 0, c * P:(c + 1) * P], ident[:, :])
            mm.then_inc(modf_done, 1)
            with pe.Fori(0, 2) as h:
                for mm_ in range(8):
                    slot = mm_ % 2
                    pe.wait_ge(w_split, h * 8 + mm_ + 1)
                    pe.wait_ge(proj_copied, h * 8 + mm_ + 1)
                    for k in range(KC):
                        if mm_ == 0:
                            pe.wait_ge(lo_ready, k + 1)
                        for w, parts in ((w_hi, (hn_hi, hn_lo)), (w_lo, (hn_hi,))):
                            for hn in parts:
                                for c, (t0, n) in enumerate(CH):
                                    mm = pe.matmul(psum[:, 3 * slot + c, 0:n], w[:, slot, k, :], hn[:, k, t0:t0 + n],
                                                   start=(k == 0 and w is w_hi and hn is hn_hi),
                                                   stop=(k == KC - 1 and w is w_lo))
                    mm.then_inc(proj_done, 1)
                    if mm_ == 0:
                        pe.wait_ge(mod_copied, h + 1)
                    pe.wait_ge(wm_loaded[mm_ % 2], h * 64 + 16 * (mm_ // 2 + 1))
                    mod_chunk(mm_, wm[:, mm_ % 2, :])

        @block.scalar
        def _(act):
            act.sem_inc(proj_copied, 2)
            act.sem_inc(mod_copied, 1)

            for t in range(TILES):
                r, slot = rows(t), t % 2
                act.wait_ge(xT_done, t + 1)
                src = psum[:, 2 * slot:2 * slot + 2, :].rearrange("p b (k c) -> p (b k) c", c=P)[:, :, 0:r]
                act.activation(xT[:, :, t * P:t * P + r], src, ACT.Copy).then_inc(xT_copied, 1)
            for k in range(KC):
                act.wait_ge(hn_ready, k + 1)
                act.activation(hn_hi[:, k, :], xT[:, k, :], ACT.Copy).then_inc(hi_ready, 1)
            with act.Fori(0, 2) as h:
                for mm in range(8):
                    slot = mm % 2
                    act.wait_ge(proj_done, h * 8 + mm + 1)
                    for c, (t0, n) in enumerate(CH):
                        cp = act.activation(proj[:, bass.ds(h * 8 + mm, 1), t0:t0 + n].rearrange("p a n -> p (a n)"),
                                            psum[:, 3 * slot + c, 0:n], ACT.Copy)
                    cp.then_inc(proj_copied, 1)
                act.wait_ge(wm_used, h * 8 + 2 * KC)
                act.activation(modrow[:, bass.ds(h + 1, 1), :].rearrange("p a n -> p (a n)"), psum[:, 7, :], ACT.Copy).then_inc(mod_copied, 1)

        @block.vector
        def _(dve):
            step = Tally(a_dve)

            def then(ins):
                step.inc(ins)
                dve.wait_ge(a_dve, step.now)

            dve.wait_ge(cT_done, 1)
            dve.wait_ge(const_ready, 3)
            for b in range(2):
                cp = dve.tensor_copy(cT[:, :, b], psum[:, 6, b * KC:(b + 1) * KC])
            cp.then_inc(cT_ready, 1)
            dve.tensor_copy(ext[:, :, 0:HIST], psum[:, 6, 16:80].rearrange("p (g c) -> p g c", c=16)[:, :, 0:HIST]).then_inc(hist_ready, 1)
            def split(m, slot, loaded, free):
                dve.wait_ge(w_loaded[slot], loaded)
                if free is not None:
                    dve.wait_ge(proj_done, free)
                dve.tensor_copy(w_hi[:, slot, :, :], w_raw[:, slot, :, :]).then_inc(w_hi_ready, 1)
                dve.wait_ge(w_hi_ready, m + 1)
                dve.tensor_tensor(w_lo[:, slot, :, :], w_raw[:, slot, :, :], w_hi[:, slot, :, :].bitcast(F32),
                                  ALU.subtract).then_inc(w_split, 1)

            for g, (lo, hi) in enumerate(GROUPS):
                dve.wait_ge(x_loaded[g], 16)
                tiles = [(t, rows(t), xp[:, t, :] if t < PT else stage[:, 0, :]) for t in range(lo, hi)]
                for t, r, x in tiles:
                    for half in range(2):
                        st = dve.bn_stats(stats[0:r, t, half, :], x[0:r, half * 512:(half + 1) * 512])
                then(st)
                for t, r, x in tiles:
                    ag = dve.bn_aggr(mv[0:r, t, :], stats[0:r, t, :, :].rearrange("p b n -> p (b n)"))
                then(ag)
                dve.tensor_scalar(vpe[:, lo:hi], mv[:, lo:hi, 1], EPS, None, ALU.add).then_inc(vpe_ready, 1)
                dve.wait_ge(rstd_ready, g + 1)
                for t, r, x in tiles:
                    dve.tensor_scalar(x[0:r, :], x[0:r, :], mv[0:r, t, 0:1], rstd[0:r, t:t + 1], ALU.subtract, ALU.mult).then_inc(xn_ready, 1)
            dve.wait_ge(modb_loaded, 32)
            for lo, hi, sec in ((64, P, 0), (0, 64, 1), (0, P, 2)):
                dve.tensor_scalar(modb[lo:hi, sec, :], modb[lo:hi, sec, :], 1.0, None, ALU.add).then_inc(modb_one, 1)
            dve.wait_ge(modb_one, 3)
            dve.wait_ge(wm_used, KC)
            dve.tensor_tensor(modrow[:, 0, :], psum[:, 7, :], modb[:, 0, :], ALU.add).then_inc(mod_sum0, 1)
            split(0, 0, 16, None)
            dve.wait_ge(modf_done, 1)
            dve.tensor_copy(modf[:, :, :, :], psum[:, 6, :].rearrange("p (c j n) -> p c j n", c=4, j=4)[:, :, :, 0:2]).then_inc(modf_ready, 1)
            dve.wait_ge(modf_ready, 1)
            dve.wait_ge(xT_copied, TILES)

            def low(k):
                dve.wait_ge(hi_ready, k + 1)
                dve.tensor_tensor(hn_lo[:, k, :], xT[:, k, :], hn_hi[:, k, :].bitcast(F32), ALU.subtract).then_inc(lo_ready, 1)

            for k in range(KC):
                c, j = k % 4, k // 4
                for b, (t0, t1) in enumerate(((0, SEQ), (SEQ, NT))):
                    ins = dve.tensor_scalar(xT[:, k, t0:t1], xT[:, k, t0:t1], modf[:, c, 2 + j, b:b + 1], modf[:, c, j, b:b + 1],
                                            ALU.mult, ALU.add)
                ins.then_inc(hn_ready, 1)
                if k:
                    low(k - 1)
            low(KC - 1)
            split(1, 1, 16, None)

            with dve.Fori(0, 7) as i:
                for s in range(2):
                    split(i * 2 + 2 + s, s, i * 16 + 32, i * 2 + 1 + s)


def attention_units():
    units = []
    for order, i in enumerate((PT,) + tuple(range(PT))):
        for p in range(PAIRS):
            q = order * PAIRS + p
            if i < PT:
                n_all = (i + 1) * P
                starts = list(range(0, n_all, 512))[::-1]
                for s0 in starts:
                    n = min(512, n_all - s0)
                    units.append((i, p, 1024 - n_all + s0, n, False, s0, s0 == starts[0], s0 == 0, q))
            else:
                units.append((i, p, 1024 - DEC, DEC, False, SEQ, True, False, q))
                units.append((i, p, 1024 - DEC - PAST, PAST, True, 0, False, True, q))
    return units


def block_b(nc, ident, mhalf, psum, proj, utail, logits, mod_d, x1_d, hn2_d, x_prompt, x_sample,
            y_d, cache_k, cache_v, w_pool, pool_scale, w_out, ln1_g, ln1_b, w_group, b_group,
            w_router, b_router, k_prompt, v_prompt, pool_prompt, k_sample, v_sample, pool_sample):
    units = attention_units()
    nu = len(units)
    with ExitStack() as ctx:
        def sb(name, shape, dt=F32):
            return ctx.enter_context(nc.sbuf_tensor(name, shape, dt))

        def sem(name):
            return ctx.enter_context(nc.semaphore(name))

        v_nat = sb("v_nat", [P, TILES, 512])
        v_old = sb("v_old", [P, PAST // P, 512])
        wo_hi = sb("wo_hi", [P, KC, D], F32R)
        wo_raw, wo_lo = one_room(nc, ctx, [P, KC, D], ("wo_raw", F32), ("wo_lo", F32R))
        stay = sb("stay", [P, 2, 2, 512])
        take, mixin1 = one_room(nc, ctx, [P, 2, 2, 512], ("take", F32), ("mixin1", F32R))
        left = sb("left", [P, 2, 1025])
        aT = sb("aT", [P, 2, 2, 4, P])
        mixin0 = sb("mixin0", [P, 2, KC, P], F32R)
        wgr = sb("wgr", [P, KC, NLOG])
        blog = sb("blog", [P, NLOG])
        wp = sb("wp", [P, 4, P])
        psc = sb("psc", [P, 4])
        identb = sb("identb", [P, P], BF16)
        mask = sb("mask", [P, P], BF16)
        zeros = sb("zeros", [P, 256])
        st1 = sb("st1", [P, 2, 6])
        mv1 = sb("mv1", [P, 2])
        ve = sb("ve", [P, 2])
        rs = sb("rs", [P, 2])
        vroom = proj[:, 12:16, :].rearrange("p a b -> p (a b)")
        k_old = vroom[:, 0:4 * PAST].rearrange("p (a b) -> p a b", b=PAST)
        vo_room = v_old[:, :, :].rearrange("p a b -> p (a b)")
        vn_room = v_nat[:, :, :].rearrange("p a b -> p (a b)")
        g1, sc2, sh2, l1g = [vroom[:, n * D:(n + 1) * D] for n in range(4)]
        l1b, xb = [vo_room[:, n * D:(n + 1) * D] for n in range(2)]
        g1s, sc2s, sh2s = [vn_room[:, n * D:(n + 1) * D] for n in range(3)]
        res = stay[:, :, :, :].rearrange("p a b c -> p a (b c)")
        mixin1 = mixin1[:, :, :, :].rearrange("p a b c -> p a (b c)").rearrange("p a (k c) -> p a k c", c=P)
        hn2 = aT[:, :, :, :, :].rearrange("p a b c d -> p a (b c d)")
        hn2T = left[:, :, :].rearrange("p a b -> p (a b)")[:, 0:D].rearrange("p (k c) -> p k c", c=P)
        mixin = [mixin0[:, :, :, :], mixin1]
        k_st = stay[:, :, 0, :]
        tail_st = stay[0:HIST, :, 1, :]
        kc = take[:, :, :, :].rearrange("p a b c -> p (a b) c")

        w_loaded, wo_loaded, rows_in, kc_loaded = map(sem, ("bw_loaded", "wo_loaded", "rows_in", "kc_loaded"))
        wo_hi_ready, wo_split, mix_hi_ready, mix_lo_ready = map(sem, ("wo_hi_ready", "wo_split", "mix_hi_ready", "mix_lo_ready"))
        b_const0, b_const = map(sem, ("b_const0", "b_const"))
        kv_turned, k_copied, v_copied = map(sem, ("kv_turned", "k_copied", "v_copied"))
        k_stored = [sem("k_stored0"), sem("k_stored1")]
        out_stored = sem("out_stored")
        tail_turned, tail_copied = map(sem, ("tail_turned", "tail_copied"))
        old_turned, old_copied = map(sem, ("old_turned", "old_copied"))
        pool_mixed, pool_copied = map(sem, ("pool_mixed", "pool_copied"))
        z_done, stay_ready, take_ready, left_ready, a_ready = map(sem, ("z_done", "stay_ready", "take_ready", "left_ready", "a_ready"))
        a_turned, aT_copied, pv_done, att_copied = map(sem, ("a_turned", "aT_copied", "pv_done", "att_copied"))
        mix_done, mix_copied = map(sem, ("mix_done", "mix_copied"))
        xb_loaded, res_ready, b_dve = map(sem, ("xb_loaded", "res_ready", "b_dve"))
        var_ready, rstd_ready = map(sem, ("var_ready", "b_rstd_ready"))
        n1_ready, x1_mid, x1_ready, n2_ready, hn2_mid, hn2_ready = map(sem, ("n1_ready", "x1_mid", "x1_ready", "n2_ready", "hn2_mid", "hn2_ready"))
        x1_stored = [sem("x1_stored0"), sem("x1_stored1")]
        hn2_stored = [sem("hn2_stored0"), sem("hn2_stored1")]
        h_turned, h_copied, logits_done, logits_copied = map(sem, ("h_turned", "h_copied", "logits_done", "logits_copied"))
        sample_rows = sem("sample_rows")
        POOL_PIECES = ((0, 512), (512, 512), (SEQ, DEC))
        POOL_FROM = 2
        sample_units = sum(u[0] == PT for u in units)
        zeros_ready, spare_zeroed = map(sem, ("zeros_ready", "spare_zeroed"))

        block = ctx.enter_context(nc.Block())

        def mod_row(dst, b, part):
            return dst, mod_d[b, part * D:(part + 1) * D].partition_broadcast(P)

        @block.sync
        def _(sp):
            sp.dma_start(kc, cache_k[0, 0].rearrange("(s p) h d -> p s (h d)", p=P)).then_inc(kc_loaded, 16)
            sp.dma_start(wp[:, :, :], w_pool[0].rearrange("g c d -> c g d")).then_inc(w_loaded, 16)
            sp.dma_start(psc[:, :], pool_scale[0].rearrange("(g p) -> p g", p=P), allow_slow_non_contiguous=True).then_inc(w_loaded, 16)
            sp.dma_start(v_old[:, :, :], cache_v[0, 0].rearrange("(s p) h d -> p s (h d)", p=P)).then_inc(w_loaded, 16)
            sp.dma_start(wgr[:, :, 0:NG], w_group[0].rearrange("(k p) n -> p k n", p=P)).then_inc(w_loaded, 16)
            sp.dma_start(wgr[:, :, NG:NLOG], w_router[0].rearrange("(k p) n -> p k n", p=P)).then_inc(w_loaded, 16)
            sp.dma_start(blog[:, 0:NG], b_group[0].partition_broadcast(P)).then_inc(w_loaded, 16)
            sp.dma_start(blog[:, NG:NLOG], b_router[0].partition_broadcast(P)).then_inc(w_loaded, 16)
            for t in range(TILES):
                r = rows(t)
                ko, vo = (k_prompt[0, 0, t * P:t * P + r], v_prompt[0, 0, t * P:t * P + r]) if t < PT else (k_sample[0, 0], v_sample[0, 0])
                sp.wait_ge(k_copied, t + 1)
                sp.dma_start(ko.rearrange("t h d -> t (h d)"), k_st[0:r, t % 2, :]).then_inc(k_stored[t % 2], 16)
                sp.wait_ge(v_copied, t + 1)
                sp.dma_start(vo.rearrange("t h d -> t (h d)"), v_nat[0:r, t, :]).then_inc(out_stored, 16)
            sp.wait_ge(tail_copied, 2)
            sp.dma_start(pool_prompt[0, 0], tail_st[:, 0, :]).then_inc(out_stored, 16)
            sp.dma_start(pool_sample[0, 0], tail_st[:, 1, :]).then_inc(out_stored, 16)

            sp.dma_start(wo_raw[:, :, :], w_out[0].rearrange("(k p) n -> p k n", p=P)).then_inc(wo_loaded, 16)
            sp.wait_ge(pv_done, sample_units)
            for dst, src in (mod_row(g1, 0, 2), mod_row(sh2, 0, 3), mod_row(sc2, 0, 4),
                             (l1g, ln1_g[0].partition_broadcast(P)), (l1b, ln1_b[0].partition_broadcast(P))):
                sp.dma_start(dst, src).then_inc(rows_in, 16)
            def load_x(j):
                src = x_prompt[0, j * P:(j + 1) * P, :] if j < PT else x_sample[0]
                sp.dma_start(xb[0:rows(j), :], src).then_inc(xb_loaded, 16)

            def store_hn2(j):
                sp.wait_ge(hn2_ready, j + 1)
                sp.dma_start(hn2_d[j * P:j * P + rows(j), :], hn2[0:rows(j), j % 2, :]).then_inc(hn2_stored[j % 2], 16)

            load_x(0)
            sp.wait_ge(pv_done, nu)
            for dst, src in (mod_row(g1s, 1, 2), mod_row(sh2s, 1, 3), mod_row(sc2s, 1, 4)):
                sp.dma_start(dst, src).then_inc(sample_rows, 16)
            for j in range(TILES):
                if j + 1 < TILES:
                    sp.wait_ge(res_ready, j + 1)
                    load_x(j + 1)
                sp.wait_ge(x1_ready, j + 1)
                sp.dma_start(x1_d[j * P:j * P + rows(j), :], res[0:rows(j), j % 2, :]).then_inc(x1_stored[j % 2], 16)
                if j >= 1:
                    store_hn2(j - 1)
            store_hn2(PT)
            sp.wait_ge(k_stored[0], 16 * 5)
            sp.wait_ge(k_stored[1], 16 * 4)
            sp.wait_ge(out_stored, 16 * (TILES + 2))
            for q in (x1_stored, hn2_stored):
                sp.wait_ge(q[0], 16 * 5)
                sp.wait_ge(q[1], 16 * 4)

        @block.gpsimd
        def _(pool):
            pool.memset(zeros[:, :], 0.0).then_inc(zeros_ready, 1)
            pool.memset(mask[:, :], MASKED).then_inc(b_const0, 1)
            pool.tensor_copy(identb[:, :], ident[:, :]).then_inc(b_const, 1)
            pool.memset(left[:, :, 1024:1025], 1.0).then_inc(b_const, 1)
            pool.memset(logits[:, PT, :], 0.0).then_inc(b_const, 1)
            pool.wait_ge(b_const0, 1)
            pool.affine_select(out=mask[:, :], in_=mask[:, :], compare_op=ALU.is_ge, fill=0.0, base=0,
                               pattern=[[1, P]], channel_multiplier=-1).then_inc(b_const, 1)
            pool.wait_ge(rows_in, 16 * 5)
            pool.wait_ge(zeros_ready, 1)
            spare = y_d[SLOT_TILES_MIN * P:NSLOT, :].rearrange("(p a) (b n) -> p (a b) n", p=P, n=256)
            pool.dma_start(spare, zeros[:, None, :].broadcast_to(list(spare.shape))).then_inc(spare_zeroed, 16)
            for j in range(TILES):
                r, s = rows(j), j % 2
                pool.wait_ge(var_ready, 2 * j + 1)
                pool.tensor_tensor(rs[:, 0:1], ve[:, 0:1], mhalf[:, 0:1], ALU.pow).then_inc(rstd_ready, 1)
                pool.wait_ge(n1_ready, j + 1)
                pool.tensor_tensor(res[0:r, s, :], res[0:r, s, :], l1g[0:r, :], ALU.mult).then_inc(x1_mid, 1)
                pool.wait_ge(x1_mid, j + 1)
                pool.tensor_tensor(res[0:r, s, :], res[0:r, s, :], l1b[0:r, :], ALU.add).then_inc(x1_ready, 1)
                pool.wait_ge(var_ready, 2 * j + 2)
                pool.tensor_tensor(rs[:, 1:2], ve[:, 1:2], mhalf[:, 0:1], ALU.pow).then_inc(rstd_ready, 1)
                pool.wait_ge(n2_ready, j + 1)
                if j == PT:
                    pool.wait_ge(sample_rows, 48)
                scale, shift = (sc2, sh2) if j < PT else (sc2s, sh2s)
                pool.tensor_tensor(hn2[0:r, s, :], hn2[0:r, s, :], scale[0:r, :], ALU.mult).then_inc(hn2_mid, 1)
                pool.wait_ge(hn2_mid, j + 1)
                pool.tensor_tensor(hn2[0:r, s, :], hn2[0:r, s, :], shift[0:r, :], ALU.add).then_inc(hn2_ready, 1)
            pool.wait_ge(spare_zeroed, 16)

        @block.tensor
        def _(pe):
            for t in range(TILES):
                r, s = rows(t), t % 2
                if t >= 2:
                    pe.wait_ge(k_copied, t - 1)
                    pe.wait_ge(v_copied, t - 1)
                for f in range(4):
                    pe.transpose(psum[0:r, 2 * s, f * P:(f + 1) * P], proj[:, 8 + f, t * P:t * P + r], ident[:, :])
                for f in range(4):
                    mm = pe.transpose(psum[0:r, 2 * s + 1, f * P:(f + 1) * P], proj[:, 12 + f, t * P:t * P + r], ident[:, :])
                mm.then_inc(kv_turned, 1)
            for b in range(2):
                for g in range(4):
                    mm = pe.transpose(psum[0:HIST, 4 + b, g * P:(g + 1) * P], utail[:, g, b, :], ident[:, :])
            mm.then_inc(tail_turned, 1)
            pe.wait_ge(kc_loaded, 16)
            pe.wait_ge(k_copied, TILES)
            pe.wait_ge(v_copied, TILES)
            for p in range(PAIRS):
                for s in range(4):
                    mm = pe.transpose(psum[:, p, s * P:(s + 1) * P], kc[:, s, p * P:(p + 1) * P], ident[:, :])
            mm.then_inc(old_turned, 1)
            pe.wait_ge(w_loaded, 16 * 7)

            def pool_map(n):
                g, (t0, w) = n // 3, POOL_PIECES[n % 3]
                if n:
                    pe.wait_ge(pool_copied, n)
                pe.matmul(psum[:, 7, 0:w], wp[:, g, :], proj[:, g, t0:t0 + w], start=True, stop=True).then_inc(pool_mixed, 1)

            pe.wait_ge(old_copied, 1)
            pe.wait_ge(b_const, 4)

            def scores(u):
                i, p, at, n, old, s0, top, *_ = units[u]
                r, s = rows(i), u % 2
                if u >= 2:
                    pe.wait_ge(take_ready, u - 1)
                for h in range(2):
                    qT = proj[64 * h:64 * h + 64, 4 + p, i * P:i * P + r]
                    k = k_old[64 * h:64 * h + 64, p, :] if old else proj[64 * h:64 * h + 64, 8 + p, s0:s0 + n]
                    mm = pe.matmul(psum[0:r, 2 * s + h, 0:n], qT, k, start=True, stop=not top)
                if top:
                    for h in range(2):
                        lo = 64 * h if r == DEC else 0
                        mm = pe.matmul(psum[0:r, 2 * s + h, n - r:n], identb[lo:lo + r, lo:lo + r], mask[lo:lo + r, lo:lo + r],
                                       start=False, stop=True)
                mm.then_inc(z_done, 1)

            def turn(u):
                i, p, at, n, *_ = units[u]
                r, s = rows(i), u % 2
                pe.wait_ge(a_ready, u + 1)
                for h in range(2):
                    if u >= 1:
                        pe.wait_ge(aT_copied, 2 * u - 1 + h)
                    for b in range(0, n, P):
                        m = min(P, n - b)
                        mm = pe.transpose(psum[0:m, 4 + h, b:b + r], take[0:r, s, h, b:b + m], ident[0:r, 0:r])
                    mm.then_inc(a_turned, 1)

            def values(u):
                i, p, at, n, old, s0, top, bottom, q = units[u]
                r, s = rows(i), u % 2
                pe.wait_ge(aT_copied, 2 * u + 2)
                if top and q:
                    pe.wait_ge(att_copied, q)
                nb = -(-n // P)
                for b in range(nb):
                    m = min(P, n - b * P)
                    v = v_old[0:m, b, :] if old else v_nat[0:m, s0 // P + b, :]
                    for h in range(2):
                        c = p * P + 64 * h
                        mm = pe.matmul(psum[64 * h:64 * h + 64, 6, 0:r], v[:, c:c + 64], aT[0:m, s, h, b, 0:r],
                                       start=(top and b == 0), stop=(bottom and b == nb - 1))
                mm.then_inc(pv_done, 1)

            def mix(j):
                r, s = rows(j), j % 2
                pe.wait_ge(mix_lo_ready, j + 1)
                pe.wait_ge(wo_split, KC)
                if j >= 2:
                    pe.wait_ge(mix_copied, j - 1)
                if j == 0:
                    pe.wait_ge(take_ready, nu)
                for k in range(KC):
                    for part, w in ((0, wo_hi), (0, wo_lo), (1, wo_hi)):
                        for half in range(2):
                            mm = pe.matmul(psum[0:r, 2 * s + half, :], mixin[s][:, part, k, 0:r], w[:, k, 512 * half:512 * half + 512],
                                           start=(k == 0 and part == 0 and w is wo_hi), stop=(k == KC - 1 and part == 1))
                mm.then_inc(mix_done, 1)

            def turn_h(j):
                r = rows(j)
                pe.wait_ge(hn2_ready, j + 1)
                if j:
                    pe.wait_ge(h_copied, j)
                for k in range(KC):
                    mm = pe.transpose(psum[:, 4 + k // 4, (k % 4) * P:(k % 4) * P + r], hn2[0:r, j % 2, k * P:(k + 1) * P], ident[0:r, 0:r])
                mm.then_inc(h_turned, 1)

            def router(j):
                r = rows(j)
                pe.wait_ge(h_copied, j + 1)
                if j:
                    pe.wait_ge(logits_copied, j)
                for k in range(KC):
                    mm = pe.matmul(psum[0:r, 7, 0:NLOG], hn2T[:, k, 0:r], wgr[:, k, :], start=(k == 0), stop=(k == KC - 1))
                mm.then_inc(logits_done, 1)

            for u in range(nu + 2):
                if u < nu:
                    scores(u)
                if 0 <= u - POOL_FROM < 12:
                    pool_map(u - POOL_FROM)
                if 1 <= u <= nu:
                    turn(u - 1)
                if u >= 2:
                    values(u - 2)
            for j in range(TILES + 2):
                if j < TILES:
                    mix(j)
                if j >= 2:
                    turn_h(j - 2)
                    router(j - 2)

        @block.scalar
        def _(act):
            for t in range(TILES):
                r, s = rows(t), t % 2
                act.wait_ge(kv_turned, t + 1)
                if t >= 2:
                    act.wait_ge(k_stored[s], 16 * (t // 2))
                act.activation(k_st[0:r, s, :], psum[0:r, 2 * s, :], ACT.Copy).then_inc(k_copied, 1)
            act.wait_ge(w_loaded, 16 * 7)
            act.wait_ge(tail_turned, 1)
            for b in range(2):
                act.activation(tail_st[:, b, :], psum[0:HIST, 4 + b, :], ACT.Copy).then_inc(tail_copied, 1)
            act.wait_ge(old_turned, 1)
            act.activation(k_old, psum[:, 0:4, :], ACT.Copy).then_inc(old_copied, 1)
            act.wait_ge(k_stored[0], 16 * 5)
            act.wait_ge(k_stored[1], 16 * 4)
            act.wait_ge(out_stored, 16 * (TILES + 2))

            def sticks(u):
                i, p, at, n, *_ = units[u]
                r, s = rows(i), u % 2
                act.wait_ge(z_done, u + 1)
                if u >= 2:
                    act.wait_ge(a_ready, u - 1)
                act.activation(stay[0:r, s, :, 0:n], psum[0:r, 2 * s:2 * s + 2, 0:n], ACT.Sigmoid, scale=-0.125).then_inc(stay_ready, 1)
                if u >= 2:
                    act.wait_ge(a_turned, 2 * (u - 1))
                act.activation(take[0:r, s, :, 0:n], psum[0:r, 2 * s:2 * s + 2, 0:n], ACT.Sigmoid, scale=0.125).then_inc(take_ready, 1)

            def copy_pool(n):
                g, (t0, w) = n // 3, POOL_PIECES[n % 3]
                act.wait_ge(pool_mixed, n + 1)
                act.activation(proj[:, g, t0:t0 + w], psum[:, 7, 0:w], ACT.Copy, scale=psc[:, g:g + 1]).then_inc(pool_copied, 1)

            def copy_aT(u):
                i, p, at, n, *_ = units[u]
                r, s, nb = rows(i), u % 2, -(-n // P)
                m = min(P, n)
                for h in range(2):
                    act.wait_ge(a_turned, 2 * u + h + 1)
                    if u >= 2 and h == 0:
                        act.wait_ge(pv_done, u - 1)
                    src = psum[0:m, 4 + h, :].rearrange("p (b c) -> p b c", c=P)[:, 0:nb, 0:r]
                    act.activation(aT[0:m, s, h, 0:nb, 0:r], src, ACT.Copy).then_inc(aT_copied, 1)

            def mix_high(j):
                r, s = rows(j), j % 2
                if j >= 2:
                    act.wait_ge(mix_done, j - 1)
                if j == 1:
                    act.wait_ge(a_turned, 2 * nu)
                act.activation(mixin[s][:, 0, :, 0:r], proj[:, 0:KC, j * P:j * P + r], ACT.Copy).then_inc(mix_hi_ready, 1)

            def copy_h(j):
                r = rows(j)
                act.wait_ge(h_turned, j + 1)
                if j:
                    act.wait_ge(logits_done, j)
                for half in range(2):
                    src = psum[:, 4 + half, :].rearrange("p (k c) -> p k c", c=P)[:, :, 0:r]
                    cp = act.activation(hn2T[:, 4 * half:4 * half + 4, 0:r], src, ACT.Copy)
                cp.then_inc(h_copied, 1)

            for u in range(nu + 1):
                if u < nu:
                    sticks(u)
                if u >= 1:
                    copy_aT(u - 1)
                if 0 <= u - POOL_FROM < 12:
                    copy_pool(u - POOL_FROM)
            act.wait_ge(att_copied, TILES * PAIRS)
            mix_high(0)
            mix_high(1)
            for j in range(TILES):
                if j + 2 < TILES:
                    mix_high(j + 2)
                copy_h(j)

        @block.vector
        def _(dve):
            step = Tally(b_dve)

            def then(ins):
                step.inc(ins)
                dve.wait_ge(b_dve, step.n)

            for t in range(TILES):
                r, s = rows(t), t % 2
                dve.wait_ge(kv_turned, t + 1)
                dve.tensor_copy(v_nat[0:r, t, :], psum[0:r, 2 * s + 1, :]).then_inc(v_copied, 1)
            dve.wait_ge(b_const, 4)

            def weights(u):
                i, p, at, n, old, s0, top, *_ = units[u]
                r, s = rows(i), u % 2
                dve.wait_ge(stay_ready, u + 1)
                if u:
                    dve.wait_ge(a_ready, u)
                for h in range(2):
                    first = 1.0 if top else left[0:r, h, at + n:at + n + 1]
                    w = stay[0:r, s, h, 0:n][:, ::-1]
                    ins = dve.tensor_tensor_scan(left[0:r, h, at:at + n][:, ::-1], w, w, first, ALU.mult, ALU.bypass)
                ins.then_inc(left_ready, 1)
                dve.wait_ge(take_ready, u + 1)
                dve.wait_ge(left_ready, u + 1)
                dve.tensor_tensor(take[0:r, s, :, 0:n], take[0:r, s, :, 0:n], left[0:r, :, at + 1:at + 1 + n], ALU.mult).then_inc(a_ready, 1)

            def copy_att(u):
                i, p = units[u][0:2]
                r = rows(i)
                dve.wait_ge(pv_done, u + 1)
                dve.tensor_copy(proj[:, 4 + p, i * P:i * P + r], psum[:, 6, 0:r]).then_inc(att_copied, 1)

            def split_wo(k):
                if k == 0:
                    dve.wait_ge(wo_loaded, 16)
                raw = wo_raw[:, k, :]
                dve.tensor_copy(wo_hi[:, k, :], raw).then_inc(wo_hi_ready, 1)
                dve.wait_ge(wo_hi_ready, k + 1)
                dve.tensor_tensor(wo_lo[:, k, :], raw, wo_hi[:, k, :].bitcast(F32), ALU.subtract).then_inc(wo_split, 1)

            def mix_low(j):
                r, s = rows(j), j % 2
                dve.wait_ge(mix_hi_ready, j + 1)
                dve.tensor_tensor(mixin[s][:, 1, :, 0:r], proj[:, 0:KC, j * P:j * P + r], mixin[s][:, 0, :, 0:r].bitcast(F32),
                                  ALU.subtract).then_inc(mix_lo_ready, 1)

            def copy_mix(j):
                r, s = rows(j), j % 2
                dve.wait_ge(mix_done, j + 1)
                if j >= 2:
                    dve.wait_ge(x1_stored[s], 16 * (j // 2))
                if j == PT:
                    dve.wait_ge(sample_rows, 48)
                gate = g1 if j < PT else g1s
                dve.tensor_tensor(res[0:r, s, :], psum[0:r, 2 * s:2 * s + 2, :].rearrange("p b n -> p (b n)"), gate[0:r, :],
                                  ALU.mult).then_inc(mix_copied, 1)

            def moments(src, r, j, which):
                for half in range(2):
                    st = dve.bn_stats(st1[0:r, half, :], src[:, half * 512:(half + 1) * 512])
                then(st)
                then(dve.bn_aggr(mv1[0:r, :], st1[0:r, :, :].rearrange("p b n -> p (b n)")))
                dve.tensor_scalar(ve[0:r, which:which + 1], mv1[0:r, 1:2], EPS, None, ALU.add).then_inc(var_ready, 1)

            def residual(j):
                r, s = rows(j), j % 2
                dve.wait_ge(xb_loaded, 16 * (j + 1))
                dve.wait_ge(mix_copied, j + 1)
                dve.scalar_tensor_tensor(out=res[0:r, s, :], in0=xb[0:r, :], scalar=ALPHA, in1=res[0:r, s, :],
                                         op0=ALU.mult, op1=ALU.add).then_inc(res_ready, 1)
                dve.wait_ge(res_ready, j + 1)
                moments(res[0:r, s, :], r, j, 0)

            def norm1(j):
                r, s = rows(j), j % 2
                dve.wait_ge(rstd_ready, 2 * j + 1)
                dve.tensor_scalar(res[0:r, s, :], res[0:r, s, :], mv1[0:r, 0:1], rs[0:r, 0:1], ALU.subtract, ALU.mult).then_inc(n1_ready, 1)

            def norm2(j):
                r, s = rows(j), j % 2
                dve.wait_ge(rstd_ready, 2 * j + 2)
                if j >= 2:
                    dve.wait_ge(hn2_stored[s], 16 * (j // 2))
                    dve.wait_ge(h_turned, j - 1)
                dve.tensor_scalar(hn2[0:r, s, :], res[0:r, s, :], mv1[0:r, 0:1], rs[0:r, 1:2], ALU.subtract, ALU.mult).then_inc(n2_ready, 1)

            def copy_logits(j):
                r = rows(j)
                dve.wait_ge(logits_done, j + 1)
                dve.tensor_tensor(logits[0:r, j, :], psum[0:r, 7, 0:NLOG], blog[0:r, :], ALU.add).then_inc(logits_copied, 1)

            dve.wait_ge(w_loaded, 16 * 7)
            for u in range(nu + 2):
                if u < nu:
                    weights(u)
                if u >= 2 and units[u - 2][7]:
                    copy_att(u - 2)
                if u % 2 == 0 and 8 <= u < 8 + 2 * KC:
                    split_wo(u // 2 - 4)
            dve.wait_ge(rows_in, 16 * 5)
            mix_low(0)
            for j in range(TILES + 1):
                if j + 1 < TILES:
                    mix_low(j + 1)
                if j >= 1:
                    dve.wait_ge(x1_ready, j)
                    moments(res[0:rows(j - 1), (j - 1) % 2, :], rows(j - 1), j - 1, 1)
                    norm2(j - 1)
                if j < TILES:
                    copy_mix(j)
                    residual(j)
                    norm1(j)
                if j >= 2:
                    copy_logits(j - 2)
            copy_logits(TILES - 1)


def block_c(nc, ident, psum, logits, hn2_d, y_d, slots, gates, w_up, w_down):
    with ExitStack() as ctx:
        def sb(name, shape, dt=F32):
            return ctx.enter_context(nc.sbuf_tensor(name, shape, dt))

        def sem(name):
            return ctx.enter_context(nc.semaphore(name))

        NW = 3
        MADE_SO = "the routing tables are made on chip within these bounds"
        TC = SLOT_TILES + 2
        UP, DN = KC * 2 * DE, 2 * D
        WE = UP + DN
        we_hi = sb("we_hi", [P, NW * WE], F32R)
        we_raw, we_lo = one_room(nc, ctx, [P, NW * WE], ("we_raw", F32), ("we_lo", F32R))
        xg = sb("xg", [P, 2, D])
        outs, onehot = one_room(nc, ctx, [P, 3, D], ("outs", F32), ("onehot", F32R))
        xf = outs[:, 2, :].rearrange("p (k c) -> p k c", c=P)
        x_hi = sb("x_hi", [P, 2, KC, P], F32R)
        x_lo = sb("x_lo", [P, 2, KC, P], F32R)
        au = sb("au", [P, 2 * DE])
        sg = sb("sg", [P, DE])
        actv = sb("actv", [P, DE])
        atf = sb("atf", [P, 2, P])
        at_hi = sb("at_hi", [P, 2, P], F32R)
        at_lo = sb("at_lo", [P, 2, P], F32R)
        yst = outs[:, 0:2, :]
        prio = sb("prio", [P, 4])
        gmax = sb("gmax", [P, TILES, 1])
        gsh = sb("gsh", [P, TILES, NG])
        goh = sb("goh", [P, TILES, NG])
        gex = sb("gex", [P, TILES, NG])
        pg = sb("pg", [P, TILES, 1])
        sel = sb("sel", [P, TILES, NE])
        el = sb("el", [P, TILES, EPG])
        tmp4 = sb("tmp4", [P, TILES, EPG])
        l1, l2 = sb("l1", [P, TILES, 1]), sb("l2", [P, TILES, 1])
        best = sb("best", [P, TILES, 1])
        oh = [sb("oh1", [P, TILES, EPG]), sb("oh2", [P, TILES, EPG])]
        e12 = [sb("e1", [P, TILES, NE]), sb("e2", [P, TILES, NE])]
        both = sb("both", [P, TILES, NE])
        rank = sb("rank", [P, TILES, NE])
        before = sb("before", [P, TILES + 1, NE])
        cnt = sb("cnt", [P, TILES, NE])
        tri = sb("tri", [P, P])
        ones = sb("ones", [P, P])
        needf = sb("needf", [P, NE])
        needi = sb("needi", [P, NE], I32)
        cum = sb("cum", [P, NE])
        base = sb("base", [P, NE])
        sv = sb("sv", [P, TILES, NE])
        slotf = sb("slotf", [P, TILES, 2])
        posi = sb("posi", [P, TILES, 2], I32)
        posf = sb("posf", [P, TILES, 2])
        stf = sb("stf", [P, TILES, 2])
        tiota = sb("tiota", [P, TC])
        ciota = sb("ciota", [P, P])
        tokid = sb("tokid", [P, TILES])
        onp = onehot[:, :, :].rearrange("p a b -> p (a b)")[:, 0:TILES * 2 * P].rearrange("p (t c n) -> p t c n", c=2, n=P)
        ont = sb("ont", [P, TILES, 2, 3, TC], F32R)
        xg_room = xg[:, :, :].rearrange("p a b -> p (a b)")
        cmp = xg_room[:, 0:TC * NE].rearrange("p (t e) -> p t e", e=NE)
        onf = xg_room[:, TC * NE:TC * NE + TILES * 2 * TC].rearrange("p (t c n) -> p t c n", c=2, n=TC)
        g_hi = sb("g_hi", [P, TILES, 2], F32R)
        g_lo = sb("g_lo", [P, TILES, 2])
        gslot = sb("gslot", [P, TC])
        texpf = sb("texpf", [P, TC])
        tab = sb("tab", [P, TC], I32)
        texp = sb("texp", [P, TC], I32)
        tpack = sb("tpack", [P, TC + 1])
        tq = sb("tq", [P, TC], I32)
        tqf = sb("tqf", [P, TC])
        cumi = sb("cumi", [P, NE], I32)
        ntile = sb("ntile", [P, 1], I32)
        ntf = sb("ntf", [P, 1])
        ids = sb("ids", [P, TC], I32)
        idst = sb("idst", [P, 2], I32)

        r_const, r_dve, r_exp, r_shift, r_both, r_counts = map(sem, ("r_const", "r_dve", "r_exp", "r_shift", "r_both", "r_counts"))
        oneh_ready, tables_ready, ids_ready = map(sem, ("oneh_ready", "tables_ready", "ids_ready"))
        oneh_used = sem("oneh_used")
        up_loaded = [sem(f"up_loaded{s}") for s in range(NW)]
        down_loaded = [sem(f"down_loaded{s}") for s in range(NW)]
        wh_ready, up_ready, down_ready = map(sem, ("wh_ready", "up_ready", "down_ready"))
        gathered = [sem("gathered0"), sem("gathered1")]
        idst_ready = sem("idst_ready")
        x_turned, x_copied, x_ready = map(sem, ("x_turned", "x_copied", "x_ready"))
        up_done, au_copied, act_mid, act_ready = map(sem, ("up_done", "au_copied", "act_mid", "act_ready"))
        act_turned, at_copied, at_ready = map(sem, ("act_turned", "at_copied", "at_ready"))
        down_done, y_copied = map(sem, ("down_done", "y_copied"))
        y_stored = [sem("y_stored0"), sem("y_stored1")]
        y_complete = sem("y_complete")

        def wide(ap, n):
            return ap.broadcast_to(list(ap.shape[:-1]) + [n])

        block = ctx.enter_context(nc.Block())

        @block.sync
        def _(sp):
            def load(e, s, last):
                up = w_up[0, bass.ds(e, 1)].rearrange("a (k p) n -> p (a k) n", p=P)
                dn = w_down[0, bass.ds(e, 1)].rearrange("a (k p) n -> p (a k) n", p=P)
                at = s * WE
                if last is not None:
                    sp.wait_ge(up_done, last + 1)
                sp.dma_start(we_raw[:, at:at + UP].rearrange("p (k n) -> p k n", k=KC), up).then_inc(up_loaded[s], 16)
                if last is not None:
                    sp.wait_ge(down_done, last + 1)
                sp.dma_start(we_raw[:, at + UP:at + WE].rearrange("p (k n) -> p k n", k=2), dn).then_inc(down_loaded[s], 16)

            def tiles_to(e):
                return sp.value_load(cumi[0:1, bass.ds(e, 1)], min_val=0, max_val=SLOT_TILES)

            for e in range(NW):
                load(e, e, None)
            sp.wait_ge(tables_ready, 1)
            with sp.Fori(1, NE // NW) as i:
                for s in range(NW):
                    load(i * NW + s, s, tiles_to(i * NW + (s - NW)))
            for e in range(NE // NW * NW, NE):
                load(e, e % NW, tiles_to(e - NW))
            sp.wait_ge(y_complete, 1)

        @block.vector
        def _(dve):
            step = Tally(r_dve)

            def then(ins):
                step.inc(ins)
                dve.wait_ge(r_dve, step.n)

            G = logits[:, :, 0:NG]
            dve.wait_ge(r_const, 5)

            def pick(dst, v, top):
                then(dve.tensor_reduce(top[:, :, :].rearrange("p t a -> p (t a)"), v, AX_X, ALU.max))
                then(dve.tensor_tensor(tmp4[:, :, :], v, wide(top[:, :, :], 4), ALU.is_equal))
                then(dve.tensor_tensor(tmp4[:, :, :], tmp4[:, :, :], prio[:, None, :].broadcast_to([P, TILES, 4]), ALU.mult))
                then(dve.tensor_reduce(best[:, :, :].rearrange("p t a -> p (t a)"), tmp4[:, :, :], AX_X, ALU.max))
                then(dve.tensor_tensor(dst, tmp4[:, :, :], wide(best[:, :, :], 4), ALU.is_equal))

            pick(goh[:, :, :], G, gmax)
            dve.tensor_tensor(gsh[:, :, :], G, wide(gmax[:, :, :], NG), ALU.subtract).then_inc(r_shift, 1)
            sel4 = sel[:, :, :].rearrange("p t (g e) -> p t g e", g=NG)
            then(dve.tensor_tensor(sel4, logits[:, :, NG:NLOG].rearrange("p t (g e) -> p t g e", g=NG),
                                   goh[:, :, :, None].broadcast_to([P, TILES, NG, EPG]), ALU.mult))
            then(dve.tensor_reduce(el[:, :, :], sel[:, :, :].rearrange("p t (g e) -> p t e g", g=NG), AX_X, ALU.add))
            pick(oh[0][:, :, :], el[:, :, :], l1)
            then(dve.scalar_tensor_tensor(out=el[:, :, :], in0=oh[0][:, :, :], scalar=-3.0e38, in1=el[:, :, :],
                                          op0=ALU.mult, op1=ALU.add))
            pick(oh[1][:, :, :], el[:, :, :], l2)
            then(dve.tensor_tensor(l1[:, :, :], l2[:, :, :], l1[:, :, :], ALU.subtract))
            dve.tensor_copy(l2[:, :, :], l1[:, :, :]).then_inc(r_shift, 1)
            for c in range(2):
                dve.tensor_tensor(e12[c][:, :, :].rearrange("p t (g e) -> p t g e", g=NG),
                                  goh[:, :, :, None].broadcast_to([P, TILES, NG, EPG]),
                                  oh[c][:, :, None, :].broadcast_to([P, TILES, NG, EPG]), ALU.mult).then_inc(r_dve, 1)
                step.n += 1
            dve.wait_ge(r_dve, step.n)
            for c in range(2):
                ms = dve.memset(e12[c][DEC:P, PT, :], 0.0)
            then(ms)
            dve.tensor_tensor(both[:, :, :], e12[0][:, :, :], e12[1][:, :, :], ALU.add).then_inc(r_both, 1)
            dve.wait_ge(r_exp, 2)
            then(dve.tensor_reduce(pg[:, :, :].rearrange("p t a -> p (t a)"), gex[:, :, :], AX_X, ALU.add))
            then(dve.tensor_scalar(l1[:, :, :], l2[:, :, :], 1.0, None, ALU.add))
            then(dve.tensor_tensor(l1[:, :, :], l1[:, :, :], pg[:, :, :], ALU.mult))
            then(dve.reciprocal(gates[:, :, 0:1], l1[:, :, :]))
            then(dve.tensor_tensor(gates[:, :, 1:2], gates[:, :, 0:1], l2[:, :, :], ALU.mult))
            dve.wait_ge(r_counts, 1)
            dve.tensor_copy(rank[:, :, :], psum[:, 6, 0:TILES * NE].rearrange("p (t e) -> p t e", e=NE))
            then(dve.tensor_copy(cnt[:, :, :], psum[:, 7, 0:TILES * NE].rearrange("p (t e) -> p t e", e=NE)))
            for t in range(TILES):
                then(dve.tensor_tensor(before[:, t + 1, :], before[:, t, :], cnt[:, t, :], ALU.add))
            then(dve.tensor_scalar(needi[:, :], before[:, TILES, :], float(P - 1), None, ALU.add))
            then(dve.tensor_scalar(needi[:, :], needi[:, :], 7, None, ALU.logical_shift_right))
            then(dve.tensor_copy(needf[:, :], needi[:, :]))
            then(dve.tensor_tensor_scan(cum[:, :], needf[:, :], needf[:, :], 0.0, ALU.add, ALU.bypass))
            then(dve.tensor_tensor(base[:, :], cum[:, :], needf[:, :], ALU.subtract))
            then(dve.tensor_scalar(base[:, :], base[:, :], float(P), None, ALU.mult))
            then(dve.tensor_tensor(sv[:, :, :], rank[:, :, :], before[:, 0:TILES, :], ALU.add))
            then(dve.tensor_tensor(sv[:, :, :], sv[:, :, :], base[:, None, :].broadcast_to([P, TILES, NE]), ALU.add))
            for c in range(2):
                then(dve.tensor_tensor(sel[:, :, :], sv[:, :, :], e12[c][:, :, :], ALU.mult))
                then(dve.tensor_reduce(slotf[:, :, c], sel[:, :, :], AX_X, ALU.add))
            then(dve.tensor_copy(slots[:, :, :], slotf[:, :, :]))
            then(dve.tensor_scalar(posi[:, :, :], slots[:, :, :], P - 1, None, ALU.bitwise_and))
            then(dve.tensor_copy(posf[:, :, :], posi[:, :, :]))
            then(dve.tensor_scalar(posi[:, :, :], slots[:, :, :], 7, None, ALU.logical_shift_right))
            then(dve.tensor_copy(stf[:, :, :], posi[:, :, :]))
            full = [P, TILES, 2]
            dve.tensor_tensor(onp, ciota[:, None, None, :].broadcast_to(full + [P]), posf[:, :, :, None].broadcast_to(full + [P]), ALU.is_equal)
            dve.tensor_copy(g_hi[:, :, :], gates[:, :, :])
            then(dve.tensor_tensor(onf, tiota[:, None, None, :].broadcast_to(full + [TC]),
                                   stf[:, :, :, None].broadcast_to(full + [TC]), ALU.is_equal))
            then(dve.tensor_tensor(g_lo[:, :, :], gates[:, :, :], g_hi[:, :, :].bitcast(F32), ALU.subtract))
            for n, v in enumerate((tokid[:, :, None, None], g_hi[:, :, :, None].bitcast(F32), g_lo[:, :, :, None])):
                last = dve.tensor_tensor(ont[:, :, :, n, :], onf, v.broadcast_to(full + [TC]), ALU.mult)
            last.then_inc(oneh_ready, 1)
            then(dve.tensor_tensor(cmp, cum[:, None, :].broadcast_to([P, TC, NE]),
                                   tiota[:, :, None].broadcast_to([P, TC, NE]), ALU.is_le))
            then(dve.tensor_reduce(texpf[:, :], cmp, AX_X, ALU.add))
            then(dve.tensor_scalar(texp[:, :], texpf[:, :], float(NE - 1), None, ALU.min))
            then(dve.tensor_copy(cumi[:, :], cum[:, :]))
            then(dve.tensor_scalar(tq[:, :], texp[:, :], 11.0, None, ALU.mult))
            then(dve.tensor_scalar(tq[:, :], tq[:, :], 5, None, ALU.logical_shift_right))
            then(dve.tensor_copy(tqf[:, :], tq[:, :]))
            then(dve.scalar_tensor_tensor(out=tqf[:, :], in0=tqf[:, :], scalar=-float(NW), in1=texp[:, :], op0=ALU.mult, op1=ALU.add))
            then(dve.memset(tpack[:, 0:1], 0.0))
            then(dve.scalar_tensor_tensor(out=tpack[:, 1:TC + 1], in0=tqf[:, :], scalar=16.0, in1=texp[:, :], op0=ALU.mult, op1=ALU.add))
            then(dve.scalar_tensor_tensor(out=tab[:, :], in0=tpack[:, 1:TC + 1], scalar=64.0, in1=tpack[:, 0:TC], op0=ALU.mult, op1=ALU.add))
            then(dve.tensor_scalar(ntile[:, :], cum[:, NE - 1:NE], 1.0, None, ALU.add))
            then(dve.tensor_scalar(ntile[:, :], ntile[:, :], 1, None, ALU.logical_shift_right))
            dve.tensor_scalar(ntile[:, :], ntile[:, :], 1, None, ALU.subtract).then_inc(tables_ready, 1)
            dve.wait_ge(oneh_used, 1)
            dve.tensor_copy(ids[:, :], psum[:, 6, 0:TC]).then_inc(ids_ready, 1)
            then(dve.tensor_copy(gslot[:, :], psum[:, 6, TC:2 * TC]))
            dve.tensor_tensor(gslot[:, :], psum[:, 6, 2 * TC:3 * TC], gslot[:, :], ALU.add).then_inc(ids_ready, 1)
            dve.wait_ge(tables_ready, 1)

            def split(e, s, turn):
                for n, (lo, hi, loaded, ready) in enumerate(((0, UP, up_loaded, up_ready), (UP, WE, down_loaded, down_ready))):
                    dve.wait_ge(loaded[s], turn * 16 + 16)
                    a, b = s * WE + lo, s * WE + hi
                    raw = we_raw[:, a:b]
                    dve.tensor_copy(we_hi[:, a:b], raw).then_inc(wh_ready, 1)
                    dve.wait_ge(wh_ready, e * 2 + (n + 1))
                    dve.tensor_tensor(we_lo[:, a:b], raw, we_hi[:, a:b].bitcast(F32), ALU.subtract).then_inc(ready, 1)

            with dve.Fori(0, NE // NW) as i:
                for s in range(NW):
                    split(i * NW + s, s, i)
            for e in range(NE // NW * NW, NE):
                split(e, e % NW, e // NW)

        @block.gpsimd
        def _(pool):
            pool.iota(tiota[:, :], [[1, TC]], base=0, channel_multiplier=0, allow_small_or_imprecise_dtypes=True).then_inc(r_const, 1)
            pool.iota(ciota[:, :], [[1, P]], base=0, channel_multiplier=0, allow_small_or_imprecise_dtypes=True).then_inc(r_const, 1)
            pool.iota(tokid[:, :], [[P, TILES]], base=0, channel_multiplier=1, allow_small_or_imprecise_dtypes=True).then_inc(r_const, 1)
            pool.iota(prio[:, :], [[-1, 4]], base=4, channel_multiplier=0, allow_small_or_imprecise_dtypes=True).then_inc(r_const, 1)
            pool.memset(before[:, 0, :], 0.0).then_inc(r_const, 1)
            pool.memset(ones[:, :], 1.0).then_inc(r_const, 1)
            pool.wait_ge(r_const, 6)
            pool.affine_select(out=tri[:, :], in_=ones[:, :], compare_op=ALU.is_gt, fill=0.0, base=0,
                               pattern=[[1, P]], channel_multiplier=-1).then_inc(r_const, 1)
            pool.wait_ge(ids_ready, 1)

            def name_tokens(t, s, turned):
                if turned is not None:
                    pool.wait_ge(x_turned, turned)
                pool.tensor_copy(idst[:, s:s + 1], ids[:, bass.ds(t, 1)]).then_inc(idst_ready, 1)

            def gather(s):
                pool.indirect_dma_start(xg[:, s, :], None, hn2_d, bass.IndirectOffsetOnAxis(idst[:, s:s + 1], 0)).then_inc(gathered[s], 16)

            def low_x(t, s, up):
                pool.wait_ge(x_copied, t + 1)
                if up is not None:
                    pool.wait_ge(up_done, up + 1)
                pool.tensor_tensor(x_lo[:, s, :, :], xf, x_hi[:, s, :, :].bitcast(F32), ALU.subtract).then_inc(x_ready, 1)

            def low_act(t, used, gathers=True):
                if gathers:
                    pool.wait_ge(idst_ready, t + 4)
                pool.wait_ge(at_copied, t + 1)
                if used is not None:
                    pool.wait_ge(down_done, used)
                pool.tensor_tensor(at_lo[:, :, :], atf[:, :, :], at_hi[:, :, :].bitcast(F32), ALU.subtract).then_inc(at_ready, 1)

            def gate_act(t, turned):
                pool.wait_ge(au_copied, t + 1)
                pool.tensor_tensor(sg[:, :], au[:, 0:DE], sg[:, :], ALU.mult).then_inc(act_mid, 1)
                if turned is not None:
                    pool.wait_ge(act_turned, turned)
                pool.wait_ge(act_mid, t + 1)
                pool.tensor_tensor(actv[:, :], sg[:, :], au[:, DE:2 * DE], ALU.mult).then_inc(act_ready, 1)

            for t in range(2):
                name_tokens(t, t, None)
            pool.wait_ge(idst_ready, 2)
            gather(0)
            gather(1)
            low_x(0, 0, None)
            low_x(1, 1, None)
            name_tokens(2, 0, 1)
            pool.wait_ge(idst_ready, 3)
            gather(0)
            gate_act(0, None)
            low_x(2, 0, 1)
            name_tokens(3, 1, 2)
            low_act(0, None)
            gather(1)
            gate_act(1, 1)
            more = pool.value_load(ntile[0:1, 0:1], min_val=SLOT_TILES_MIN // 2, max_val=SLOT_TILES // 2 - 1)
            with pool.Fori(1, more + 1) as i:
                for s in range(2):
                    t = i * 2 + s
                    low_x(t + 1, 1 - s, t)
                    name_tokens(t + 2, s, t + 1)
                    low_act(t - 1, t)
                    gather(s)
                    gate_act(t, t)
            low_act(more * 2 + 1, more * 2 + 2, False)
            pool.wait_ge(gathered[1], more * 16 + 32)

        @block.scalar
        def _(act):
            act.sem_inc(y_stored[1], 16)
            act.wait_ge(r_shift, 1)
            act.activation(gex[:, :, :], gsh[:, :, :], ACT.Exp).then_inc(r_exp, 1)
            act.wait_ge(r_shift, 2)
            act.activation(l2[:, :, :], l2[:, :, :], ACT.Exp).then_inc(r_exp, 1)

            def copy_x(t, s, up, low):
                act.wait_ge(x_turned, t + 1)
                if up is not None:
                    act.wait_ge(up_done, up + 1)
                src = psum[:, 0:2, :].rearrange("p b (k c) -> p (b k) c", c=P)
                act.activation(x_hi[:, s, :, :], src, ACT.Copy)
                if low is not None:
                    act.wait_ge(x_ready, low)
                act.activation(xf, src, ACT.Copy).then_inc(x_copied, 1)

            def copy_act(t, used, low):
                act.wait_ge(act_turned, t + 1)
                if used is not None:
                    act.wait_ge(down_done, used)
                    act.wait_ge(at_ready, low)
                src = psum[:, 3, 0:2 * P].rearrange("p (k c) -> p k c", c=P)
                act.activation(at_hi[:, :, :], src, ACT.Copy)
                act.activation(atf[:, :, :], src, ACT.Copy).then_inc(at_copied, 1)

            def swish(t, free):
                act.wait_ge(up_done, t + 2)
                if free is not None:
                    act.wait_ge(act_ready, free)
                act.activation(sg[:, :], psum[:, 2, 0:DE], ACT.Sigmoid)
                act.activation(au[:, :], psum[:, 2, :], ACT.Copy).then_inc(au_copied, 1)

            def copy_y(t, s, stored):
                gate = gslot[:, t:t + 1] if isinstance(t, int) else gslot[:, bass.ds(t, 1)]
                act.wait_ge(down_done, t + 2)
                if stored is not None:
                    act.wait_ge(y_stored[s], stored)
                act.activation(yst[:, s, :], psum[:, 4:6, :].rearrange("p b n -> p (b n)"), ACT.Copy,
                               scale=gate).then_inc(y_copied, 1)

            def store_y(t, s):
                act.wait_ge(y_copied, t + 1)
                act.dma_start(y_d[bass.ds(t * P, P), :], yst[:, s, :]).then_inc(y_stored[s], 16)

            act.wait_ge(ids_ready, 2)
            copy_x(0, 0, None, None)
            copy_x(1, 1, None, 1)
            swish(0, None)
            copy_x(2, 0, 1, 2)
            copy_act(0, None, None)
            swish(1, 1)
            copy_y(0, 0, None)
            more = act.value_load(ntile[0:1, 0:1], min_val=SLOT_TILES_MIN // 2, max_val=SLOT_TILES // 2 - 1)
            with act.Fori(1, more + 1) as i:
                for s in range(2):
                    t = i * 2 + s
                    copy_x(t + 1, 1 - s, t, t + 1)
                    store_y(t - 2, s)
                    copy_act(t - 1, t, t - 1)
                    swish(t, t)
                    copy_y(t - 1, 1 - s, i * 16)
            store_y(more * 2, 0)
            copy_act(more * 2 + 1, more * 2 + 2, more * 2 + 1)
            copy_y(more * 2 + 1, 1, more * 16 + 16)
            store_y(more * 2 + 1, 1)
            act.wait_ge(y_stored[0], more * 16 + 16)
            act.wait_ge(y_stored[1], more * 16 + 32)
            act.sem_inc(y_complete, 1)

        @block.tensor
        def _(pe):
            pe.sem_inc(down_done, 1)
            pe.sem_inc(up_done, 1)
            pe.wait_ge(r_both, 1)
            pe.wait_ge(r_const, 7)
            pe.matmul(psum[:, 6, 0:TILES * NE], tri[:, :], both[:, :, :].rearrange("p t e -> p (t e)"), start=True, stop=True)
            pe.matmul(psum[:, 7, 0:TILES * NE], ones[:, :], both[:, :, :].rearrange("p t e -> p (t e)"), start=True, stop=True).then_inc(r_counts, 1)
            for t in range(TILES):
                r = rows(t)
                pe.wait_ge(oneh_ready, 1)
                for c in range(2):
                    mm = pe.matmul(psum[:, 6, 0:3 * TC], onp[0:r, t, c, :], ont[0:r, t, c, :, :].rearrange("p n t -> p (n t)"), start=(t == 0 and c == 0),
                                   stop=(t == PT and c == 1))
            mm.then_inc(oneh_used, 1)
            pe.wait_ge(tables_ready, 1)

            def turn_x(t, s, count, copied):
                pe.wait_ge(gathered[s], count)
                if copied is not None:
                    pe.wait_ge(x_copied, copied)
                for k in range(KC):
                    mm = pe.transpose(psum[:, k // 4, (k % 4) * P:(k % 4 + 1) * P], xg[:, s, k * P:(k + 1) * P], ident[:, :])
                mm.then_inc(x_turned, 1)

            def turn_act(t, copied):
                pe.wait_ge(act_ready, t + 1)
                if copied is not None:
                    pe.wait_ge(at_copied, copied)
                for k in range(2):
                    mm = pe.transpose(psum[:, 3, k * P:(k + 1) * P], actv[:, k * P:(k + 1) * P], ident[:, :])
                mm.then_inc(act_turned, 1)

            def places(t):
                both = pe.value_load(tab[0:1, bass.ds(t, 1)], min_val=0, max_val=4095)
                return [(v & 15, nc.s_assert_within(pe.snap(((v >> 4) & 3) * WE), 0, (NW - 1) * WE,
                                                    skip_runtime_bounds_check_because=MADE_SO)) for v in (both & 63, both >> 6)]

            def up(t, s, place, copied):
                e, at = place
                pe.wait_ge(x_ready, t + 1)
                pe.wait_ge(up_ready, e + 1)
                if copied is not None:
                    pe.wait_ge(au_copied, copied)
                for k in range(KC):
                    for x, w in ((x_hi, we_hi), (x_hi, we_lo), (x_lo, we_hi)):
                        mm = pe.matmul(psum[:, 2, :], x[:, s, k, :], w[:, bass.ds(at + k * 2 * DE, 2 * DE)],
                                       start=(k == 0 and x is x_hi and w is we_hi), stop=(k == KC - 1 and x is x_lo))
                mm.then_inc(up_done, 1)

            def down(t, place, copied):
                e, at = place
                pe.wait_ge(at_ready, t + 1)
                pe.wait_ge(down_ready, e + 1)
                if copied is not None:
                    pe.wait_ge(y_copied, copied)
                for k in range(2):
                    for x, w in ((at_hi, we_hi), (at_hi, we_lo), (at_lo, we_hi)):
                        for half in range(2):
                            mm = pe.matmul(psum[:, 4 + half, :], x[:, k, :], w[:, bass.ds(at + (UP + k * D + half * 512), 512)],
                                           start=(k == 0 and x is at_hi and w is we_hi), stop=(k == 1 and x is at_lo))
                mm.then_inc(down_done, 1)

            turn_x(0, 0, 16, None)
            turn_x(1, 1, 16, 1)
            first, second = places(1)
            up(0, 0, first, None)
            turn_x(2, 0, 32, 2)
            turn_act(0, None)
            up(1, 1, second, 1)
            down(0, first, None)
            more = pe.value_load(ntile[0:1, 0:1], min_val=SLOT_TILES_MIN // 2, max_val=SLOT_TILES // 2 - 1)
            with pe.Fori(1, more + 1) as i:
                for s in range(2):
                    t = i * 2 + s
                    turn_x(t + 1, 1 - s, i * 16 + 16 * (s + 1), t + 1)
                    turn_act(t - 1, t - 1)
                    before, this = places(t)
                    up(t, s, this, t)
                    down(t - 1, before, t - 1)
            turn_act(more * 2 + 1, more * 2 + 1)
            down(more * 2 + 1, places(more * 2 + 2)[0], more * 2 + 1)


def block_d(nc, mhalf, mod_d, x1_d, y_d, slots, gates, ln2_g, ln2_b, y_prompt, y_sample):
    with ExitStack() as ctx:
        def sb(name, shape, dt=F32):
            return ctx.enter_context(nc.sbuf_tensor(name, shape, dt))

        def sem(name):
            return ctx.enter_context(nc.semaphore(name))

        NB = 4
        y = sb("y", [P, NB, D])
        x1 = sb("x1", [P, NB, D])
        g2 = sb("g2", [P, 2, D])
        l2g, l2b = sb("l2g", [P, D]), sb("l2b", [P, D])
        st = sb("st2", [P, 2, 6])
        mv = sb("mv2", [P, TILES, 2])
        ve = sb("ve2", [P, TILES])
        rs = sb("rs2", [P, TILES])
        shift = sb("shift2", [P, TILES])
        gate_row = [sem("gate_row_prompt"), sem("gate_row_sample")]
        d_rows = sem("d_rows")
        y_in = [sem(f"y_in{n}") for n in range(NB)]
        x1_moved = [sem(f"x1_moved{n}") for n in range(NB)]
        scaled, d_sum, d_var, d_rstd, d_shift, normed, gained, finished, d_dve = map(
            sem, ("scaled", "d_sum", "d_var", "d_rstd", "d_shift", "normed", "gained", "finished", "d_dve"))
        block = ctx.enter_context(nc.Block())

        @block.sync
        def _(sp):
            def load(j):
                s = j % NB
                if j >= NB:
                    sp.wait_ge(x1_moved[s], 32 * (j // NB))
                sp.dma_start(x1[0:rows(j), s, :], x1_d[j * P:j * P + rows(j), :]).then_inc(x1_moved[s], 16)

            load(0)
            sp.dma_start(g2[:, 0, :], mod_d[0, 5 * D:6 * D].partition_broadcast(P)).then_inc(gate_row[0], 16)
            sp.wait_ge(y_in[0], 32)
            load(1)
            sp.dma_start(l2g[:, :], ln2_g[0].partition_broadcast(P)).then_inc(d_rows, 16)
            sp.dma_start(l2b[:, :], ln2_b[0].partition_broadcast(P)).then_inc(d_rows, 16)
            sp.wait_ge(y_in[1], 32)
            load(2)
            sp.dma_start(g2[:, 1, :], mod_d[1, 5 * D:6 * D].partition_broadcast(P)).then_inc(gate_row[1], 16)
            load(3)
            for j in range(TILES):
                s = j % NB
                dst = y_prompt[0, j * P:(j + 1) * P, :] if j < PT else y_sample[0]
                sp.wait_ge(finished, j + 1)
                sp.dma_start(dst, x1[0:rows(j), s, :]).then_inc(x1_moved[s], 16)
                if j >= 1 and j - 1 + NB < TILES:
                    load(j - 1 + NB)
            for s in range(NB):
                sp.wait_ge(x1_moved[s], 32 * len(range(s, TILES, NB)))

        @block.gpsimd
        def _(pool):
            def first(j):
                r, s = rows(j), j % NB
                if j >= NB:
                    pool.wait_ge(d_sum, j - NB + 1)
                pool.indirect_dma_start(y[0:r, s, :], None, y_d,
                                        bass.IndirectOffsetOnAxis(slots[0:r, j, 0:1], 0)).then_inc(y_in[s], 16)

            def second(j):
                r, s = rows(j), j % NB
                pool.wait_ge(y_in[s], 32 * (j // NB) + 16)
                pool.indirect_dma_start(y[0:r, s, :], None, y_d, bass.IndirectOffsetOnAxis(slots[0:r, j, 1:2], 0),
                                        compute_op=ALU.add).then_inc(y_in[s], 16)

            first(0)
            for j in range(1, NB):
                first(j)
                second(j - 1)
            for j in range(TILES + 1):
                if j < TILES:
                    r = rows(j)
                    pool.wait_ge(d_var, j + 1)
                    pool.tensor_tensor(rs[0:r, j:j + 1], ve[0:r, j:j + 1], mhalf[0:r, 0:1], ALU.pow).then_inc(d_rstd, 1)
                if j + NB < TILES:
                    first(j + NB)
                if j + NB - 1 < TILES:
                    second(j + NB - 1)
                if j >= 1:
                    r, s = rows(j - 1), (j - 1) % NB
                    if j == 1:
                        pool.wait_ge(d_rows, 32)
                    pool.wait_ge(gained, j)
                    pool.tensor_tensor(x1[0:r, s, :], x1[0:r, s, :], l2b[0:r, :], ALU.add).then_inc(finished, 1)

        @block.scalar
        def _(act):
            for j in range(TILES):
                r, s = rows(j), j % NB
                act.wait_ge(d_shift, j + 1)
                act.activation(x1[0:r, s, :], x1[0:r, s, :], ACT.Identity, bias=shift[0:r, j:j + 1],
                               scale=rs[0:r, j:j + 1]).then_inc(normed, 1)

        @block.vector
        def _(dve):
            step = Tally(d_dve)

            def then(ins):
                step.inc(ins)
                dve.wait_ge(d_dve, step.n)

            def scale(j):
                r, s = rows(j), j % NB
                dve.wait_ge(y_in[s], 32 * (j // NB) + 32)
                if j in (0, PT):
                    dve.wait_ge(gate_row[j // PT], 16)
                dve.tensor_tensor(y[0:r, s, :], y[0:r, s, :], g2[0:r, j // PT, :], ALU.mult).then_inc(scaled, 1)

            def residual(j):
                r, s = rows(j), j % NB
                dve.wait_ge(scaled, j + 1)
                dve.wait_ge(x1_moved[s], 32 * (j // NB) + 16)
                dve.scalar_tensor_tensor(out=x1[0:r, s, :], in0=x1[0:r, s, :], scalar=ALPHA, in1=y[0:r, s, :],
                                         op0=ALU.mult, op1=ALU.add).then_inc(d_sum, 1)
                dve.wait_ge(d_sum, j + 1)
                for half in range(2):
                    b = dve.bn_stats(st[0:r, half, :], x1[0:r, s, half * 512:(half + 1) * 512])
                then(b)
                then(dve.bn_aggr(mv[0:r, j, :], st[0:r, :, :].rearrange("p b n -> p (b n)")))
                dve.tensor_scalar(ve[0:r, j:j + 1], mv[0:r, j, 1:2], EPS, None, ALU.add).then_inc(d_var, 1)

            def turn_mean(j):
                r = rows(j)
                dve.wait_ge(d_rstd, j + 1)
                dve.scalar_tensor_tensor(out=shift[0:r, j:j + 1], in0=mv[0:r, j, 0:1], scalar=-1.0, in1=rs[0:r, j:j + 1],
                                         op0=ALU.mult, op1=ALU.mult).then_inc(d_shift, 1)

            def gain(j):
                r, s = rows(j), j % NB
                dve.wait_ge(normed, j + 1)
                dve.tensor_tensor(x1[0:r, s, :], x1[0:r, s, :], l2g[0:r, :], ALU.mult).then_inc(gained, 1)

            for j in range(TILES + 1):
                if j < TILES:
                    scale(j)
                if j >= 1:
                    turn_mean(j - 1)
                if j < TILES:
                    residual(j)
                if j == 1:
                    dve.wait_ge(d_rows, 32)
                if j >= 1:
                    gain(j - 1)


_INS = ["x_prompt", "x_sample", "c_prompt", "c_sample", "cache_k", "cache_v", "state_pool",
        "w_mod", "b_mod", "w_in", "w_pool", "pool_scale", "w_out", "ln1_g", "ln1_b", "ln2_g", "ln2_b",
        "w_group", "b_group", "w_router", "b_router", "w_up", "w_down"]
_OUTS = [(1, SEQ, D), (1, DEC, D), (1, 1, SEQ, HEADS, DH), (1, 1, SEQ, HEADS, DH), (1, 1, HIST, 512),
         (1, 1, DEC, HEADS, DH), (1, 1, DEC, HEADS, DH), (1, 1, HIST, 512)]


def kernel(**inputs):
    import numpy as _np
    import concourse.bacc as _bacc
    from concourse.bass_utils import run_bass_kernel_spmd as _run

    nc = _bacc.Bacc("TRN2", target_bir_lowering=False, num_devices=1)
    arrays, args = {}, []
    for name in _INS:
        a = _np.ascontiguousarray(inputs[name])
        arrays[f"in_{name}_dram"] = a
        args.append(nc.dram_tensor(f"in_{name}_dram", a.shape, mybir.dt.from_np(a.dtype), kind="ExternalInput").ap())
    for i, shape in enumerate(_OUTS):
        args.append(nc.dram_tensor(f"out_{i}_dram", shape, F32, kind="ExternalOutput").ap())
    build(nc, *args)
    r = _run(nc, [arrays], core_ids=[0])
    return tuple(r.results[0][f"out_{i}_dram"] for i in range(len(_OUTS)))
```

```python
from contextlib import ExitStack, contextmanager

import concourse.bass as bass
from concourse import mybir

ALU = mybir.AluOpType
ACT = mybir.ActivationFunctionType
AX_X = mybir.AxisListType.X
F32 = mybir.dt.float32
F32R = mybir.dt.float32r
BF16 = mybir.dt.bfloat16
I32 = mybir.dt.int32

P = 128
D = 1024
KC = D // P
SEQ, DEC = 1024, 64
NT = SEQ + DEC
PT = SEQ // P
TILES = PT + 1
PAST = 512
HEADS, DH = 8, 64
PAIRS = HEADS // 2
NMOD = 6 * D
SECS = 3
WIN = (2, 4, 8, 16)
HIST = 15
EPS = 1e-5
ALPHA = 2.0 ** 0.25
FC = 16
CH = [(0, 364), (364, 364), (728, 360)]
GROUPS = [(0, 4), (4, 8), (8, 9)]
NG, EPG, NE = 4, 4, 16
DE = 256
SLOT_TILES = (2 * NT - NE) // P + NE
SLOT_TILES_MIN = -(-2 * NT // P)
NSLOT = SLOT_TILES * P
NLOG = NG + NE
MASKED = -1.0e30


def rows(i):
    return P if i < PT else DEC


def one_room(nc, ctx, shape, *tensors):
    out = []
    for n, (name, dt) in enumerate(tensors):
        guard = nc.sbuf_tensor(name, shape, dt)
        if n < len(tensors) - 1:
            out.append(guard.__enter__())
            guard.__exit__(None, None, None)
        else:
            out.append(ctx.enter_context(guard))
    return out


class Tally:

    def __init__(self, sem):
        self.sem, self.n, self.turns = sem, 0, 0

    def inc(self, ins, by=1):
        ins.then_inc(self.sem, by)
        self.n += by
        return ins

    @property
    def now(self):
        return self.turns + self.n if not isinstance(self.turns, int) or self.turns else self.n


@contextmanager
def turns(eng, count, per):
    before = {t: t.n for t in per}
    with eng.Fori(0, count) as i:
        for t, by in per.items():
            t.turns = i * by
        yield i
    for t, by in per.items():
        assert t.n - before[t] == by, (t.sem, t.n - before[t], by)
        t.turns = 0
        t.n = before[t] + by * count


def build(nc, x_prompt, x_sample, c_prompt, c_sample, cache_k, cache_v, state_pool,
          w_mod, b_mod, w_in, w_pool, pool_scale, w_out, ln1_g, ln1_b, ln2_g, ln2_b,
          w_group, b_group, w_router, b_router, w_up, w_down,
          y_prompt, y_sample, k_prompt, v_prompt, pool_prompt, k_sample, v_sample, pool_sample):
    def dram(name, shape, dt=F32):
        return nc.dram_tensor(name, shape, dt, kind="Internal").ap()

    mod_d = dram("mod_d", [2, NMOD])
    x1_d = dram("x1_d", [NT, D])
    hn2_d = dram("hn2_d", [NT, D])
    y_d = dram("y_d", [NSLOT, D])

    with ExitStack() as outer:
        def osb(name, shape, dt=F32):
            return outer.enter_context(nc.sbuf_tensor(name, shape, dt))

        ident = osb("ident", [P, P])
        psum = outer.enter_context(nc.psum_tensor("psum", [P, 8, 512], F32))
        logits = osb("logits", [P, TILES, NLOG])
        mhalf = osb("mhalf", [P, 16])
        slots = osb("slots", [P, TILES, 2], I32)
        gates = osb("gates", [P, TILES, 2])
        with ExitStack() as mid:
            proj = mid.enter_context(nc.sbuf_tensor("proj", [P, FC, NT], F32))
            utail = mid.enter_context(nc.sbuf_tensor("utail", [P, 4, 2, HIST], F32))
            block_a(nc, ident, mhalf, psum, proj, utail, mod_d, x_prompt, x_sample, c_prompt,
                    c_sample, w_mod, b_mod, w_in, state_pool)
            block_b(nc, ident, mhalf, psum, proj, utail, logits, mod_d, x1_d, hn2_d, x_prompt,
                    x_sample, y_d, cache_k, cache_v, w_pool, pool_scale, w_out, ln1_g, ln1_b,
                    w_group, b_group, w_router, b_router, k_prompt, v_prompt, pool_prompt,
                    k_sample, v_sample, pool_sample)
        block_c(nc, ident, psum, logits, hn2_d, y_d, slots, gates, w_up, w_down)
        block_d(nc, mhalf, mod_d, x1_d, y_d, slots, gates, ln2_g, ln2_b, y_prompt, y_sample)


def block_a(nc, ident, mhalf, psum, proj, utail, mod_d, x_prompt, x_sample, c_prompt, c_sample,
            w_mod, b_mod, w_in, state_pool):
    with ExitStack() as ctx:
        def sb(name, shape, dt=F32):
            return ctx.enter_context(nc.sbuf_tensor(name, shape, dt))

        def sem(name):
            return ctx.enter_context(nc.semaphore(name))

        wm0a, hn_hi = one_room(nc, ctx, [P, KC, NT], ("wm0a", F32), ("hn_hi", F32R))
        wm0b, hn_lo = one_room(nc, ctx, [P, KC, NT], ("wm0b", F32), ("hn_lo", F32R))
        wm = sb("wm", [P, 2, 2048])
        w_raw = sb("w_raw", [P, 2, KC, P])
        w_hi = sb("w_hi", [P, 2, KC, P], F32R)
        w_lo = sb("w_lo", [P, 2, KC, P], F32R)
        stage = sb("stage", [P, 2, D])
        modf = sb("modf", [P, 4, 4, 2])
        crow = sb("crow", [16, P])
        cT = sb("cT", [P, KC, 32])
        modb = sb("modb", [P, SECS, 512])
        modrow = sb("modrow", [P, SECS, 512])
        hist = sb("hist", [HIST, 512])
        ext = sb("ext", [P, 4, HIST + DEC])
        exs = sb("exs", [P, 2, HIST + DEC])
        rcnt = sb("rcnt", [P, HIST])
        stats = sb("stats", [P, TILES, 2, 6])
        mv = sb("mv", [P, TILES, 2])
        vpe = sb("vpe", [P, TILES])
        rstd = sb("rstd", [P, TILES])
        arena = proj[:, :, :].rearrange("p a b -> p (a b)")
        xp = arena[:, 0:PT * D].rearrange("p (t d) -> p t d", d=D)
        xT = arena[:, PT * D:PT * D + KC * NT].rearrange("p (k c) -> p k c", c=NT)
        wm0 = [r[:, :, :].rearrange("p k c -> p (k c)")[:, 0:KC // 2 * 2048].rearrange("p (k n) -> p k n", n=2048)
               for r in (wm0a, wm0b)]

        c_loaded, modb_loaded = map(sem, ("c_loaded", "modb_loaded"))
        x_loaded = [sem("x_loaded_prompt0"), sem("x_loaded_prompt1"), sem("x_loaded_sample")]
        wm0_loaded = [sem(f"wm0_loaded{n}") for n in range(KC // 2)]
        wm_loaded = [sem("wm_loaded0"), sem("wm_loaded1")]
        w_loaded = [sem("w_loaded0"), sem("w_loaded1")]
        ident0, ident_ready, const_ready = map(sem, ("ident0", "ident_ready", "const_ready"))
        cT_done, cT_ready, hist_ready = map(sem, ("cT_done", "cT_ready", "hist_ready"))
        modb_ready, modb_one = map(sem, ("modb_ready", "modb_one"))
        wm_used, mod_copied, mod_ready, mod_stored = map(sem, ("wm_used", "mod_copied", "mod_ready", "mod_stored"))
        mod_sum0 = sem("mod_sum0")
        modf_done, hn_ready = map(sem, ("modf_done", "hn_ready"))
        vpe_ready, rstd_ready, a_dve = map(sem, ("vpe_ready", "rstd_ready", "a_dve"))
        xn_ready, xT_done, xT_copied, hi_ready, lo_ready = map(sem, ("xn_ready", "xT_done", "xT_copied", "hi_ready", "lo_ready"))
        w_split, w_hi_ready, proj_done, proj_copied = map(sem, ("w_split", "w_hi_ready", "proj_done", "proj_copied"))
        pool_step = sem("pool_step")

        block = ctx.enter_context(nc.Block())

        @block.sync
        def _(sp):
            sp.dma_start(crow[0:KC, :], c_prompt.rearrange("o (k p) -> (o k) p", p=P)).then_inc(c_loaded, 16)
            sp.dma_start(crow[KC:2 * KC, :], c_sample.rearrange("o (k p) -> (o k) p", p=P)).then_inc(c_loaded, 16)
            sp.dma_start(hist[:, :], state_pool[0, 0]).then_inc(c_loaded, 16)
            for g in range(2):
                src = x_prompt[0, g * 4 * P:(g + 1) * 4 * P, :].rearrange("(t p) d -> p t d", p=P)
                sp.dma_start(xp[:, 4 * g:4 * g + 4, :], src).then_inc(x_loaded[g], 16)
            sp.dma_start(stage[0:DEC, 0, :], x_sample[0]).then_inc(x_loaded[2], 16)

            def load_w(m, slot):
                src = w_in[0, :, bass.ds(m * P, P)].rearrange("(k p) c -> p k c", p=P)
                sp.dma_start(w_raw[:, slot, :, :], src).then_inc(w_loaded[slot], 16)

            for n in range(KC // 2):
                src = w_mod[0, n * 2 * P:(n + 1) * 2 * P, 0:2048].rearrange("(k p) n -> p k n", p=P)
                sp.dma_start(wm0[n // 2][:, n % 2 * 2:n % 2 * 2 + 2, :], src).then_inc(wm0_loaded[n], 16)
                if n == 0:
                    sp.wait_ge(modb_ready, 1)
                    for b in range(2):
                        sp.dma_start(modb[b:P:32, :, :], b_mod[0].rearrange("(s j n) -> j s n", j=4, n=512)).then_inc(modb_loaded, 16)
            load_w(0, 0)
            load_w(1, 1)
            for m in range(FC):
                if m >= 2:
                    sp.wait_ge(w_split, m - 1)
                    load_w(m, m % 2)
                    sp.wait_ge(wm_used, KC + m - 1)
                sec, k = 1 + m // KC, m % KC
                sp.dma_start(wm[:, m % 2, :], w_mod[0, k * P:(k + 1) * P, sec * 2048:(sec + 1) * 2048]).then_inc(wm_loaded[m % 2], 16)
            sp.wait_ge(mod_stored, 32 * (SECS - 1))

        @block.gpsimd
        def _(pool):
            step = Tally(pool_step)

            def then(ins):
                step.inc(ins)
                pool.wait_ge(pool_step, step.n)

            pool.memset(ident[:, :], 0.0).then_inc(ident0, 1)
            pool.wait_ge(ident0, 1)
            pool.affine_select(out=ident[:, :], in_=ident[:, :], compare_op=ALU.not_equal, fill=1.0, base=0,
                               pattern=[[-1, P]], channel_multiplier=1).then_inc(ident_ready, 1)
            pool.memset(modb[:, :, :], 0.0).then_inc(modb_ready, 1)
            pool.memset(cT[:, :, :], 0.0).then_inc(const_ready, 1)
            pool.memset(mv[:, :, :], 0.0).then_inc(const_ready, 1)
            pool.memset(mhalf[:, :], -0.5).then_inc(const_ready, 1)
            for n in range(HIST):
                pool.memset(rcnt[:, n:n + 1], 1.0 / (n + 1)).then_inc(const_ready, 1)
            pool.wait_ge(const_ready, 3)
            for g, (lo, hi) in enumerate(GROUPS):
                pool.wait_ge(vpe_ready, g + 1)
                pool.tensor_tensor(rstd[:, lo:hi], vpe[:, lo:hi], mhalf[:, lo:hi], ALU.pow).then_inc(rstd_ready, 1)

            def store_mod(sec):
                for b in range(2):
                    pool.dma_start(mod_d[b, sec * 2048:(sec + 1) * 2048].rearrange("(j n) -> j n", j=4),
                                   modrow[b:P:32, sec, :]).then_inc(mod_stored, 16)

            pool.wait_ge(proj_copied, 2 + 4)
            pool.wait_ge(hist_ready, 1)
            for g in range(4):
                u = proj[:, g, :]
                pool.tensor_copy(utail[:, g, 0, :], u[:, SEQ - HIST:SEQ])
                then(pool.tensor_copy(utail[:, g, 1, :], u[:, NT - HIST:NT]))
                src = u[:, 0:SEQ]
                for level in range(g + 1):
                    w = 1 << level
                    dst = stage[:, level % 2, :]
                    pool.tensor_copy(dst[:, 0:w], src[:, 0:w])
                    then(pool.tensor_tensor(dst[:, w:SEQ], src[:, w:SEQ], src[:, 0:SEQ - w], ALU.add))
                    src = dst
                w = WIN[g]
                if w > 2:
                    pool.tensor_tensor(src[:, 0:w - 1], src[:, 0:w - 1], rcnt[:, 0:w - 1], ALU.mult)
                    then(pool.tensor_scalar(src[:, w - 1:SEQ], src[:, w - 1:SEQ], 1.0 / w, None, ALU.mult))
                else:
                    then(pool.tensor_scalar(src[:, 1:SEQ], src[:, 1:SEQ], 0.5, None, ALU.mult))
                then(pool.tensor_tensor(u[:, 0:SEQ], src[:, :], u[:, 0:SEQ], ALU.subtract))
                then(pool.tensor_copy(ext[:, g, HIST:HIST + DEC], u[:, SEQ:NT]))
                src, n = ext[:, g, :], HIST + DEC
                for level in range(g + 1):
                    w = 1 << level
                    n -= w
                    dst = exs[:, level % 2, 0:n]
                    then(pool.tensor_tensor(dst, src[:, w:w + n], src[:, 0:n], ALU.add))
                    src = dst
                then(pool.tensor_scalar(src[:, n - DEC:n], src[:, n - DEC:n], 1.0 / WIN[g], None, ALU.mult))
                then(pool.tensor_tensor(u[:, SEQ:NT], src[:, n - DEC:n], u[:, SEQ:NT], ALU.subtract))
            pool.wait_ge(modb_one, 3)
            for sec in range(1, SECS):
                pool.wait_ge(mod_copied, sec + 1)
                pool.tensor_tensor(modrow[:, sec, :], modrow[:, sec, :], modb[:, sec, :], ALU.add).then_inc(mod_ready, 1)
                pool.wait_ge(mod_ready, sec)
                store_mod(sec)

        @block.tensor
        def _(pe):
            psM = psum[:, 7, :]
            pe.wait_ge(ident_ready, 1)
            pe.wait_ge(c_loaded, 48)
            pe.transpose(psum[:, 6, 0:16], crow[:, :], ident[0:16, 0:16])
            for g in range(4):
                last = pe.transpose(psum[:, 6, 16 + 16 * g:16 + 16 * g + HIST], hist[:, g * P:(g + 1) * P], ident[0:HIST, 0:HIST])
            last.then_inc(cT_done, 1)
            pe.wait_ge(cT_ready, 1)

            def mod_chunk(k, w):
                for j in range(4):
                    mm = pe.matmul(psM[32 * j:32 * j + 32, :], cT[:, k, :], w[:, 512 * j:512 * j + 512],
                                   start=(k == 0), stop=(k == KC - 1), tile_position=(0, 32 * j))
                mm.then_inc(wm_used, 1)

            def turn(t):
                r, slot = rows(t), t % 2
                pe.wait_ge(xn_ready, t + 1)
                if t >= 2:
                    pe.wait_ge(xT_copied, t - 1)
                src = xp[:, t, :] if t < PT else stage[:, 0, :]
                for k in range(KC):
                    mm = pe.transpose(psum[:, 2 * slot + k // 4, (k % 4) * P:(k % 4) * P + r],
                                      src[0:r, k * P:(k + 1) * P], ident[0:r, 0:r])
                mm.then_inc(xT_done, 1)

            for n, tiles in enumerate(((0, 1, 2, 3), (4, 5), (6, 7), (8,))):
                for t in tiles:
                    turn(t)
                pe.wait_ge(wm0_loaded[n], 16)
                for k in (2 * n, 2 * n + 1):
                    mod_chunk(k, wm0[n // 2][:, k % 4, :])
            pe.wait_ge(mod_sum0, 1)
            pe.wait_ge(hist_ready, 1)
            for c in range(4):
                mm = pe.transpose(psum[:, 6, c * P:(c + 1) * P], modrow[:, 0, c * P:(c + 1) * P], ident[:, :])
            mm.then_inc(modf_done, 1)
            with pe.Fori(0, 2) as h:
                for mm_ in range(8):
                    slot = mm_ % 2
                    pe.wait_ge(w_split, h * 8 + mm_ + 1)
                    pe.wait_ge(proj_copied, h * 8 + mm_ + 1)
                    for k in range(KC):
                        if mm_ == 0:
                            pe.wait_ge(lo_ready, k + 1)
                        for w, parts in ((w_hi, (hn_hi, hn_lo)), (w_lo, (hn_hi,))):
                            for hn in parts:
                                for c, (t0, n) in enumerate(CH):
                                    last = pe.matmul(psum[:, 3 * slot + c, 0:n], w[:, slot, k, :], hn[:, k, t0:t0 + n],
                                                     start=(k == 0 and w is w_hi and hn is hn_hi),
                                                     stop=(k == KC - 1 and w is w_lo))
                        if k == KC // 2:
                            if mm_ == 0:
                                pe.wait_ge(mod_copied, h + 1)
                            pe.wait_ge(wm_loaded[mm_ % 2], h * 64 + 16 * (mm_ // 2 + 1))
                            mod_chunk(mm_, wm[:, mm_ % 2, :])
                    last.then_inc(proj_done, 1)

        @block.scalar
        def _(act):
            act.sem_inc(proj_copied, 2)
            act.sem_inc(mod_copied, 1)

            for t in range(TILES):
                r, slot = rows(t), t % 2
                act.wait_ge(xT_done, t + 1)
                src = psum[:, 2 * slot:2 * slot + 2, :].rearrange("p b (k c) -> p (b k) c", c=P)[:, :, 0:r]
                act.activation(xT[:, :, t * P:t * P + r], src, ACT.Copy).then_inc(xT_copied, 1)
            for k in range(KC):
                act.wait_ge(hn_ready, k + 1)
                act.activation(hn_hi[:, k, :], xT[:, k, :], ACT.Copy).then_inc(hi_ready, 1)
            with act.Fori(0, 2) as h:
                for mm in range(8):
                    slot = mm % 2
                    if mm == 7:
                        act.wait_ge(wm_used, h * 8 + 2 * KC)
                        act.activation(modrow[:, bass.ds(h + 1, 1), :].rearrange("p a n -> p (a n)"), psum[:, 7, :], ACT.Copy).then_inc(mod_copied, 1)
                    act.wait_ge(proj_done, h * 8 + mm + 1)
                    for c, (t0, n) in enumerate(CH):
                        cp = act.activation(proj[:, bass.ds(h * 8 + mm, 1), t0:t0 + n].rearrange("p a n -> p (a n)"),
                                            psum[:, 3 * slot + c, 0:n], ACT.Copy)
                    cp.then_inc(proj_copied, 1)

        @block.vector
        def _(dve):
            step = Tally(a_dve)

            def then(ins):
                step.inc(ins)
                dve.wait_ge(a_dve, step.now)

            dve.wait_ge(cT_done, 1)
            dve.wait_ge(const_ready, 3)
            for b in range(2):
                cp = dve.tensor_copy(cT[:, :, b], psum[:, 6, b * KC:(b + 1) * KC])
            cp.then_inc(cT_ready, 1)
            dve.tensor_copy(ext[:, :, 0:HIST], psum[:, 6, 16:80].rearrange("p (g c) -> p g c", c=16)[:, :, 0:HIST]).then_inc(hist_ready, 1)
            def split(m, slot, loaded, free):
                dve.wait_ge(w_loaded[slot], loaded)
                if free is not None:
                    dve.wait_ge(proj_done, free)
                dve.tensor_copy(w_hi[:, slot, :, :], w_raw[:, slot, :, :]).then_inc(w_hi_ready, 1)
                dve.wait_ge(w_hi_ready, m + 1)
                dve.tensor_tensor(w_lo[:, slot, :, :], w_raw[:, slot, :, :], w_hi[:, slot, :, :].bitcast(F32),
                                  ALU.subtract).then_inc(w_split, 1)

            for g, (lo, hi) in enumerate(GROUPS):
                dve.wait_ge(x_loaded[g], 16)
                tiles = [(t, rows(t), xp[:, t, :] if t < PT else stage[:, 0, :]) for t in range(lo, hi)]
                for t, r, x in tiles:
                    for half in range(2):
                        st = dve.bn_stats(stats[0:r, t, half, :], x[0:r, half * 512:(half + 1) * 512])
                then(st)
                for t, r, x in tiles:
                    ag = dve.bn_aggr(mv[0:r, t, :], stats[0:r, t, :, :].rearrange("p b n -> p (b n)"))
                then(ag)
                dve.tensor_scalar(vpe[:, lo:hi], mv[:, lo:hi, 1], EPS, None, ALU.add).then_inc(vpe_ready, 1)
                dve.wait_ge(rstd_ready, g + 1)
                for t, r, x in tiles:
                    dve.tensor_scalar(x[0:r, :], x[0:r, :], mv[0:r, t, 0:1], rstd[0:r, t:t + 1], ALU.subtract, ALU.mult).then_inc(xn_ready, 1)
            dve.wait_ge(modb_loaded, 32)
            for lo, hi, sec in ((64, P, 0), (0, 64, 1), (0, P, 2)):
                dve.tensor_scalar(modb[lo:hi, sec, :], modb[lo:hi, sec, :], 1.0, None, ALU.add).then_inc(modb_one, 1)
            dve.wait_ge(modb_one, 3)
            dve.wait_ge(wm_used, KC)
            dve.tensor_tensor(modrow[:, 0, :], psum[:, 7, :], modb[:, 0, :], ALU.add).then_inc(mod_sum0, 1)
            split(0, 0, 16, None)
            dve.wait_ge(modf_done, 1)
            then(dve.tensor_copy(modf[:, :, :, :], psum[:, 6, :].rearrange("p (c j n) -> p c j n", c=4, j=4)[:, :, :, 0:2]))
            dve.wait_ge(xT_copied, TILES)

            def low(k):
                dve.wait_ge(hi_ready, k + 1)
                dve.tensor_tensor(hn_lo[:, k, :], xT[:, k, :], hn_hi[:, k, :].bitcast(F32), ALU.subtract).then_inc(lo_ready, 1)

            for k in range(KC):
                c, j = k % 4, k // 4
                for b, (t0, t1) in enumerate(((0, SEQ), (SEQ, NT))):
                    ins = dve.tensor_scalar(xT[:, k, t0:t1], xT[:, k, t0:t1], modf[:, c, 2 + j, b:b + 1], modf[:, c, j, b:b + 1],
                                            ALU.mult, ALU.add)
                ins.then_inc(hn_ready, 1)
                if k:
                    low(k - 1)
            low(KC - 1)
            split(1, 1, 16, None)

            with dve.Fori(0, 7) as i:
                for s in range(2):
                    split(i * 2 + 2 + s, s, i * 16 + 32, i * 2 + 1 + s)


def attention_units():
    units = []
    for order, i in enumerate((PT,) + tuple(range(PT))):
        for p in range(PAIRS):
            q = order * PAIRS + p
            if i < PT:
                n_all = (i + 1) * P
                starts = list(range(0, n_all, 512))[::-1]
                for s0 in starts:
                    n = min(512, n_all - s0)
                    units.append((i, p, 1024 - n_all + s0, n, False, s0, s0 == starts[0], s0 == 0, q))
            else:
                units.append((i, p, 1024 - DEC, DEC, False, SEQ, True, False, q))
                units.append((i, p, 1024 - DEC - PAST, PAST, True, 0, False, True, q))
    return units


LATE = PT - 1


UNITS = len(attention_units())
MIX_AT = (15, 18, 24, 30, 36, 42, 50)
LAST_NORM = 4


def steps_beside():
    at = {}
    for j, h in enumerate(MIX_AT):
        n = MIX_AT[j + 1] if j + 1 < LATE else h + LAST_NORM
        for u, step in ((h - 1, "P"), (n, "S"), (h, "M0"), (n + 1, "N"), (h + 1, "M1"), (n + 3, "T0"), (n + 4, "T1"), (n + 5, "R")):
            at.setdefault(u, []).append((step, j))
    order = {"S": 0, "N": 1, "M0": 2, "M1": 3, "P": 4, "T0": 5, "T1": 6, "R": 7}
    for u in at:
        at[u].sort(key=lambda x: order[x[0]])
    over = [x for u in sorted(at) if u > UNITS for x in at.pop(u)]
    norms, turns_, router = [[x for x in over if x[0] in kind] for kind in (("S", "N"), ("T0", "T1"), ("R",))]
    a, b = LATE, PT
    at[UNITS + 1] = [("P", a), ("P", b)] + norms + [("M0", a), ("M1", a), ("S", a)] + turns_ + [("M0", b)] + router + [
        ("N", a), ("M1", b), ("S", b), ("T0", a), ("T1", a), ("R", a), ("N", b), ("T0", b), ("T1", b), ("R", b)]
    return at


def block_b(nc, ident, mhalf, psum, proj, utail, logits, mod_d, x1_d, hn2_d, x_prompt, x_sample,
            y_d, cache_k, cache_v, w_pool, pool_scale, w_out, ln1_g, ln1_b, w_group, b_group,
            w_router, b_router, k_prompt, v_prompt, pool_prompt, k_sample, v_sample, pool_sample):
    units = attention_units()
    nu = len(units)
    with ExitStack() as ctx:
        def sb(name, shape, dt=F32):
            return ctx.enter_context(nc.sbuf_tensor(name, shape, dt))

        def sem(name):
            return ctx.enter_context(nc.semaphore(name))

        v_nat = sb("v_nat", [P, TILES, 512])
        v_old = sb("v_old", [P, PAST // P, 512])
        wo_hi = sb("wo_hi", [P, KC, D], F32R)
        wo_raw, wo_lo = one_room(nc, ctx, [P, KC, D], ("wo_raw", F32), ("wo_lo", F32R))
        stay = sb("stay", [P, 2, 2, 512])
        take, mixin1 = one_room(nc, ctx, [P, 2, 2, 512], ("take", F32), ("mixin1", F32R))
        left = sb("left", [P, 2, 1025])
        aT = sb("aT", [P, 2, 2, 4, P])
        mixin0 = sb("mixin0", [P, 2, KC, P], F32R)
        wgr = sb("wgr", [P, KC, NLOG])
        blog = sb("blog", [P, NLOG])
        wp = sb("wp", [P, 4, P])
        small = sb("small", [P, 24])
        psc, ve, rs = small[:, 0:4], small[:, 4:6], small[:, 6:8]
        mv1 = small[:, 8:12].rearrange("p (a b) -> p a b", b=2)
        st1 = small[:, 12:24].rearrange("p (a b) -> p a b", b=6)
        identb = sb("identb", [P, P], BF16)
        mask = sb("mask", [P, P], BF16)
        zeros = sb("zeros", [P, P])
        hn2T = sb("hn2T", [P, KC, P])
        vroom = proj[:, 12:16, :].rearrange("p a b -> p (a b)")
        k_old = vroom[:, 0:4 * PAST].rearrange("p (a b) -> p a b", b=PAST)
        vo_room = v_old[:, :, :].rearrange("p a b -> p (a b)")
        vn_room = v_nat[:, :, :].rearrange("p a b -> p (a b)")
        g1, sc2, sh2, l1g = [vroom[:, n * D:(n + 1) * D] for n in range(4)]
        l1b, xb = [vo_room[:, n * D:(n + 1) * D] for n in range(2)]
        g1s, sc2s, sh2s = [vn_room[:, n * D:(n + 1) * D] for n in range(3)]
        late_res = stay[:, :, :, :].rearrange("p a b c -> p (a b c)")[:, 0:D].rearrange("p (k c) -> p k c", c=P)
        mixin1 = mixin1[:, :, :, :].rearrange("p a b c -> p a (b c)").rearrange("p a (k c) -> p a k c", c=P)
        late_hn2 = aT[:, :, :, :, :].rearrange("p a b c d -> p a (b c) d")
        mixin = [mixin0[:, :, :, :]] * PT + [mixin1]

        def tile_of(j):
            return (proj[:, 0:KC, j * P:(j + 1) * P] if j < PT else late_res)[0:rows(j)]

        def hn2_of(j):
            return tile_of(j) if j < LATE else late_hn2[0:rows(j), j - LATE]

        def mix_bank(j, half):
            return 7 if j < LATE else 2 * (j - LATE) + half

        def turn_bank(j, half):
            return 7 if j < LATE else 4 + half

        def by_chunk(row):
            return row.rearrange("p (k c) -> p k c", c=P)

        beside = steps_beside()
        k_st = stay[:, :, 0, :]
        tail_st = stay[0:HIST, :, 1, :]
        kc = take[:, :, :, :].rearrange("p a b c -> p (a b) c")

        w_loaded, wo_loaded, rows_in, kc_loaded = map(sem, ("bw_loaded", "wo_loaded", "rows_in", "kc_loaded"))
        wo_hi_ready, wo_split, mix_hi_ready, mix_lo_ready = map(sem, ("wo_hi_ready", "wo_split", "mix_hi_ready", "mix_lo_ready"))
        b_const0, b_const = map(sem, ("b_const0", "b_const"))
        kv_turned, k_copied, v_copied = map(sem, ("kv_turned", "k_copied", "v_copied"))
        k_stored = [sem("k_stored0"), sem("k_stored1")]
        out_stored = sem("out_stored")
        tail_turned, tail_copied = map(sem, ("tail_turned", "tail_copied"))
        pool_mixed, pool_copied = map(sem, ("pool_mixed", "pool_copied"))
        z_done, stay_ready, take_ready, left_ready, a_ready = map(sem, ("z_done", "stay_ready", "take_ready", "left_ready", "a_ready"))
        a_turned, aT_copied, pv_done, att_copied = map(sem, ("a_turned", "aT_copied", "pv_done", "att_copied"))
        mix_done, mix_copied = map(sem, ("mix_done", "mix_copied"))
        xb_loaded, res_ready, b_dve = map(sem, ("xb_loaded", "res_ready", "b_dve"))
        var_ready, rstd_ready = map(sem, ("var_ready", "b_rstd_ready"))
        n1_ready, x1_mid, x1_ready, n2_ready, hn2_mid, hn2_ready = map(sem, ("n1_ready", "x1_mid", "x1_ready", "n2_ready", "hn2_mid", "hn2_ready"))
        x1_stored = [sem("x1_stored0"), sem("x1_stored1")]
        hn2_stored = [sem("hn2_stored0"), sem("hn2_stored1")]
        h_turned, h_copied, logits_done, logits_copied = map(sem, ("h_turned", "h_copied", "logits_done", "logits_copied"))
        sample_rows = sem("sample_rows")
        POOL_PIECES = ((0, 512), (512, 512), (SEQ, DEC))
        POOL_FROM, SPLIT_FROM = 2, 5
        sample_units = sum(u[0] == PT for u in units)
        zeros_ready, spare_zeroed = map(sem, ("zeros_ready", "spare_zeroed"))

        block = ctx.enter_context(nc.Block())

        def mod_row(dst, b, part):
            return dst, mod_d[b, part * D:(part + 1) * D].partition_broadcast(P)

        @block.sync
        def _(sp):
            sp.dma_start(kc, cache_k[0, 0].rearrange("(s p) h d -> p s (h d)", p=P)).then_inc(kc_loaded, 16)
            for t in range(TILES):
                r = rows(t)
                ko, vo = (k_prompt[0, 0, t * P:t * P + r], v_prompt[0, 0, t * P:t * P + r]) if t < PT else (k_sample[0, 0], v_sample[0, 0])
                sp.wait_ge(k_copied, t + 1)
                sp.dma_start(ko.rearrange("t h d -> t (h d)"), k_st[0:r, t % 2, :]).then_inc(k_stored[t % 2], 16)
                sp.wait_ge(v_copied, t + 1)
                sp.dma_start(vo.rearrange("t h d -> t (h d)"), v_nat[0:r, t, :]).then_inc(out_stored, 16)
                if t == 3:
                    sp.dma_start(wp[:, :, :], w_pool[0].rearrange("g c d -> c g d")).then_inc(w_loaded, 16)
                    sp.dma_start(psc, pool_scale[0].rearrange("(g p) -> p g", p=P), allow_slow_non_contiguous=True).then_inc(w_loaded, 16)
                    sp.dma_start(v_old[:, :, :], cache_v[0, 0].rearrange("(s p) h d -> p s (h d)", p=P)).then_inc(w_loaded, 16)
                    sp.dma_start(wgr[:, :, 0:NG], w_group[0].rearrange("(k p) n -> p k n", p=P)).then_inc(w_loaded, 16)
                    sp.dma_start(wgr[:, :, NG:NLOG], w_router[0].rearrange("(k p) n -> p k n", p=P)).then_inc(w_loaded, 16)
                    sp.dma_start(blog[:, 0:NG], b_group[0].partition_broadcast(P)).then_inc(w_loaded, 16)
                    sp.dma_start(blog[:, NG:NLOG], b_router[0].partition_broadcast(P)).then_inc(w_loaded, 16)
            sp.wait_ge(tail_copied, 2)
            sp.dma_start(pool_prompt[0, 0], tail_st[:, 0, :]).then_inc(out_stored, 16)
            sp.dma_start(pool_sample[0, 0], tail_st[:, 1, :]).then_inc(out_stored, 16)

            sp.dma_start(wo_raw[:, :, :], w_out[0].rearrange("(k p) n -> p k n", p=P)).then_inc(wo_loaded, 16)
            sp.wait_ge(pv_done, sample_units)
            for dst, src in (mod_row(g1, 0, 2), mod_row(sh2, 0, 3), mod_row(sc2, 0, 4),
                             (l1g, ln1_g[0].partition_broadcast(P)), (l1b, ln1_b[0].partition_broadcast(P))):
                sp.dma_start(dst, src).then_inc(rows_in, 16)
            def load_x(j):
                src = x_prompt[0, j * P:(j + 1) * P, :] if j < PT else x_sample[0]
                sp.dma_start(xb[0:rows(j), :], src).then_inc(xb_loaded, 16)

            def store_hn2(j):
                sp.wait_ge(hn2_ready, j + 1)
                sp.dma_start(hn2_d[j * P:j * P + rows(j), :].rearrange("p (k c) -> p k c", c=P), hn2_of(j)).then_inc(hn2_stored[j % 2], 16)

            load_x(0)
            for j in range(TILES):
                if j + 1 < TILES:
                    sp.wait_ge(res_ready, j + 1)
                    load_x(j + 1)
                if j == LATE:
                    sp.wait_ge(pv_done, nu)
                    for dst, src in (mod_row(g1s, 1, 2), mod_row(sh2s, 1, 3), mod_row(sc2s, 1, 4)):
                        sp.dma_start(dst, src).then_inc(sample_rows, 16)
                sp.wait_ge(x1_ready, j + 1)
                sp.dma_start(x1_d[j * P:j * P + rows(j), :].rearrange("p (k c) -> p k c", c=P), tile_of(j)).then_inc(x1_stored[j % 2], 16)
                if j >= 1:
                    store_hn2(j - 1)
            store_hn2(PT)
            sp.wait_ge(k_stored[0], 16 * 5)
            sp.wait_ge(k_stored[1], 16 * 4)
            sp.wait_ge(out_stored, 16 * (TILES + 2))
            for q in (x1_stored, hn2_stored):
                sp.wait_ge(q[0], 16 * 5)
                sp.wait_ge(q[1], 16 * 4)

        @block.gpsimd
        def _(pool):
            pool.memset(zeros[:, :], 0.0).then_inc(zeros_ready, 1)
            pool.memset(mask[:, :], MASKED).then_inc(b_const0, 1)
            pool.tensor_copy(identb[:, :], ident[:, :]).then_inc(b_const, 1)
            pool.memset(left[:, :, 1024:1025], 1.0).then_inc(b_const, 1)
            pool.memset(logits[:, PT, :], 0.0).then_inc(b_const, 1)
            pool.wait_ge(b_const0, 1)
            pool.affine_select(out=mask[:, :], in_=mask[:, :], compare_op=ALU.is_ge, fill=0.0, base=0,
                               pattern=[[1, P]], channel_multiplier=-1).then_inc(b_const, 1)
            pool.wait_ge(rows_in, 16 * 5)
            pool.wait_ge(zeros_ready, 1)
            spare = y_d[SLOT_TILES_MIN * P:NSLOT, :].rearrange("(p a) (b n) -> p (a b) n", p=P, n=P)
            pool.dma_start(spare, zeros[:, None, :].broadcast_to(list(spare.shape))).then_inc(spare_zeroed, 16)
            for j in range(TILES):
                r, s = rows(j), j % 2
                pool.wait_ge(var_ready, 2 * j + 1)
                pool.tensor_tensor(rs[:, 0:1], ve[:, 0:1], mhalf[:, 0:1], ALU.pow).then_inc(rstd_ready, 1)
                x = tile_of(j)
                pool.wait_ge(n1_ready, j + 1)
                if j < LATE:
                    pool.tensor_tensor(x, x, by_chunk(l1g)[0:r], ALU.mult).then_inc(x1_mid, 1)
                    pool.wait_ge(x1_mid, j + 1)
                pool.tensor_tensor(x, x, by_chunk(l1b)[0:r], ALU.add).then_inc(x1_ready, 1)
                pool.wait_ge(var_ready, 2 * j + 2)
                pool.tensor_tensor(rs[:, 1:2], ve[:, 1:2], mhalf[:, 0:1], ALU.pow).then_inc(rstd_ready, 1)
                pool.wait_ge(n2_ready, j + 1)
                if j == PT:
                    pool.wait_ge(sample_rows, 48)
                shift = sh2 if j < PT else sh2s
                x = hn2_of(j)
                if j < LATE:
                    pool.tensor_tensor(x, x, by_chunk(sc2)[0:r], ALU.mult).then_inc(hn2_mid, 1)
                    pool.wait_ge(hn2_mid, j + 1)
                pool.tensor_tensor(x, x, by_chunk(shift)[0:r], ALU.add).then_inc(hn2_ready, 1)
            pool.wait_ge(spare_zeroed, 16)

        @block.tensor
        def _(pe):
            for t in range(TILES):
                r, s = rows(t), t % 2
                if t >= 2:
                    pe.wait_ge(k_copied, t - 1)
                    pe.wait_ge(v_copied, t - 1)
                for f in range(4):
                    pe.transpose(psum[0:r, 2 * s, f * P:(f + 1) * P], proj[:, 8 + f, t * P:t * P + r], ident[:, :])
                for f in range(4):
                    mm = pe.transpose(psum[0:r, 2 * s + 1, f * P:(f + 1) * P], proj[:, 12 + f, t * P:t * P + r], ident[:, :])
                mm.then_inc(kv_turned, 1)
            for b in range(2):
                for g in range(4):
                    mm = pe.transpose(psum[0:HIST, 4 + b, g * P:(g + 1) * P], utail[:, g, b, :], ident[:, :])
            mm.then_inc(tail_turned, 1)
            pe.wait_ge(kc_loaded, 16)
            pe.wait_ge(k_copied, TILES)
            pe.wait_ge(v_copied, TILES)
            for p in range(PAIRS):
                for s in range(4):
                    mm = pe.transpose(psum[:, p, s * P:(s + 1) * P], kc[:, s, p * P:(p + 1) * P], ident[:, :])
            mm.then_inc(tail_turned, 1)
            pe.wait_ge(w_loaded, 16 * 7)

            last7 = []

            def take_bank(bank, reader):
                if bank == 7:
                    for sm, value in last7:
                        pe.wait_ge(sm, value)
                    last7[:] = [reader]

            def pool_map(n):
                g, (t0, w) = n // 3, POOL_PIECES[n % 3]
                take_bank(7, (pool_copied, n + 1))
                pe.matmul(psum[:, 7, 0:w], wp[:, g, :], proj[:, g, t0:t0 + w], start=True, stop=True).then_inc(pool_mixed, 1)

            pe.wait_ge(tail_copied, 3)
            pe.wait_ge(b_const, 4)

            def scores(u):
                i, p, at, n, old, s0, top, *_ = units[u]
                r, s = rows(i), u % 2
                if u >= 2:
                    pe.wait_ge(take_ready, u - 1)
                for h in range(2):
                    qT = proj[64 * h:64 * h + 64, 4 + p, i * P:i * P + r]
                    k = k_old[64 * h:64 * h + 64, p, :] if old else proj[64 * h:64 * h + 64, 8 + p, s0:s0 + n]
                    mm = pe.matmul(psum[0:r, 2 * s + h, 0:n], qT, k, start=True, stop=not top)
                if top:
                    for h in range(2):
                        lo = 64 * h if r == DEC else 0
                        mm = pe.matmul(psum[0:r, 2 * s + h, n - r:n], identb[lo:lo + r, lo:lo + r], mask[lo:lo + r, lo:lo + r],
                                       start=False, stop=True)
                mm.then_inc(z_done, 1)

            def turn(u):
                i, p, at, n, *_ = units[u]
                r, s = rows(i), u % 2
                pe.wait_ge(a_ready, u + 1)
                for h in range(2):
                    if u >= 1:
                        pe.wait_ge(aT_copied, 2 * u - 1 + h)
                    for b in range(0, n, P):
                        m = min(P, n - b)
                        mm = pe.transpose(psum[0:m, 4 + h, b:b + r], take[0:r, s, h, b:b + m], ident[0:r, 0:r])
                    mm.then_inc(a_turned, 1)

            def values(u):
                i, p, at, n, old, s0, top, bottom, q = units[u]
                r, s = rows(i), u % 2
                pe.wait_ge(aT_copied, 2 * u + 2)
                if top and q:
                    pe.wait_ge(att_copied, q)
                nb = -(-n // P)
                for b in range(nb):
                    m = min(P, n - b * P)
                    v = v_old[0:m, b, :] if old else v_nat[0:m, s0 // P + b, :]
                    for h in range(2):
                        c = p * P + 64 * h
                        mm = pe.matmul(psum[64 * h:64 * h + 64, 6, 0:r], v[:, c:c + 64], aT[0:m, s, h, b, 0:r],
                                       start=(top and b == 0), stop=(bottom and b == nb - 1))
                mm.then_inc(pv_done, 1)

            def mix(j, half):
                r, bank = rows(j), mix_bank(j, half)
                pe.wait_ge(mix_lo_ready, j + 1)
                if j == 0:
                    pe.wait_ge(wo_split, KC)
                if j == LATE:
                    pe.wait_ge(take_ready, nu)
                take_bank(bank, (mix_copied, 2 * j + half + 1))
                for k in range(KC):
                    for part, w in ((0, wo_hi), (0, wo_lo), (1, wo_hi)):
                        mm = pe.matmul(psum[0:r, bank, :], mixin[j][:, part, k, 0:r], w[:, k, 512 * half:512 * half + 512],
                                       start=(k == 0 and part == 0 and w is wo_hi), stop=(k == KC - 1 and part == 1))
                mm.then_inc(mix_done, 1)

            def turn_h(j, half):
                r, bank = rows(j), turn_bank(j, half)
                pe.wait_ge(hn2_ready, j + 1)
                if bank != 7:
                    pe.wait_ge(aT_copied, 2 * nu)
                    if j > LATE:
                        pe.wait_ge(h_copied, 2 * j)
                take_bank(bank, (h_copied, 2 * j + half + 1))
                for k in range(4):
                    mm = pe.transpose(psum[:, bank, k * P:k * P + r], hn2_of(j)[:, 4 * half + k, :], ident[0:r, 0:r])
                mm.then_inc(h_turned, 1)

            def router(j):
                r = rows(j)
                pe.wait_ge(h_copied, 2 * j + 2)
                take_bank(7, (logits_copied, j + 1))
                for k in range(KC):
                    mm = pe.matmul(psum[0:r, 7, 0:NLOG], hn2T[:, k, 0:r], wgr[:, k, :], start=(k == 0), stop=(k == KC - 1))
                mm.then_inc(logits_done, 1)

            def run_beside(u):
                for step, j in beside.get(u, ()):
                    if step in ("M0", "M1"):
                        mix(j, int(step[1]))
                    elif step in ("T0", "T1"):
                        turn_h(j, int(step[1]))
                    elif step == "R":
                        router(j)

            for u in range(nu + 2):
                if u < nu:
                    scores(u)
                if 0 <= u - POOL_FROM < 12:
                    pool_map(u - POOL_FROM)
                if 1 <= u <= nu:
                    turn(u - 1)
                if u >= 2:
                    values(u - 2)
                run_beside(u)

        @block.scalar
        def _(act):
            for t in range(TILES):
                r, s = rows(t), t % 2
                act.wait_ge(kv_turned, t + 1)
                if t >= 2:
                    act.wait_ge(k_stored[s], 16 * (t // 2))
                act.activation(k_st[0:r, s, :], psum[0:r, 2 * s, :], ACT.Copy).then_inc(k_copied, 1)
            act.wait_ge(w_loaded, 16 * 7)
            act.wait_ge(tail_turned, 1)
            for b in range(2):
                act.activation(tail_st[:, b, :], psum[0:HIST, 4 + b, :], ACT.Copy).then_inc(tail_copied, 1)
            act.wait_ge(tail_turned, 2)
            act.activation(k_old, psum[:, 0:4, :], ACT.Copy).then_inc(tail_copied, 1)
            act.wait_ge(k_stored[0], 16 * 5)
            act.wait_ge(k_stored[1], 16 * 4)
            act.wait_ge(out_stored, 16 * (TILES + 2))

            def sticks(u):
                i, p, at, n, *_ = units[u]
                r, s = rows(i), u % 2
                act.wait_ge(z_done, u + 1)
                if u >= 2:
                    act.wait_ge(a_ready, u - 1)
                act.activation(stay[0:r, s, :, 0:n], psum[0:r, 2 * s:2 * s + 2, 0:n], ACT.Sigmoid, scale=-0.125).then_inc(stay_ready, 1)
                if u >= 2:
                    act.wait_ge(a_turned, 2 * (u - 1))
                act.activation(take[0:r, s, :, 0:n], psum[0:r, 2 * s:2 * s + 2, 0:n], ACT.Sigmoid, scale=0.125).then_inc(take_ready, 1)

            def copy_pool(n):
                g, (t0, w) = n // 3, POOL_PIECES[n % 3]
                act.wait_ge(pool_mixed, n + 1)
                act.activation(proj[:, g, t0:t0 + w], psum[:, 7, 0:w], ACT.Copy, scale=psc[:, g:g + 1]).then_inc(pool_copied, 1)

            def copy_aT(u):
                i, p, at, n, *_ = units[u]
                r, s, nb = rows(i), u % 2, -(-n // P)
                m = min(P, n)
                for h in range(2):
                    act.wait_ge(a_turned, 2 * u + h + 1)
                    if u >= 2 and h == 0:
                        act.wait_ge(pv_done, u - 1)
                    src = psum[0:m, 4 + h, :].rearrange("p (b c) -> p b c", c=P)[:, 0:nb, 0:r]
                    act.activation(aT[0:m, s, h, 0:nb, 0:r], src, ACT.Copy).then_inc(aT_copied, 1)

            def mix_high(j):
                r = rows(j)
                act.wait_ge(att_copied, PAIRS * min(j + 2, TILES))
                if 1 <= j < PT:
                    act.wait_ge(mix_done, 2 * j)
                if j == PT:
                    act.wait_ge(a_turned, 2 * nu)
                act.activation(mixin[j][:, 0, :, 0:r], proj[:, 0:KC, j * P:j * P + r], ACT.Copy).then_inc(mix_hi_ready, 1)

            def copy_h(j, half):
                r = rows(j)
                act.wait_ge(h_turned, 2 * j + half + 1)
                if half == 0 and j:
                    act.wait_ge(logits_done, j)
                src = psum[:, turn_bank(j, half), :].rearrange("p (k c) -> p k c", c=P)[:, :, 0:r]
                act.activation(hn2T[:, 4 * half:4 * half + 4, 0:r], src, ACT.Copy).then_inc(h_copied, 1)

            def run_beside(u):
                for step, j in beside.get(u, ()):
                    if step == "P":
                        mix_high(j)
                    elif step in ("T0", "T1"):
                        copy_h(j, int(step[1]))

            for u in range(nu + 2):
                if u < nu:
                    sticks(u)
                if 1 <= u <= nu:
                    copy_aT(u - 1)
                if 0 <= u - POOL_FROM < 12:
                    copy_pool(u - POOL_FROM)
                run_beside(u)

        @block.vector
        def _(dve):
            step = Tally(b_dve)

            def then(ins):
                step.inc(ins)
                dve.wait_ge(b_dve, step.n)

            for t in range(TILES):
                r, s = rows(t), t % 2
                dve.wait_ge(kv_turned, t + 1)
                dve.tensor_copy(v_nat[0:r, t, :], psum[0:r, 2 * s + 1, :]).then_inc(v_copied, 1)
            dve.wait_ge(b_const, 4)

            def weights(u):
                i, p, at, n, old, s0, top, *_ = units[u]
                r, s = rows(i), u % 2
                dve.wait_ge(stay_ready, u + 1)
                if u:
                    dve.wait_ge(a_ready, u)
                for h in range(2):
                    first = 1.0 if top else left[0:r, h, at + n:at + n + 1]
                    w = stay[0:r, s, h, 0:n][:, ::-1]
                    ins = dve.tensor_tensor_scan(left[0:r, h, at:at + n][:, ::-1], w, w, first, ALU.mult, ALU.bypass)
                ins.then_inc(left_ready, 1)
                dve.wait_ge(take_ready, u + 1)
                dve.wait_ge(left_ready, u + 1)
                dve.tensor_tensor(take[0:r, s, :, 0:n], take[0:r, s, :, 0:n], left[0:r, :, at + 1:at + 1 + n], ALU.mult).then_inc(a_ready, 1)

            def copy_att(u):
                i, p = units[u][0:2]
                r = rows(i)
                dve.wait_ge(pv_done, u + 1)
                dve.tensor_copy(proj[:, 4 + p, i * P:i * P + r], psum[:, 6, 0:r]).then_inc(att_copied, 1)

            def split_wo(k):
                if k == 0:
                    dve.wait_ge(wo_loaded, 16)
                raw = wo_raw[:, k, :]
                dve.tensor_copy(wo_hi[:, k, :], raw).then_inc(wo_hi_ready, 1)
                dve.wait_ge(wo_hi_ready, k + 1)
                dve.tensor_tensor(wo_lo[:, k, :], raw, wo_hi[:, k, :].bitcast(F32), ALU.subtract).then_inc(wo_split, 1)

            def mix_low(j):
                r = rows(j)
                dve.wait_ge(mix_hi_ready, j + 1)
                dve.tensor_tensor(mixin[j][:, 1, :, 0:r], proj[:, 0:KC, j * P:j * P + r], mixin[j][:, 0, :, 0:r].bitcast(F32),
                                  ALU.subtract).then_inc(mix_lo_ready, 1)

            def copy_mix(j, half):
                r = rows(j)
                dve.wait_ge(mix_done, 2 * j + half + 1)
                if j == 0:
                    dve.wait_ge(rows_in, 16 * 5)
                if j == PT:
                    dve.wait_ge(sample_rows, 48)
                gate = (g1 if j < PT else g1s)[0:r, 512 * half:512 * half + 512]
                dve.tensor_tensor(tile_of(j)[:, 4 * half:4 * half + 4, :], by_chunk(psum[0:r, mix_bank(j, half), :]), by_chunk(gate),
                                  ALU.mult).then_inc(mix_copied, 1)

            def moments(j, which):
                r, x = rows(j), tile_of(j)
                for half in range(2):
                    st = dve.bn_stats(st1[0:r, half, :], x[:, 4 * half:4 * half + 4, :])
                then(st)
                then(dve.bn_aggr(mv1[0:r, which, :], st1[0:r].rearrange("p b n -> p (b n)")))
                dve.tensor_scalar(ve[0:r, which:which + 1], mv1[0:r, which, 1:2], EPS, None, ALU.add).then_inc(var_ready, 1)

            def residual(j):
                r, x = rows(j), tile_of(j)
                dve.wait_ge(xb_loaded, 16 * (j + 1))
                dve.wait_ge(mix_copied, 2 * j + 2)
                dve.scalar_tensor_tensor(out=x, in0=by_chunk(xb)[0:r], scalar=ALPHA, in1=x, op0=ALU.mult, op1=ALU.add).then_inc(res_ready, 1)
                dve.wait_ge(res_ready, j + 1)
                moments(j, 0)
                dve.wait_ge(rstd_ready, 2 * j + 1)
                ins = dve.tensor_scalar(x, x, mv1[0:r, 0, 0:1], rs[0:r, 0:1], ALU.subtract, ALU.mult)
                if j >= LATE:
                    then(ins)
                    ins = dve.tensor_tensor(x, x, by_chunk(l1g)[0:r], ALU.mult)
                ins.then_inc(n1_ready, 1)

            def norm2(j):
                r = rows(j)
                dve.wait_ge(x1_ready, j + 1)
                moments(j, 1)
                dve.wait_ge(rstd_ready, 2 * j + 2)
                if j < LATE:
                    dve.wait_ge(x1_stored[j % 2], 16 * (j // 2 + 1))
                ins = dve.tensor_scalar(hn2_of(j), tile_of(j), mv1[0:r, 1, 0:1], rs[0:r, 1:2], ALU.subtract, ALU.mult)
                if j >= LATE:
                    then(ins)
                    ins = dve.tensor_tensor(hn2_of(j), hn2_of(j), by_chunk(sc2 if j < PT else sc2s)[0:r], ALU.mult)
                ins.then_inc(n2_ready, 1)

            def copy_logits(j):
                r = rows(j)
                dve.wait_ge(logits_done, j + 1)
                dve.tensor_tensor(logits[0:r, j, :], psum[0:r, 7, 0:NLOG], blog[0:r, :], ALU.add).then_inc(logits_copied, 1)

            def run_beside(u):
                for step, j in beside.get(u, ()):
                    if step in ("M0", "M1"):
                        copy_mix(j, int(step[1]))
                    elif step != "T0" and step != "T1":
                        {"P": mix_low, "S": residual, "N": norm2, "R": copy_logits}[step](j)

            dve.wait_ge(w_loaded, 16 * 7)
            for u in range(nu + 2):
                if u < nu:
                    weights(u)
                if u >= 2 and units[u - 2][7]:
                    copy_att(u - 2)
                if 0 <= u - SPLIT_FROM < KC:
                    split_wo(u - SPLIT_FROM)
                run_beside(u)


def block_c(nc, ident, psum, logits, hn2_d, y_d, slots, gates, w_up, w_down):
    with ExitStack() as ctx:
        def sb(name, shape, dt=F32):
            return ctx.enter_context(nc.sbuf_tensor(name, shape, dt))

        def sem(name):
            return ctx.enter_context(nc.semaphore(name))

        NW = 3
        MADE_SO = "the routing tables are made on chip within these bounds"
        TC = SLOT_TILES + 2
        UP, DN = KC * 2 * DE, 2 * D
        WE = UP + DN
        we_hi = sb("we_hi", [P, NW * WE], F32R)
        we_raw, we_lo = one_room(nc, ctx, [P, NW * WE], ("we_raw", F32), ("we_lo", F32R))
        xg = sb("xg", [P, 2, D])
        outs, onehot = one_room(nc, ctx, [P, 3, D], ("outs", F32), ("onehot", F32R))
        xf = outs[:, 2, :].rearrange("p (k c) -> p k c", c=P)
        x_hi = sb("x_hi", [P, 2, KC, P], F32R)
        x_lo = sb("x_lo", [P, 2, KC, P], F32R)
        au = sb("au", [P, 2 * DE])
        sg = sb("sg", [P, DE])
        actv = sb("actv", [P, DE])
        atf = sb("atf", [P, 2, P])
        at_hi = sb("at_hi", [P, 2, P], F32R)
        at_lo = sb("at_lo", [P, 2, P], F32R)
        yst = outs[:, 0:2, :]
        prio = sb("prio", [P, 4])
        gmax = sb("gmax", [P, TILES, 1])
        gsh = sb("gsh", [P, TILES, NG])
        goh = sb("goh", [P, TILES, NG])
        gex = sb("gex", [P, TILES, NG])
        pg = sb("pg", [P, TILES, 1])
        sel = sb("sel", [P, TILES, NE])
        el = sb("el", [P, TILES, EPG])
        tmp4 = sb("tmp4", [P, TILES, EPG])
        l1, l2 = sb("l1", [P, TILES, 1]), sb("l2", [P, TILES, 1])
        best = sb("best", [P, TILES, 1])
        oh = [sb("oh1", [P, TILES, EPG]), sb("oh2", [P, TILES, EPG])]
        e12 = [sb("e1", [P, TILES, NE]), sb("e2", [P, TILES, NE])]
        both = sb("both", [P, TILES, NE])
        rank = sb("rank", [P, TILES, NE])
        before = sb("before", [P, TILES + 1, NE])
        cnt = sb("cnt", [P, TILES, NE])
        tri = sb("tri", [P, P])
        ones = sb("ones", [P, P])
        needf = sb("needf", [P, NE])
        needi = sb("needi", [P, NE], I32)
        cum = sb("cum", [P, NE])
        base = sb("base", [P, NE])
        sv = sb("sv", [P, TILES, NE])
        slotf = sb("slotf", [P, TILES, 2])
        posi = sb("posi", [P, TILES, 2], I32)
        posf = sb("posf", [P, TILES, 2])
        stf = sb("stf", [P, TILES, 2])
        tiota = sb("tiota", [P, TC])
        ciota = sb("ciota", [P, P])
        tokid = sb("tokid", [P, TILES])
        onp = onehot[:, :, :].rearrange("p a b -> p (a b)")[:, 0:TILES * 2 * P].rearrange("p (t c n) -> p t c n", c=2, n=P)
        ont = sb("ont", [P, TILES, 2, 3, TC], F32R)
        xg_room = xg[:, :, :].rearrange("p a b -> p (a b)")
        cmp = xg_room[:, 0:TC * NE].rearrange("p (t e) -> p t e", e=NE)
        eqr = xg_room[:, 1200:1200 + NE * NE].rearrange("p (r e) -> p r e", e=NE)
        eqe = xg_room[:, 1500:1500 + NE * NE].rearrange("p (r e) -> p r e", e=NE)
        onf = xg_room[:, TC * NE:TC * NE + TILES * 2 * TC].rearrange("p (t c n) -> p t c n", c=2, n=TC)
        g_hi = sb("g_hi", [P, TILES, 2], F32R)
        g_lo = sb("g_lo", [P, TILES, 2])
        gslot = sb("gslot", [P, TC])
        texpf = sb("texpf", [P, TC])
        tab = sb("tab", [P, TC], I32)
        texp = sb("texp", [P, TC], I32)
        tpack = sb("tpack", [P, TC + 1])
        tq = sb("tq", [P, TC], I32)
        tqf = sb("tqf", [P, TC])
        has = sb("has", [P, NE])
        upto = sb("upto", [P, NE])
        rk = sb("rk", [P, NE])
        rk2 = sb("rk2", [P, NE])
        exof = sb("exof", [P, NE], I32)
        cumi = sb("cumi", [P, NE], I32)
        ntile = sb("ntile", [P, 1], I32)
        ntf = sb("ntf", [P, 1])
        ids = sb("ids", [P, TC], I32)
        idst = sb("idst", [P, 2], I32)

        r_const, r_dve, r_exp, r_shift, r_both, r_counts = map(sem, ("r_const", "r_dve", "r_exp", "r_shift", "r_both", "r_counts"))
        oneh_ready, tables_ready, ids_ready = map(sem, ("oneh_ready", "tables_ready", "ids_ready"))

        up_loaded = [[sem(f"up_loaded{s}_{half}") for half in range(2)] for s in range(NW)]
        down_loaded = [sem(f"down_loaded{s}") for s in range(NW)]
        wh_ready, up_ready, down_ready = map(sem, ("wh_ready", "up_ready", "down_ready"))
        gathered = [sem("gathered0"), sem("gathered1")]
        idst_ready = sem("idst_ready")
        x_turned, x_copied, x_ready = map(sem, ("x_turned", "x_copied", "x_ready"))
        up_done, au_copied, act_mid, act_ready = map(sem, ("up_done", "au_copied", "act_mid", "act_ready"))
        act_turned, at_copied, at_ready = map(sem, ("act_turned", "at_copied", "at_ready"))
        down_done, y_copied = map(sem, ("down_done", "y_copied"))
        y_stored = [sem("y_stored0"), sem("y_stored1")]
        y_complete = sem("y_complete")

        def wide(ap, n):
            return ap.broadcast_to(list(ap.shape[:-1]) + [n])

        block = ctx.enter_context(nc.Block())

        @block.sync
        def _(sp):
            def load(e, s, last):
                x = sp.value_load(exof[0:1, bass.ds(e, 1)], min_val=0, max_val=NE - 1)
                up = w_up[0, bass.ds(x, 1)].rearrange("a (k p) n -> p (a k) n", p=P)
                dn = w_down[0, bass.ds(x, 1)].rearrange("a (k p) n -> p (a k) n", p=P)
                at = s * WE
                if last is not None:
                    sp.wait_ge(down_ready, e - (NW - 1))
                    sp.wait_ge(up_done, last)
                for half in range(2):
                    a, b = at + half * UP // 2, at + (half + 1) * UP // 2
                    sp.dma_start(we_raw[:, a:b].rearrange("p (k n) -> p k n", k=KC // 2),
                                 up[:, half * KC // 2:(half + 1) * KC // 2, :]).then_inc(up_loaded[s][half], 16)
                if last is not None:
                    sp.wait_ge(down_done, last)
                sp.dma_start(we_raw[:, at + UP:at + WE].rearrange("p (k n) -> p k n", k=2), dn).then_inc(down_loaded[s], 16)

            def tiles_to(e):
                return sp.value_load(cumi[0:1, bass.ds(e, 1)], min_val=1, max_val=SLOT_TILES + 1)

            sp.wait_ge(tables_ready, 1)
            load(0, 0, None)
            load(1, 1, None)
            sp.wait_ge(gathered[1], 16)
            load(2, 2, None)
            sp.wait_ge(tables_ready, 2)
            with sp.Fori(1, NE // NW) as i:
                for s in range(NW):
                    load(i * NW + s, s, tiles_to(i * NW + (s - NW)))
            for e in range(NE // NW * NW, NE):
                load(e, e % NW, tiles_to(e - NW))
            sp.wait_ge(y_complete, 1)

        @block.vector
        def _(dve):
            step = Tally(r_dve)

            def then(ins):
                step.inc(ins)
                dve.wait_ge(r_dve, step.n)

            G = logits[:, :, 0:NG]
            dve.wait_ge(r_const, 5)

            def pick(dst, v, top):
                then(dve.tensor_reduce(top[:, :, :].rearrange("p t a -> p (t a)"), v, AX_X, ALU.max))
                then(dve.tensor_tensor(tmp4[:, :, :], v, wide(top[:, :, :], 4), ALU.is_equal))
                then(dve.tensor_tensor(tmp4[:, :, :], tmp4[:, :, :], prio[:, None, :].broadcast_to([P, TILES, 4]), ALU.mult))
                then(dve.tensor_reduce(best[:, :, :].rearrange("p t a -> p (t a)"), tmp4[:, :, :], AX_X, ALU.max))
                then(dve.tensor_tensor(dst, tmp4[:, :, :], wide(best[:, :, :], 4), ALU.is_equal))

            pick(goh[:, :, :], G, gmax)
            dve.tensor_tensor(gsh[:, :, :], G, wide(gmax[:, :, :], NG), ALU.subtract).then_inc(r_shift, 1)
            sel4 = sel[:, :, :].rearrange("p t (g e) -> p t g e", g=NG)
            then(dve.tensor_tensor(sel4, logits[:, :, NG:NLOG].rearrange("p t (g e) -> p t g e", g=NG),
                                   goh[:, :, :, None].broadcast_to([P, TILES, NG, EPG]), ALU.mult))
            then(dve.tensor_reduce(el[:, :, :], sel[:, :, :].rearrange("p t (g e) -> p t e g", g=NG), AX_X, ALU.add))
            pick(oh[0][:, :, :], el[:, :, :], l1)
            then(dve.scalar_tensor_tensor(out=el[:, :, :], in0=oh[0][:, :, :], scalar=-3.0e38, in1=el[:, :, :],
                                          op0=ALU.mult, op1=ALU.add))
            pick(oh[1][:, :, :], el[:, :, :], l2)
            then(dve.tensor_tensor(l1[:, :, :], l2[:, :, :], l1[:, :, :], ALU.subtract))
            dve.tensor_copy(l2[:, :, :], l1[:, :, :]).then_inc(r_shift, 1)
            for c in range(2):
                dve.tensor_tensor(e12[c][:, :, :].rearrange("p t (g e) -> p t g e", g=NG),
                                  goh[:, :, :, None].broadcast_to([P, TILES, NG, EPG]),
                                  oh[c][:, :, None, :].broadcast_to([P, TILES, NG, EPG]), ALU.mult).then_inc(r_dve, 1)
                step.n += 1
            dve.wait_ge(r_dve, step.n)
            for c in range(2):
                ms = dve.memset(e12[c][DEC:P, PT, :], 0.0)
            then(ms)
            dve.tensor_tensor(both[:, :, :], e12[0][:, :, :], e12[1][:, :, :], ALU.add).then_inc(r_both, 1)
            dve.wait_ge(r_exp, 2)
            then(dve.tensor_reduce(pg[:, :, :].rearrange("p t a -> p (t a)"), gex[:, :, :], AX_X, ALU.add))
            then(dve.tensor_scalar(l1[:, :, :], l2[:, :, :], 1.0, None, ALU.add))
            then(dve.tensor_tensor(l1[:, :, :], l1[:, :, :], pg[:, :, :], ALU.mult))
            then(dve.reciprocal(gates[:, :, 0:1], l1[:, :, :]))
            then(dve.tensor_tensor(gates[:, :, 1:2], gates[:, :, 0:1], l2[:, :, :], ALU.mult))
            dve.wait_ge(r_counts, 1)
            dve.tensor_copy(rank[:, :, :], psum[:, 6, 0:TILES * NE].rearrange("p (t e) -> p t e", e=NE))
            then(dve.tensor_copy(cnt[:, :, :], psum[:, 7, 0:TILES * NE].rearrange("p (t e) -> p t e", e=NE)))
            for t in range(TILES):
                then(dve.tensor_tensor(before[:, t + 1, :], before[:, t, :], cnt[:, t, :], ALU.add))
            then(dve.tensor_scalar(needi[:, :], before[:, TILES, :], float(P - 1), None, ALU.add))
            then(dve.tensor_scalar(needi[:, :], needi[:, :], 7, None, ALU.logical_shift_right))
            then(dve.tensor_copy(needf[:, :], needi[:, :]))
            then(dve.tensor_scalar(has[:, :], needf[:, :], 0.0, None, ALU.is_gt))
            then(dve.tensor_tensor_scan(upto[:, :], has[:, :], has[:, :], 0.0, ALU.add, ALU.bypass))
            then(dve.tensor_tensor(rk2[:, :], ciota[:, 0:NE], upto[:, :], ALU.subtract))
            then(dve.tensor_scalar(rk2[:, :], rk2[:, :], upto[:, NE - 1:NE], None, ALU.add))
            then(dve.scalar_tensor_tensor(out=rk[:, :], in0=upto[:, :], scalar=-1.0, in1=rk2[:, :], op0=ALU.add, op1=ALU.subtract))
            then(dve.tensor_tensor(rk[:, :], rk[:, :], has[:, :], ALU.mult))
            then(dve.tensor_tensor(rk[:, :], rk[:, :], rk2[:, :], ALU.add))
            square = [P, NE, NE]
            then(dve.tensor_tensor(eqr, rk[:, None, :].broadcast_to(square), ciota[:, 0:NE, None].broadcast_to(square), ALU.is_equal))
            then(dve.tensor_tensor(eqe, eqr, ciota[:, None, 0:NE].broadcast_to(square), ALU.mult))
            then(dve.tensor_reduce(rk2[:, :], eqe, AX_X, ALU.add))
            dve.tensor_copy(exof[:, :], rk2[:, :]).then_inc(tables_ready, 1)
            then(dve.tensor_tensor_scan(cum[:, :], needf[:, :], needf[:, :], 0.0, ALU.add, ALU.bypass))
            then(dve.tensor_tensor(base[:, :], cum[:, :], needf[:, :], ALU.subtract))
            then(dve.tensor_scalar(base[:, :], base[:, :], float(P), None, ALU.mult))
            then(dve.tensor_tensor(sv[:, :, :], rank[:, :, :], before[:, 0:TILES, :], ALU.add))
            then(dve.tensor_tensor(sv[:, :, :], sv[:, :, :], base[:, None, :].broadcast_to([P, TILES, NE]), ALU.add))
            for c in range(2):
                then(dve.tensor_tensor(sel[:, :, :], sv[:, :, :], e12[c][:, :, :], ALU.mult))
                then(dve.tensor_reduce(slotf[:, :, c], sel[:, :, :], AX_X, ALU.add))
            then(dve.tensor_copy(slots[:, :, :], slotf[:, :, :]))
            then(dve.tensor_scalar(posi[:, :, :], slots[:, :, :], P - 1, None, ALU.bitwise_and))
            then(dve.tensor_copy(posf[:, :, :], posi[:, :, :]))
            then(dve.tensor_scalar(posi[:, :, :], slots[:, :, :], 7, None, ALU.logical_shift_right))
            then(dve.tensor_copy(stf[:, :, :], posi[:, :, :]))
            full = [P, TILES, 2]
            dve.tensor_tensor(onp, ciota[:, None, None, :].broadcast_to(full + [P]), posf[:, :, :, None].broadcast_to(full + [P]), ALU.is_equal)
            dve.tensor_copy(g_hi[:, :, :], gates[:, :, :])
            then(dve.tensor_tensor(onf, tiota[:, None, None, :].broadcast_to(full + [TC]),
                                   stf[:, :, :, None].broadcast_to(full + [TC]), ALU.is_equal))
            then(dve.tensor_tensor(g_lo[:, :, :], gates[:, :, :], g_hi[:, :, :].bitcast(F32), ALU.subtract))
            for n, v in enumerate((tokid[:, :, None, None], g_hi[:, :, :, None].bitcast(F32), g_lo[:, :, :, None])):
                last = dve.tensor_tensor(ont[:, :, :, n, :], onf, v.broadcast_to(full + [TC]), ALU.mult)
            last.then_inc(oneh_ready, 1)
            then(dve.tensor_tensor(cmp, cum[:, None, :].broadcast_to([P, TC, NE]),
                                   tiota[:, :, None].broadcast_to([P, TC, NE]), ALU.is_le))
            then(dve.tensor_tensor(cmp, cmp, has[:, None, :].broadcast_to([P, TC, NE]), ALU.mult))
            then(dve.tensor_reduce(texpf[:, :], cmp, AX_X, ALU.add))
            then(dve.tensor_scalar(upto[:, :], upto[:, :], 1.0, None, ALU.subtract))
            then(dve.tensor_scalar(texp[:, :], texpf[:, :], upto[:, NE - 1:NE], None, ALU.min))
            then(dve.tensor_scalar(rk2[:, :], cum[:, :], cum[:, NE - 1:NE], None, ALU.subtract))
            then(dve.tensor_tensor(rk2[:, :], rk2[:, :], has[:, :], ALU.mult))
            then(dve.tensor_scalar(rk2[:, :], rk2[:, :], cum[:, NE - 1:NE], None, ALU.add))
            then(dve.tensor_tensor(eqe, eqr, rk2[:, None, :].broadcast_to(square), ALU.mult))
            then(dve.tensor_reduce(rk[:, :], eqe, AX_X, ALU.add))
            then(dve.tensor_scalar(cumi[:, :], rk[:, :], 1.0, None, ALU.add))
            dve.wait_ge(r_counts, 2)
            dve.tensor_copy(ids[:, :], psum[:, 6, 0:TC]).then_inc(ids_ready, 1)
            then(dve.tensor_scalar(tq[:, :], texp[:, :], 11.0, None, ALU.mult))
            then(dve.tensor_scalar(tq[:, :], tq[:, :], 5, None, ALU.logical_shift_right))
            then(dve.tensor_copy(tqf[:, :], tq[:, :]))
            then(dve.scalar_tensor_tensor(out=tqf[:, :], in0=tqf[:, :], scalar=-float(NW), in1=texp[:, :], op0=ALU.mult, op1=ALU.add))
            then(dve.memset(tpack[:, 0:1], 0.0))
            then(dve.scalar_tensor_tensor(out=tpack[:, 1:TC + 1], in0=tqf[:, :], scalar=16.0, in1=texp[:, :], op0=ALU.mult, op1=ALU.add))
            then(dve.scalar_tensor_tensor(out=tab[:, :], in0=tpack[:, 1:TC + 1], scalar=64.0, in1=tpack[:, 0:TC], op0=ALU.mult, op1=ALU.add))
            then(dve.tensor_scalar(ntile[:, :], cum[:, NE - 1:NE], 1.0, None, ALU.add))
            then(dve.tensor_scalar(ntile[:, :], ntile[:, :], 1, None, ALU.logical_shift_right))
            dve.tensor_scalar(ntile[:, :], ntile[:, :], 1, None, ALU.subtract).then_inc(tables_ready, 1)
            then(dve.tensor_copy(gslot[:, :], psum[:, 6, TC:2 * TC]))
            dve.tensor_tensor(gslot[:, :], psum[:, 6, 2 * TC:3 * TC], gslot[:, :], ALU.add).then_inc(ids_ready, 1)
            dve.wait_ge(tables_ready, 2)

            def split(e, s, turn):
                parts = ((0, UP // 2, up_loaded[s][0], up_ready), (UP // 2, UP, up_loaded[s][1], up_ready), (UP, WE, down_loaded[s], down_ready))
                for n, (lo, hi, loaded, ready) in enumerate(parts):
                    dve.wait_ge(loaded, turn * 16 + 16)
                    a, b = s * WE + lo, s * WE + hi
                    raw = we_raw[:, a:b]
                    dve.tensor_copy(we_hi[:, a:b], raw).then_inc(wh_ready, 1)
                    dve.wait_ge(wh_ready, e * 3 + (n + 1))
                    dve.tensor_tensor(we_lo[:, a:b], raw, we_hi[:, a:b].bitcast(F32), ALU.subtract).then_inc(ready, 1)

            with dve.Fori(0, NE // NW) as i:
                for s in range(NW):
                    split(i * NW + s, s, i)
            for e in range(NE // NW * NW, NE):
                split(e, e % NW, e // NW)

        @block.gpsimd
        def _(pool):
            pool.iota(tiota[:, :], [[1, TC]], base=0, channel_multiplier=0, allow_small_or_imprecise_dtypes=True).then_inc(r_const, 1)
            pool.iota(ciota[:, :], [[1, P]], base=0, channel_multiplier=0, allow_small_or_imprecise_dtypes=True).then_inc(r_const, 1)
            pool.iota(tokid[:, :], [[P, TILES]], base=0, channel_multiplier=1, allow_small_or_imprecise_dtypes=True).then_inc(r_const, 1)
            pool.iota(prio[:, :], [[-1, 4]], base=4, channel_multiplier=0, allow_small_or_imprecise_dtypes=True).then_inc(r_const, 1)
            pool.memset(before[:, 0, :], 0.0).then_inc(r_const, 1)
            pool.memset(ones[:, :], 1.0).then_inc(r_const, 1)
            pool.wait_ge(r_const, 6)
            pool.affine_select(out=tri[:, :], in_=ones[:, :], compare_op=ALU.is_gt, fill=0.0, base=0,
                               pattern=[[1, P]], channel_multiplier=-1).then_inc(r_const, 1)
            pool.wait_ge(ids_ready, 1)

            def name_tokens(t, s, turned):
                if turned is not None:
                    pool.wait_ge(x_turned, turned)
                pool.tensor_copy(idst[:, s:s + 1], ids[:, bass.ds(t, 1)]).then_inc(idst_ready, 1)

            def gather(s):
                pool.indirect_dma_start(xg[:, s, :], None, hn2_d, bass.IndirectOffsetOnAxis(idst[:, s:s + 1], 0)).then_inc(gathered[s], 16)

            def low_x(t, s, up):
                pool.wait_ge(x_copied, t + 1)
                if up is not None:
                    pool.wait_ge(up_done, up + 1)
                pool.tensor_tensor(x_lo[:, s, :, :], xf, x_hi[:, s, :, :].bitcast(F32), ALU.subtract).then_inc(x_ready, 1)

            def low_act(t, used, gathers=True):
                if gathers:
                    pool.wait_ge(idst_ready, t + 4)
                pool.wait_ge(at_copied, t + 1)
                if used is not None:
                    pool.wait_ge(down_done, used)
                pool.tensor_tensor(at_lo[:, :, :], atf[:, :, :], at_hi[:, :, :].bitcast(F32), ALU.subtract).then_inc(at_ready, 1)

            def gate_act(t, turned):
                pool.wait_ge(au_copied, t + 1)
                pool.tensor_tensor(sg[:, :], au[:, 0:DE], sg[:, :], ALU.mult).then_inc(act_mid, 1)
                if turned is not None:
                    pool.wait_ge(act_turned, turned)
                pool.wait_ge(act_mid, t + 1)
                pool.tensor_tensor(actv[:, :], sg[:, :], au[:, DE:2 * DE], ALU.mult).then_inc(act_ready, 1)

            for t in range(2):
                name_tokens(t, t, None)
            pool.wait_ge(idst_ready, 2)
            gather(0)
            gather(1)
            low_x(0, 0, None)
            low_x(1, 1, None)
            name_tokens(2, 0, 1)
            pool.wait_ge(idst_ready, 3)
            gather(0)
            gate_act(0, None)
            low_x(2, 0, 1)
            name_tokens(3, 1, 2)
            low_act(0, None)
            gather(1)
            gate_act(1, 1)
            more = pool.value_load(ntile[0:1, 0:1], min_val=SLOT_TILES_MIN // 2, max_val=SLOT_TILES // 2 - 1)
            with pool.Fori(1, more + 1) as i:
                for s in range(2):
                    t = i * 2 + s
                    low_x(t + 1, 1 - s, t)
                    name_tokens(t + 2, s, t + 1)
                    low_act(t - 1, t)
                    gather(s)
                    gate_act(t, t)
            low_act(more * 2 + 1, more * 2 + 2, False)
            pool.wait_ge(gathered[1], more * 16 + 32)

        @block.scalar
        def _(act):
            act.sem_inc(y_stored[1], 16)
            act.wait_ge(r_shift, 1)
            act.activation(gex[:, :, :], gsh[:, :, :], ACT.Exp).then_inc(r_exp, 1)
            act.wait_ge(r_shift, 2)
            act.activation(l2[:, :, :], l2[:, :, :], ACT.Exp).then_inc(r_exp, 1)

            def copy_x(t, s, up, low):
                act.wait_ge(x_turned, t + 1)
                if up is not None:
                    act.wait_ge(up_done, up + 1)
                src = psum[:, 0:2, :].rearrange("p b (k c) -> p (b k) c", c=P)
                act.activation(x_hi[:, s, :, :], src, ACT.Copy)
                if low is not None:
                    act.wait_ge(x_ready, low)
                act.activation(xf, src, ACT.Copy).then_inc(x_copied, 1)

            def copy_act(t, used, low):
                act.wait_ge(act_turned, t + 1)
                if used is not None:
                    act.wait_ge(down_done, used)
                    act.wait_ge(at_ready, low)
                src = psum[:, 3, 0:2 * P].rearrange("p (k c) -> p k c", c=P)
                act.activation(at_hi[:, :, :], src, ACT.Copy)
                act.activation(atf[:, :, :], src, ACT.Copy).then_inc(at_copied, 1)

            def swish(t, free):
                act.wait_ge(up_done, t + 2)
                if free is not None:
                    act.wait_ge(act_ready, free)
                act.activation(sg[:, :], psum[:, 2, 0:DE], ACT.Sigmoid)
                act.activation(au[:, :], psum[:, 2, :], ACT.Copy).then_inc(au_copied, 1)

            def copy_y(t, s, stored):
                gate = gslot[:, t:t + 1] if isinstance(t, int) else gslot[:, bass.ds(t, 1)]
                act.wait_ge(down_done, t + 2)
                if stored is not None:
                    act.wait_ge(y_stored[s], stored)
                act.activation(yst[:, s, :], psum[:, 4:6, :].rearrange("p b n -> p (b n)"), ACT.Copy,
                               scale=gate).then_inc(y_copied, 1)

            def store_y(t, s):
                act.wait_ge(y_copied, t + 1)
                act.dma_start(y_d[bass.ds(t * P, P), :], yst[:, s, :]).then_inc(y_stored[s], 16)

            act.wait_ge(ids_ready, 2)
            copy_x(0, 0, None, None)
            copy_x(1, 1, None, 1)
            swish(0, None)
            copy_x(2, 0, 1, 2)
            copy_act(0, None, None)
            swish(1, 1)
            copy_y(0, 0, None)
            more = act.value_load(ntile[0:1, 0:1], min_val=SLOT_TILES_MIN // 2, max_val=SLOT_TILES // 2 - 1)
            with act.Fori(1, more + 1) as i:
                for s in range(2):
                    t = i * 2 + s
                    copy_x(t + 1, 1 - s, t, t + 1)
                    store_y(t - 2, s)
                    copy_act(t - 1, t, t - 1)
                    swish(t, t)
                    copy_y(t - 1, 1 - s, i * 16)
            store_y(more * 2, 0)
            copy_act(more * 2 + 1, more * 2 + 2, more * 2 + 1)
            copy_y(more * 2 + 1, 1, more * 16 + 16)
            store_y(more * 2 + 1, 1)
            act.wait_ge(y_stored[0], more * 16 + 16)
            act.wait_ge(y_stored[1], more * 16 + 32)
            act.sem_inc(y_complete, 1)

        @block.tensor
        def _(pe):
            pe.sem_inc(down_done, 1)
            pe.sem_inc(up_done, 1)
            pe.wait_ge(r_both, 1)
            pe.wait_ge(r_const, 7)
            pe.matmul(psum[:, 6, 0:TILES * NE], tri[:, :], both[:, :, :].rearrange("p t e -> p (t e)"), start=True, stop=True)
            pe.matmul(psum[:, 7, 0:TILES * NE], ones[:, :], both[:, :, :].rearrange("p t e -> p (t e)"), start=True, stop=True).then_inc(r_counts, 1)
            for t in range(TILES):
                r = rows(t)
                pe.wait_ge(oneh_ready, 1)
                for c in range(2):
                    mm = pe.matmul(psum[:, 6, 0:3 * TC], onp[0:r, t, c, :], ont[0:r, t, c, :, :].rearrange("p n t -> p (n t)"), start=(t == 0 and c == 0),
                                   stop=(t == PT and c == 1))
            mm.then_inc(r_counts, 1)
            pe.wait_ge(tables_ready, 2)

            def turn_x(t, s, count, copied):
                pe.wait_ge(gathered[s], count)
                if copied is not None:
                    pe.wait_ge(x_copied, copied)
                for k in range(KC):
                    mm = pe.transpose(psum[:, k // 4, (k % 4) * P:(k % 4 + 1) * P], xg[:, s, k * P:(k + 1) * P], ident[:, :])
                mm.then_inc(x_turned, 1)

            def turn_act(t, copied):
                pe.wait_ge(act_ready, t + 1)
                if copied is not None:
                    pe.wait_ge(at_copied, copied)
                for k in range(2):
                    mm = pe.transpose(psum[:, 3, k * P:(k + 1) * P], actv[:, k * P:(k + 1) * P], ident[:, :])
                mm.then_inc(act_turned, 1)

            def places(t):
                both = pe.value_load(tab[0:1, bass.ds(t, 1)], min_val=0, max_val=4095)
                return [(v & 15, nc.s_assert_within(pe.snap(((v >> 4) & 3) * WE), 0, (NW - 1) * WE,
                                                    skip_runtime_bounds_check_because=MADE_SO)) for v in (both & 63, both >> 6)]

            def up(t, s, place, copied):
                e, at = place
                pe.wait_ge(x_ready, t + 1)
                if copied is not None:
                    pe.wait_ge(au_copied, copied)
                for k in range(KC):
                    if k % (KC // 2) == 0:
                        pe.wait_ge(up_ready, e * 2 + (1 + k // (KC // 2)))
                    for x, w in ((x_hi, we_hi), (x_hi, we_lo), (x_lo, we_hi)):
                        mm = pe.matmul(psum[:, 2, :], x[:, s, k, :], w[:, bass.ds(at + k * 2 * DE, 2 * DE)],
                                       start=(k == 0 and x is x_hi and w is we_hi), stop=(k == KC - 1 and x is x_lo))
                mm.then_inc(up_done, 1)

            def down(t, place, copied):
                e, at = place
                pe.wait_ge(at_ready, t + 1)
                pe.wait_ge(down_ready, e + 1)
                if copied is not None:
                    pe.wait_ge(y_copied, copied)
                for k in range(2):
                    for x, w in ((at_hi, we_hi), (at_hi, we_lo), (at_lo, we_hi)):
                        for half in range(2):
                            mm = pe.matmul(psum[:, 4 + half, :], x[:, k, :], w[:, bass.ds(at + (UP + k * D + half * 512), 512)],
                                           start=(k == 0 and x is at_hi and w is we_hi), stop=(k == 1 and x is at_lo))
                mm.then_inc(down_done, 1)

            turn_x(0, 0, 16, None)
            turn_x(1, 1, 16, 1)
            first, second = places(1)
            up(0, 0, first, None)
            turn_x(2, 0, 32, 2)
            turn_act(0, None)
            up(1, 1, second, 1)
            down(0, first, None)
            more = pe.value_load(ntile[0:1, 0:1], min_val=SLOT_TILES_MIN // 2, max_val=SLOT_TILES // 2 - 1)
            with pe.Fori(1, more + 1) as i:
                for s in range(2):
                    t = i * 2 + s
                    turn_x(t + 1, 1 - s, i * 16 + 16 * (s + 1), t + 1)
                    turn_act(t - 1, t - 1)
                    before, this = places(t)
                    up(t, s, this, t)
                    down(t - 1, before, t - 1)
            turn_act(more * 2 + 1, more * 2 + 1)
            down(more * 2 + 1, places(more * 2 + 2)[0], more * 2 + 1)


def block_d(nc, mhalf, mod_d, x1_d, y_d, slots, gates, ln2_g, ln2_b, y_prompt, y_sample):
    with ExitStack() as ctx:
        def sb(name, shape, dt=F32):
            return ctx.enter_context(nc.sbuf_tensor(name, shape, dt))

        def sem(name):
            return ctx.enter_context(nc.semaphore(name))

        NB = 4
        y = sb("y", [P, NB, D])
        x1 = sb("x1", [P, NB, D])
        g2 = sb("g2", [P, 2, D])
        l2g, l2b = sb("l2g", [P, D]), sb("l2b", [P, D])
        st = sb("st2", [P, 2, 6])
        mv = sb("mv2", [P, TILES, 2])
        ve = sb("ve2", [P, TILES])
        rs = sb("rs2", [P, TILES])
        shift = sb("shift2", [P, TILES])
        gate_row = [sem("gate_row_prompt"), sem("gate_row_sample")]
        d_rows = sem("d_rows")
        y_in = [sem(f"y_in{n}") for n in range(NB)]
        x1_moved = [sem(f"x1_moved{n}") for n in range(NB)]
        scaled, d_sum, d_var, d_rstd, d_shift, normed, gained, finished, d_dve = map(
            sem, ("scaled", "d_sum", "d_var", "d_rstd", "d_shift", "normed", "gained", "finished", "d_dve"))
        block = ctx.enter_context(nc.Block())

        @block.sync
        def _(sp):
            def load(j):
                s = j % NB
                if j >= NB:
                    sp.wait_ge(x1_moved[s], 32 * (j // NB))
                sp.dma_start(x1[0:rows(j), s, :], x1_d[j * P:j * P + rows(j), :]).then_inc(x1_moved[s], 16)

            load(0)
            sp.dma_start(g2[:, 0, :], mod_d[0, 5 * D:6 * D].partition_broadcast(P)).then_inc(gate_row[0], 16)
            sp.wait_ge(y_in[0], 32)
            load(1)
            sp.dma_start(l2g[:, :], ln2_g[0].partition_broadcast(P)).then_inc(d_rows, 16)
            sp.dma_start(l2b[:, :], ln2_b[0].partition_broadcast(P)).then_inc(d_rows, 16)
            sp.wait_ge(y_in[1], 32)
            load(2)
            sp.wait_ge(y_in[2], 32)
            load(3)
            for j in range(TILES):
                s = j % NB
                dst = y_prompt[0, j * P:(j + 1) * P, :] if j < PT else y_sample[0]
                if j == 3:
                    sp.dma_start(g2[:, 1, :], mod_d[1, 5 * D:6 * D].partition_broadcast(P)).then_inc(gate_row[1], 16)
                sp.wait_ge(finished, j + 1)
                sp.dma_start(dst, x1[0:rows(j), s, :]).then_inc(x1_moved[s], 16)
                if j >= 1 and j - 1 + NB < TILES:
                    load(j - 1 + NB)
            for s in range(NB):
                sp.wait_ge(x1_moved[s], 32 * len(range(s, TILES, NB)))

        @block.gpsimd
        def _(pool):
            def first(j):
                r, s = rows(j), j % NB
                if j >= NB:
                    pool.wait_ge(d_sum, j - NB + 1)
                pool.indirect_dma_start(y[0:r, s, :], None, y_d,
                                        bass.IndirectOffsetOnAxis(slots[0:r, j, 0:1], 0)).then_inc(y_in[s], 16)

            def second(j):
                r, s = rows(j), j % NB
                pool.wait_ge(y_in[s], 32 * (j // NB) + 16)
                pool.indirect_dma_start(y[0:r, s, :], None, y_d, bass.IndirectOffsetOnAxis(slots[0:r, j, 1:2], 0),
                                        compute_op=ALU.add).then_inc(y_in[s], 16)

            first(0)
            for j in range(1, NB):
                first(j)
                second(j - 1)
            for j in range(TILES + 1):
                if j < TILES:
                    r = rows(j)
                    pool.wait_ge(d_var, j + 1)
                    pool.tensor_tensor(rs[0:r, j:j + 1], ve[0:r, j:j + 1], mhalf[0:r, 0:1], ALU.pow).then_inc(d_rstd, 1)
                if j + NB < TILES:
                    first(j + NB)
                if j + NB - 1 < TILES:
                    second(j + NB - 1)
                if j >= 1:
                    r, s = rows(j - 1), (j - 1) % NB
                    if j == 1:
                        pool.wait_ge(d_rows, 32)
                    pool.wait_ge(gained, j)
                    pool.tensor_tensor(x1[0:r, s, :], x1[0:r, s, :], l2b[0:r, :], ALU.add).then_inc(finished, 1)

        @block.scalar
        def _(act):
            for j in range(TILES):
                r, s = rows(j), j % NB
                act.wait_ge(d_shift, j + 1)
                act.activation(x1[0:r, s, :], x1[0:r, s, :], ACT.Identity, bias=shift[0:r, j:j + 1],
                               scale=rs[0:r, j:j + 1]).then_inc(normed, 1)

        @block.vector
        def _(dve):
            step = Tally(d_dve)

            def then(ins):
                step.inc(ins)
                dve.wait_ge(d_dve, step.n)

            def scale(j):
                r, s = rows(j), j % NB
                dve.wait_ge(y_in[s], 32 * (j // NB) + 32)
                if j in (0, PT):
                    dve.wait_ge(gate_row[j // PT], 16)
                dve.tensor_tensor(y[0:r, s, :], y[0:r, s, :], g2[0:r, j // PT, :], ALU.mult).then_inc(scaled, 1)

            def residual(j):
                r, s = rows(j), j % NB
                dve.wait_ge(scaled, j + 1)
                dve.wait_ge(x1_moved[s], 32 * (j // NB) + 16)
                dve.scalar_tensor_tensor(out=x1[0:r, s, :], in0=x1[0:r, s, :], scalar=ALPHA, in1=y[0:r, s, :],
                                         op0=ALU.mult, op1=ALU.add).then_inc(d_sum, 1)
                dve.wait_ge(d_sum, j + 1)
                for half in range(2):
                    b = dve.bn_stats(st[0:r, half, :], x1[0:r, s, half * 512:(half + 1) * 512])
                then(b)
                then(dve.bn_aggr(mv[0:r, j, :], st[0:r, :, :].rearrange("p b n -> p (b n)")))
                dve.tensor_scalar(ve[0:r, j:j + 1], mv[0:r, j, 1:2], EPS, None, ALU.add).then_inc(d_var, 1)

            def turn_mean(j):
                r = rows(j)
                dve.wait_ge(d_rstd, j + 1)
                dve.scalar_tensor_tensor(out=shift[0:r, j:j + 1], in0=mv[0:r, j, 0:1], scalar=-1.0, in1=rs[0:r, j:j + 1],
                                         op0=ALU.mult, op1=ALU.mult).then_inc(d_shift, 1)

            def gain(j):
                r, s = rows(j), j % NB
                dve.wait_ge(normed, j + 1)
                dve.tensor_tensor(x1[0:r, s, :], x1[0:r, s, :], l2g[0:r, :], ALU.mult).then_inc(gained, 1)

            for j in range(TILES + 1):
                if j < TILES:
                    scale(j)
                if j >= 1:
                    turn_mean(j - 1)
                if j < TILES:
                    residual(j)
                if j == 1:
                    dve.wait_ge(d_rows, 32)
                if j >= 1:
                    gain(j - 1)


_INS = ["x_prompt", "x_sample", "c_prompt", "c_sample", "cache_k", "cache_v", "state_pool",
        "w_mod", "b_mod", "w_in", "w_pool", "pool_scale", "w_out", "ln1_g", "ln1_b", "ln2_g", "ln2_b",
        "w_group", "b_group", "w_router", "b_router", "w_up", "w_down"]
_OUTS = [(1, SEQ, D), (1, DEC, D), (1, 1, SEQ, HEADS, DH), (1, 1, SEQ, HEADS, DH), (1, 1, HIST, 512),
         (1, 1, DEC, HEADS, DH), (1, 1, DEC, HEADS, DH), (1, 1, HIST, 512)]


def kernel(**inputs):
    import numpy as _np
    import concourse.bacc as _bacc
    from concourse.bass_utils import run_bass_kernel_spmd as _run

    nc = _bacc.Bacc("TRN2", target_bir_lowering=False, num_devices=1)
    arrays, args = {}, []
    for name in _INS:
        a = _np.ascontiguousarray(inputs[name])
        arrays[f"in_{name}_dram"] = a
        args.append(nc.dram_tensor(f"in_{name}_dram", a.shape, mybir.dt.from_np(a.dtype), kind="ExternalInput").ap())
    for i, shape in enumerate(_OUTS):
        args.append(nc.dram_tensor(f"out_{i}_dram", shape, F32, kind="ExternalOutput").ap())
    build(nc, *args)
    r = _run(nc, [arrays], core_ids=[0])
    return tuple(r.results[0][f"out_{i}_dram"] for i in range(len(_OUTS)))
```
